# Optimizing a Trainium2 kernel written in Bass

```python
import math
import jax, jax.numpy as jnp
from jax import lax
import numpy as np

D_MODEL = 2048
BATCH = 1
SEQ = 256
DEPTH = 1

EPS = 1e-6
BLOCK = 128
NEG_INF = -1e30

MLA_HEADS = 8
MLA_NOPE = 128
MLA_ROPE = 64
MLA_V = 128
MLA_Q_RANK = 512
MLA_KV_RANK = 256
MLA_QK = MLA_NOPE + MLA_ROPE
ROPE_THETA = 10000.0

SWA_HEADS = 16
SWA_KV_HEADS = 2
SWA_HD = 64
SWA_GROUP = SWA_HEADS // SWA_KV_HEADS
WINDOW = 128

N_BUCKETS = 32
MAX_DISTANCE = 128

PEER_HEADS = 8
PEER_NKEYS = 128
PEER_N = PEER_NKEYS * PEER_NKEYS
PEER_DQ = 256
PEER_TOPK = 16
PEER_CHUNK = 64

MLA_OUT = MLA_HEADS * MLA_V
SWA_OUT = SWA_HEADS * SWA_HD
MIX_WIDTH = MLA_OUT + SWA_OUT
IN_SPLITS = (MLA_Q_RANK, MLA_KV_RANK, MLA_ROPE, SWA_HEADS * SWA_HD, SWA_KV_HEADS * SWA_HD, SWA_KV_HEADS * SWA_HD)
IN_COLS = sum(IN_SPLITS)


def rms_norm(x, g):
    xf = x.astype(jnp.float32)
    y = xf * lax.rsqrt(jnp.mean(xf * xf, axis=-1, keepdims=True) + EPS)
    return (y * g.astype(jnp.float32)).astype(x.dtype)

def rope(x, positions):
    half = x.shape[-1] // 2
    inv_freq = ROPE_THETA ** (-jnp.arange(half, dtype=jnp.float32) / half)
    ang = positions.astype(jnp.float32)[:, :, None, None] * inv_freq
    cos, sin = jnp.cos(ang), jnp.sin(ang)
    x1 = x[..., :half].astype(jnp.float32)
    x2 = x[..., half:].astype(jnp.float32)
    out = jnp.concatenate([x1 * cos - x2 * sin, x2 * cos + x1 * sin], axis=-1)
    return out.astype(x.dtype)

def t5_bucket(dist):
    n = jnp.maximum(dist, 0)
    max_exact = N_BUCKETS // 2
    nf = jnp.maximum(n, 1).astype(jnp.float32)
    large = max_exact + (jnp.log(nf / max_exact) / math.log(MAX_DISTANCE / max_exact)
                         * (N_BUCKETS - max_exact)).astype(jnp.int32)
    large = jnp.minimum(large, N_BUCKETS - 1)
    return jnp.where(n < max_exact, n, large)

def mla_group(q_lat, kv_lat, k_pe, positions, q_a_gain, w_q_b, kv_a_gain, w_kv_b, q_gain, k_gain):
    B, S, _ = q_lat.shape
    q = (rms_norm(q_lat, q_a_gain) @ w_q_b).reshape(B, S, MLA_HEADS, MLA_QK)
    kv = (rms_norm(kv_lat, kv_a_gain) @ w_kv_b).reshape(B, S, MLA_HEADS, MLA_NOPE + MLA_V)
    k_nope, v = kv[..., :MLA_NOPE], kv[..., MLA_NOPE:]
    k = jnp.concatenate([k_nope, jnp.broadcast_to(k_pe[:, :, None, :], (B, S, MLA_HEADS, MLA_ROPE))], axis=-1)
    q = rms_norm(q, q_gain)
    k = rms_norm(k, k_gain)
    q = jnp.concatenate([q[..., :MLA_NOPE], rope(q[..., MLA_NOPE:], positions)], axis=-1)
    k = jnp.concatenate([k[..., :MLA_NOPE], rope(k[..., MLA_NOPE:], positions)], axis=-1)
    scale = MLA_QK ** -0.5
    nb = S // BLOCK
    q_blocks = q.reshape(B, nb, BLOCK, MLA_HEADS, MLA_QK).transpose(1, 0, 2, 3, 4)
    k_idx = jnp.arange(S)

    def one_block(args):
        qb, bi = args
        s = jnp.einsum('bqhd,bkhd->bhqk', qb, k, preferred_element_type=jnp.float32) * scale
        q_idx = bi * BLOCK + jnp.arange(BLOCK)
        causal = k_idx[None, :] <= q_idx[:, None]
        s = jnp.where(causal[None, None], s, NEG_INF)
        p = jax.nn.softmax(s, axis=-1).astype(v.dtype)
        return jnp.einsum('bhqk,bkhd->bqhd', p, v)

    o = lax.map(one_block, (q_blocks, jnp.arange(nb)))
    return o.transpose(1, 0, 2, 3, 4).reshape(B, S, MLA_OUT)

def band(t, nb):
    B, S = t.shape[:2]
    rest = t.shape[2:]
    tp = jnp.pad(t, [(0, 0), (BLOCK, 0)] + [(0, 0)] * len(rest))
    prev = tp[:, :S].reshape(B, nb, BLOCK, *rest)
    cur = t.reshape(B, nb, BLOCK, *rest)
    return jnp.concatenate([prev, cur], axis=2)

def swa_group(q, k, v, positions, q_gain, k_gain, sinks, rel_table):
    B, S, _ = q.shape
    nb = S // BLOCK
    q = rms_norm(q.reshape(B, S, SWA_KV_HEADS, SWA_GROUP, SWA_HD), q_gain)
    k = rms_norm(k.reshape(B, S, SWA_KV_HEADS, SWA_HD), k_gain)
    v = v.reshape(B, S, SWA_KV_HEADS, SWA_HD)
    qb = q.reshape(B, nb, BLOCK, SWA_KV_HEADS, SWA_GROUP, SWA_HD)
    kb, vb, pb = band(k, nb), band(v, nb), band(positions, nb)
    s = jnp.einsum('bnqkgd,bnjkd->bnkgqj', qb, kb, preferred_element_type=jnp.float32) * (SWA_HD ** -0.5)
    qp = positions.reshape(B, nb, BLOCK)
    bucket = t5_bucket(qp[..., :, None] - pb[..., None, :])
    bias = rel_table[bucket].astype(jnp.float32)
    bias = bias.reshape(B, nb, BLOCK, 2 * BLOCK, SWA_KV_HEADS, SWA_GROUP).transpose(0, 1, 4, 5, 2, 3)
    s = s + bias
    q_idx = jnp.arange(S).reshape(nb, BLOCK)
    k_idx = (jnp.arange(nb) * BLOCK - BLOCK)[:, None] + jnp.arange(2 * BLOCK)[None, :]
    off = q_idx[:, :, None] - k_idx[:, None, :]
    mask = (off >= 0) & (off < WINDOW) & (k_idx[:, None, :] >= 0)
    s = jnp.where(mask[None, :, None, None], s, NEG_INF)
    sink = jnp.broadcast_to(sinks.astype(jnp.float32).reshape(SWA_KV_HEADS, SWA_GROUP)[None, None, :, :, None, None],
                            s.shape[:-1] + (1,))
    p = jax.nn.softmax(jnp.concatenate([s, sink], axis=-1), axis=-1)[..., :-1].astype(vb.dtype)
    o = jnp.einsum('bnkgqj,bnjkd->bnqkgd', p, vb)
    return o.reshape(B, S, SWA_OUT)

def peer(h, w_q, sub_keys, expert_u, expert_v):
    B, S, D = h.shape
    T = B * S
    xt = h.reshape(T, D)
    q = (xt @ w_q).reshape(T, PEER_HEADS, 2, PEER_DQ // 2)
    s = jnp.einsum('thpd,hpnd->thpn', q, sub_keys, preferred_element_type=jnp.float32)
    s_half, i_half = lax.top_k(s, PEER_TOPK)
    cand = (s_half[:, :, 0, :, None] + s_half[:, :, 1, None, :]).reshape(T, PEER_HEADS, PEER_TOPK * PEER_TOPK)
    cand_idx = (i_half[:, :, 0, :, None] * PEER_NKEYS + i_half[:, :, 1, None, :]).reshape(T, PEER_HEADS, PEER_TOPK * PEER_TOPK)
    top_s, pos = lax.top_k(cand, PEER_TOPK)
    idx = jnp.take_along_axis(cand_idx, pos, axis=-1)
    g = jax.nn.softmax(top_s, axis=-1)
    n_chunks = T // PEER_CHUNK
    HK = PEER_HEADS * PEER_TOPK

    def one_chunk(args):
        xc, ic, gc = args
        u = expert_u[ic]
        a = jnp.einsum('cd,ced->ce', xc, u, preferred_element_type=jnp.float32)
        w = (gc * jax.nn.gelu(a)).astype(xc.dtype)
        return jnp.einsum('ce,ced->cd', w, expert_v[ic])

    y = lax.map(one_chunk, (xt.reshape(n_chunks, PEER_CHUNK, D),
                            idx.reshape(n_chunks, PEER_CHUNK, HK),
                            g.reshape(n_chunks, PEER_CHUNK, HK)))
    return y.reshape(B, S, D)

def first_inputs(seed: int = 0) -> dict:
    key = jax.random.key(seed)
    ks = jax.random.split(key, 24)
    f32 = jnp.float32
    L = DEPTH

    def nrm(k, shape, scale):
        return jax.random.normal(k, shape, f32) * scale

    def gain(k, shape):
        return 1.0 + 0.05 * jax.random.normal(k, shape, f32)

    x = jax.random.normal(ks[0], (BATCH, SEQ, D_MODEL), f32)
    offset = jax.random.randint(ks[1], (BATCH, 1), 0, 1024, dtype=jnp.int32)
    positions = (offset + jnp.arange(SEQ, dtype=jnp.int32)[None, :]).astype(jnp.int32)
    return {
        "x": x,
        "positions": positions,
        "norm1_gain": gain(ks[2], (L, D_MODEL)),
        "w_in": nrm(ks[3], (L, D_MODEL, IN_COLS), D_MODEL ** -0.5),
        "q_a_gain": gain(ks[4], (L, MLA_Q_RANK)),
        "w_q_b": nrm(ks[5], (L, MLA_Q_RANK, MLA_HEADS * MLA_QK), MLA_Q_RANK ** -0.5),
        "kv_a_gain": gain(ks[6], (L, MLA_KV_RANK)),
        "w_kv_b": nrm(ks[7], (L, MLA_KV_RANK, MLA_HEADS * (MLA_NOPE + MLA_V)), MLA_KV_RANK ** -0.5),
        "mla_q_gain": gain(ks[8], (L, MLA_QK)),
        "mla_k_gain": gain(ks[9], (L, MLA_QK)),
        "swa_q_gain": gain(ks[10], (L, SWA_HD)),
        "swa_k_gain": gain(ks[11], (L, SWA_HD)),
        "swa_sinks": nrm(ks[12], (L, SWA_HEADS), 1.0),
        "rel_bias_table": nrm(ks[13], (N_BUCKETS, SWA_HEADS), 0.5),
        "group_out_gain": gain(ks[14], (L, MIX_WIDTH)),
        "w_out": nrm(ks[15], (L, MIX_WIDTH, D_MODEL), MIX_WIDTH ** -0.5),
        "norm2_gain": gain(ks[16], (L, D_MODEL)),
        "peer_w_q": nrm(ks[17], (L, D_MODEL, PEER_HEADS * PEER_DQ), D_MODEL ** -0.5),
        "peer_sub_keys": nrm(ks[18], (L, PEER_HEADS, 2, PEER_NKEYS, PEER_DQ // 2), (PEER_DQ // 2) ** -0.5),
        "peer_u": nrm(ks[19], (L, PEER_N, D_MODEL), D_MODEL ** -0.5),
        "peer_v": nrm(ks[20], (L, PEER_N, D_MODEL), 0.3),
    }

def first_block(x, positions, norm1_gain, w_in, q_a_gain, w_q_b, kv_a_gain, w_kv_b, mla_q_gain, mla_k_gain,
              swa_q_gain, swa_k_gain, swa_sinks, rel_bias_table, group_out_gain, w_out, norm2_gain,
              peer_w_q, peer_sub_keys, peer_u, peer_v):
    offsets = np.cumsum(IN_SPLITS)[:-1].tolist()
    h = x
    for l in range(DEPTH):
        n1 = rms_norm(h, norm1_gain[l])
        proj = n1 @ w_in[l]
        q_lat, kv_lat, k_pe, q_swa, k_swa, v_swa = jnp.split(proj, offsets, axis=-1)
        o_mla = mla_group(q_lat, kv_lat, k_pe, positions, q_a_gain[l], w_q_b[l], kv_a_gain[l], w_kv_b[l],
                          mla_q_gain[l], mla_k_gain[l])
        o_swa = swa_group(q_swa, k_swa, v_swa, positions, swa_q_gain[l], swa_k_gain[l], swa_sinks[l],
                          rel_bias_table)
        g_out = group_out_gain[l]
        mixed = jnp.concatenate([rms_norm(o_mla, g_out[:MLA_OUT]), rms_norm(o_swa, g_out[MLA_OUT:])], axis=-1)
        h = h + mixed @ w_out[l]
        h = h + peer(rms_norm(h, norm2_gain[l]), peer_w_q[l], peer_sub_keys[l], peer_u[l], peer_v[l])
    return h


GRID_W = 64
DA_HEADS = 4
DA_HEAD_DIM = 128
DA_WIDTH = DA_HEADS * 2 * DA_HEAD_DIM
Q_BLOCK = 128
NA_HEADS = 8
NA_HEAD_DIM = 128
NA_WIDTH = NA_HEADS * NA_HEAD_DIM
NA_KH_MAX = 8
NA_KW = 16
D_FF = 4 * D_MODEL
N_BRANCHES = 2
IN_SPLITS_2 = [DA_WIDTH, DA_WIDTH, DA_WIDTH, NA_WIDTH, NA_WIDTH, NA_WIDTH, N_BRANCHES * D_MODEL]
IN_COLS_2 = sum(IN_SPLITS_2)


def rms_norm_2(x, w):
    xf = x.astype(jnp.float32)
    y = xf * lax.rsqrt(jnp.mean(xf * xf, axis=-1, keepdims=True) + EPS)
    return (y * w.astype(jnp.float32)).astype(x.dtype)

def rope_tables(seq, dim):
    inv = 1.0 / (ROPE_THETA ** (jnp.arange(0, dim, 2, dtype=jnp.float32) / dim))
    ang = jnp.arange(seq, dtype=jnp.float32)[:, None] * inv[None, :]
    return jnp.cos(ang), jnp.sin(ang)

def apply_rope(x, cos, sin):
    xf = x.astype(jnp.float32)
    x1, x2 = jnp.split(xf, 2, axis=-1)
    c = cos[:, None, None, :]
    s = sin[:, None, None, :]
    out = jnp.concatenate([x1 * c - x2 * s, x2 * c + x1 * s], axis=-1)
    return out.astype(x.dtype)

def diff_attention(q, k, v, lam):
    B, S, H, _, d = q.shape
    nb = S // Q_BLOCK
    qb = q.reshape(B, nb, Q_BLOCK, H, 2, d).transpose(1, 0, 2, 3, 4, 5)
    scale = d ** -0.5

    def block(qi):
        s = jnp.einsum('bqhcd,bkhcd->bhcqk', qi, k, preferred_element_type=jnp.float32) * scale
        p = jax.nn.softmax(s, axis=-1)
        p = p[:, :, 0] - lam * p[:, :, 1]
        return jnp.einsum('bhqk,bkhe->bqhe', p.astype(v.dtype), v)

    o = lax.map(block, qb)
    return o.transpose(1, 0, 2, 3, 4).reshape(B, S, H, 2 * d)

def neighbourhood_attention(q, k, v, rpb):
    B, S, H, d = q.shape
    rows = S // GRID_W
    kh = min(NA_KH_MAX, rows)
    qg = q.reshape(B, rows, GRID_W, H, d).transpose(1, 0, 2, 3, 4)
    kg = k.reshape(B, rows, GRID_W, H, d)
    vg = v.reshape(B, rows, GRID_W, H, d)
    col = jnp.arange(GRID_W)
    col_start = jnp.clip(col - NA_KW // 2, 0, GRID_W - NA_KW)
    col_idx = col_start[:, None] + jnp.arange(NA_KW)[None, :]
    dc = col_idx - col[:, None] + (NA_KW - 1)
    row_ids = jnp.arange(rows)
    row_start = jnp.clip(row_ids - kh // 2, 0, rows - kh)
    scale = d ** -0.5

    def row_block(args):
        qr, r, rs = args
        kb = lax.dynamic_slice_in_dim(kg, rs, kh, axis=1)
        vb = lax.dynamic_slice_in_dim(vg, rs, kh, axis=1)
        kw = kb[:, :, col_idx]
        vw = vb[:, :, col_idx]
        dr = rs + jnp.arange(kh) - r + (NA_KH_MAX - 1)
        bias = rpb[:, dr[None, :, None], dc[:, None, :]]
        s = jnp.einsum('bqhd,bnqwhd->bhqnw', qr, kw, preferred_element_type=jnp.float32) * scale
        s = s + bias.astype(jnp.float32)[None]
        p = jax.nn.softmax(s, axis=(-2, -1))
        return jnp.einsum('bhqnw,bnqwhd->bqhd', p.astype(v.dtype), vw)

    o = lax.map(row_block, (qg, row_ids, row_start))
    return o.transpose(1, 0, 2, 3, 4).reshape(B, S, H, d)

def second_inputs(seed: int = 0) -> dict:
    key = jax.random.key(seed)
    ks = jax.random.split(key, 20)
    f32 = jnp.float32

    def nrm(k, shape, scale):
        return jax.random.normal(k, shape, f32) * scale

    def gain(k, n):
        return 1.0 + 0.05 * jax.random.normal(k, (DEPTH, n), f32)

    return {
        "x": jax.random.normal(ks[0], (BATCH, SEQ, D_MODEL), f32),
        "w_in": nrm(ks[1], (DEPTH, D_MODEL, IN_COLS_2), D_MODEL ** -0.5),
        "w_branch_a": nrm(ks[2], (DEPTH, DA_WIDTH, D_MODEL), DA_WIDTH ** -0.5),
        "w_branch_b": nrm(ks[3], (DEPTH, NA_WIDTH, D_MODEL), NA_WIDTH ** -0.5),
        "w_out": nrm(ks[4], (DEPTH, D_MODEL, D_MODEL), D_MODEL ** -0.5),
        "norm_mix_pre": gain(ks[5], D_MODEL),
        "norm_mix_post": gain(ks[6], D_MODEL),
        "norm_mlp_pre": gain(ks[7], D_MODEL),
        "norm_mlp_post": gain(ks[8], D_MODEL),
        "lam_q1": nrm(ks[9], (DEPTH, DA_HEAD_DIM), 0.1),
        "lam_k1": nrm(ks[10], (DEPTH, DA_HEAD_DIM), 0.1),
        "lam_q2": nrm(ks[11], (DEPTH, DA_HEAD_DIM), 0.1),
        "lam_k2": nrm(ks[12], (DEPTH, DA_HEAD_DIM), 0.1),
        "subln_w": gain(ks[13], 2 * DA_HEAD_DIM),
        "na_rpb": nrm(ks[14], (DEPTH, NA_HEADS, 2 * NA_KH_MAX - 1, 2 * NA_KW - 1), 0.1),
        "w_up": nrm(ks[15], (DEPTH, D_MODEL, D_FF), D_MODEL ** -0.5),
        "w_down": nrm(ks[16], (DEPTH, D_FF, D_MODEL), D_FF ** -0.5),
    }

def second_block(x, w_in, w_branch_a, w_branch_b, w_out, norm_mix_pre, norm_mix_post,
              norm_mlp_pre, norm_mlp_post, lam_q1, lam_k1, lam_q2, lam_k2, subln_w,
              na_rpb, w_up, w_down):
    B, S, _ = x.shape
    cos, sin = rope_tables(S, DA_HEAD_DIM)
    split_at = [int(c) for c in np.cumsum(IN_SPLITS_2)[:-1]]
    for l in range(DEPTH):
        lambda_init = 0.8 - 0.6 * float(np.exp(-0.3 * l))
        h = rms_norm_2(x, norm_mix_pre[l])
        proj = jnp.einsum('bsd,dc->bsc', h, w_in[l])
        qa, ka, va, qn, kn, vn, gates = jnp.split(proj, split_at, axis=-1)
        qa = apply_rope(qa.reshape(B, S, DA_HEADS, 2, DA_HEAD_DIM), cos, sin)
        ka = apply_rope(ka.reshape(B, S, DA_HEADS, 2, DA_HEAD_DIM), cos, sin)
        va = va.reshape(B, S, DA_HEADS, 2 * DA_HEAD_DIM)
        lam = (jnp.exp(jnp.sum(lam_q1[l].astype(jnp.float32) * lam_k1[l].astype(jnp.float32)))
               - jnp.exp(jnp.sum(lam_q2[l].astype(jnp.float32) * lam_k2[l].astype(jnp.float32)))
               + lambda_init)
        oa = diff_attention(qa, ka, va, lam)
        oa = (rms_norm_2(oa, subln_w[l]) * (1.0 - lambda_init)).reshape(B, S, DA_WIDTH)
        on = neighbourhood_attention(qn.reshape(B, S, NA_HEADS, NA_HEAD_DIM),
                                     kn.reshape(B, S, NA_HEADS, NA_HEAD_DIM),
                                     vn.reshape(B, S, NA_HEADS, NA_HEAD_DIM),
                                     na_rpb[l]).reshape(B, S, NA_WIDTH)
        g_a, g_b = jnp.split(jax.nn.sigmoid(gates), N_BRANCHES, axis=-1)
        mixed = (g_a * jnp.einsum('bsc,cd->bsd', oa, w_branch_a[l])
                 + g_b * jnp.einsum('bsc,cd->bsd', on, w_branch_b[l]))
        y = jnp.einsum('bsd,de->bse', mixed, w_out[l])
        x = x + rms_norm_2(y, norm_mix_post[l])
        h = rms_norm_2(x, norm_mlp_pre[l])
        u = jnp.square(jax.nn.relu(jnp.einsum('bsd,df->bsf', h, w_up[l])))
        x = x + rms_norm_2(jnp.einsum('bsf,fd->bsd', u, w_down[l]), norm_mlp_post[l])
    return x


def setup_inputs(seed=0):
    out = dict(first_inputs(seed))
    for name, value in second_inputs(seed + 1).items():
        if name != "x":
            out[name + "_2"] = value
    return out


def reference(
    x, positions, norm1_gain, w_in, q_a_gain, w_q_b, kv_a_gain, w_kv_b, mla_q_gain, mla_k_gain,
    swa_q_gain, swa_k_gain, swa_sinks, rel_bias_table, group_out_gain, w_out, norm2_gain,
    peer_w_q, peer_sub_keys, peer_u, peer_v, w_in_2, w_branch_a_2, w_branch_b_2, w_out_2,
    norm_mix_pre_2, norm_mix_post_2, norm_mlp_pre_2, norm_mlp_post_2, lam_q1_2, lam_k1_2,
    lam_q2_2, lam_k2_2, subln_w_2, na_rpb_2, w_up_2, w_down_2,
):
    x = first_block(
        x, positions, norm1_gain, w_in, q_a_gain, w_q_b, kv_a_gain, w_kv_b, mla_q_gain,
        mla_k_gain, swa_q_gain, swa_k_gain, swa_sinks, rel_bias_table, group_out_gain, w_out,
        norm2_gain, peer_w_q, peer_sub_keys, peer_u, peer_v,
    )
    return second_block(
        x, w_in_2, w_branch_a_2, w_branch_b_2, w_out_2, norm_mix_pre_2, norm_mix_post_2,
        norm_mlp_pre_2, norm_mlp_post_2, lam_q1_2, lam_k1_2, lam_q2_2, lam_k2_2, subln_w_2,
        na_rpb_2, w_up_2, w_down_2,
    )


_drawn_inputs = setup_inputs


def setup_inputs(seed=0):
    import zlib

    import numpy as np

    out = dict(_drawn_inputs(seed))
    spreads = {}
    factors = {'swa_sinks': 2.759, 'lam_k1_2': 64.0, 'na_rpb_2': 4.796, 'lam_k2_2': 3.724}
    for name, (base, spread) in spreads.items():
        noise = np.random.default_rng([zlib.crc32(name.encode()), seed]).standard_normal(out[name].shape)
        drawn = base * np.exp(spread * noise) if base else spread * noise
        out[name] = __import__('jax').numpy.asarray(drawn.astype(out[name].dtype))
    for name, factor in factors.items():
        out[name] = (out[name] * factor).astype(out[name].dtype)
    return out
```

```python
import numpy as np

NPIECE = 1024


def threshold_rows():
    import math
    thr = [float(b) for b in range(17)]
    for j in range(1, 16):
        thr.append(float(math.ceil(16.0 * 8.0 ** (j / 16.0) - 1e-9)))
    thr[0] = -3.0e38
    return np.array(thr + [3.0e38], np.float32)


def constants():
    p = np.arange(128)
    c = np.zeros((128, 882), np.float32)
    c[:, 0:128] = np.eye(128)
    c[:, 128:256] = np.where(p[None, :] <= p[:, None], 0.0, -1e30)
    c[:, 256:384] = np.where(p[None, :] > p[:, None], 0.0, -1e30)
    c[:, 384:512] = p[None, :]
    thr = threshold_rows()
    c[:, 512] = thr[p % 32]
    c[:, 513] = thr[p % 32 + 1]
    qc = p % 64
    start = np.clip(qc - 8, 0, 48)
    kc = np.arange(64)
    c[:, 514:578] = np.where((kc[None] >= start[:, None]) & (kc[None] < start[:, None] + 16), 0.0, -1e30)
    inv = (1.0 / (np.float32(10000.0) ** (np.arange(0, 128, 2, dtype=np.float32) / np.float32(128)))).astype(np.float32)
    ang = np.arange(256, dtype=np.float32)[:, None] * inv[None]
    c[:, 578:706] = np.cos(ang).astype(np.float32).reshape(2, 128, 64).transpose(1, 0, 2).reshape(128, 128)
    c[:, 706:834] = np.sin(ang).astype(np.float32).reshape(2, 128, 64).transpose(1, 0, 2).reshape(128, 128)
    c[:, 834:866] = (np.float32(10000.0) ** (-np.arange(32, dtype=np.float32) / np.float32(32)))[None]
    c[:, 866:882] = np.arange(16)[None]
    return c


def build(nc, D, out, stage=9):
    import math
    import concourse.bass as bass
    from concourse import mybir
    from contextlib import ExitStack
    from functools import partial as P

    f32, f32r = mybir.dt.float32, mybir.dt.float32r
    i32, u32 = mybir.dt.int32, mybir.dt.uint32
    ALU, ACT, AX = mybir.AluOpType, mybir.ActivationFunctionType, mybir.AxisListType
    NR, NH = 5, 3

    with ExitStack() as ctx:
        def sb(name, shape, dt=f32):
            return ctx.enter_context(nc.sbuf_tensor(name, shape, dt))

        def sem(name):
            return ctx.enter_context(nc.semaphore(name))

        raw = sb("raw", [128, NR, NPIECE])
        whi = sb("whi", [128, NH, NPIECE], f32r)
        wlo = sb("wlo", [128, NH, NPIECE], f32r)
        AH = sb("AH", [128, 16, 256], f32r)
        AL = sb("AL", [128, 16, 256], f32r)
        BH = sb("BH", [128, 16, 256], f32r)
        BL = sb("BL", [128, 16, 256], f32r)
        R = sb("R", [128, 2, 2048])
        Y = sb("Y", [128, 2, 2048])
        M = sb("M", [128, 12288])
        PTb = sb("PTb", [128, 2, 512])
        TMP = sb("TMP", [128, 1024])
        C = sb("C", [128, 882])
        GC = sb("GC", [128, 88])
        GR = sb("GR", [128, 528])
        POS = sb("POS", [128, 322], i32)
        ST = sb("ST", [128, 1150])
        banks = [ctx.enter_context(nc.psum_tensor(f"bank{i}", [128, 512], f32)) for i in range(8)]

        ident, causal, upper, iota = C[:, 0:128], C[:, 128:256], C[:, 256:384], C[:, 384:512]
        namask = C[:, 514:578]
        cos2 = C[:, 578:706].rearrange("p (t j) -> p t j", t=2)
        sin2 = C[:, 706:834].rearrange("p (t j) -> p t j", t=2)
        iota16 = C[:, 866:882]
        Yf = Y[:, :, :].rearrange("p t n -> p (t n)")
        Rf = R[:, :, :].rearrange("p t n -> p (t n)")

        def mv(a, n, src=None):
            return (M[:, a:a + n] if src is None else src[:, a:a + n])

        def bf(ap):
            return ap.bitcast(f32)

        class Queue:
            def __init__(self, wait, name):
                self.wait_ge, self.sem, self.n, self.q, self.seen = wait, sem(name), 0, [], {}

            def wait(self, toks):
                need = {}
                for tok in flat(toks):
                    s, v = tok
                    if need.get(s.name, (s, 0))[1] < v:
                        need[s.name] = (s, v)
                for name, (s, v) in need.items():
                    if self.seen.get(name, 0) < v:
                        self.seen[name] = v
                        self.q.append(P(self.wait_ge, s, v))

            def do(self, fn, *toks):
                self.wait(toks)
                self.n += 1
                self.q.append(P(signalled, fn, self.sem, 1))
                return (self.sem, self.n)

            def quiet(self, fn, *toks):
                self.wait(toks)
                self.q.append(fn)

            def dma(self, fn, s, count, *toks):
                self.wait(toks)
                self.q.append(P(signalled, fn, s, 16))
                return (s, count)

            def now(self):
                return (self.sem, self.n)

        def signalled(fn, s, n):
            fn().then_inc(s, n)

        def flat(toks):
            for t in toks:
                if t is None:
                    continue
                if isinstance(t, tuple) and len(t) == 2 and isinstance(t[1], int):
                    yield t
                else:
                    yield from flat(t)

        T = Queue(nc.tensor.wait_ge, "q_pe")
        A = Queue(nc.scalar.wait_ge, "q_act")
        V = Queue(nc.vector.wait_ge, "q_dve")
        G = Queue(nc.gpsimd.wait_ge, "q_pool")
        S = Queue(nc.sync.wait_ge, "q_sp")

        def everyone():
            return [q.now() for q in (T, A, V, G)]

        n_aux = [0]

        def load(dst, src, *toks, q=None):
            n_aux[0] += 1
            q = q or G
            e = nc.gpsimd if q is G else nc.sync
            return q.dma(P(e.dma_start, dst, src), sem(f"s_aux{n_aux[0]}"), 16, *toks)

        n_st = [0]

        def stat(n):
            a = n_st[0]
            n_st[0] += n
            assert n_st[0] <= 1150, n_st
            return ST[:, a:a + n]

        class Slots:
            def __init__(self, items, toks=()):
                self.free = [(i, list(toks)) for i in items]

            def give(self, item, *toks):
                self.free.append((item, list(toks)))

        tasks, idle = [], []

        def step(n_idle=1):
            for g in list(tasks):
                if next(g, 1) == 1:
                    tasks.remove(g)
            for _ in range(n_idle):
                if idle and next(idle[0], 1) == 1:
                    idle.pop(0)

        def take(slots):
            while not slots.free:
                step()
            return slots.free.pop(0)

        def wait_for(slots):
            while not slots.free:
                yield
            return slots.free.pop(0)

        def finish_tasks():
            while tasks:
                step(0)

        def finish_idle():
            while idle:
                step()
            finish_tasks()

        def pipelined(units, depth):
            active = []
            units = list(units)
            while units or active:
                if units and len(active) < depth:
                    active.append(units.pop(0))
                for g in list(active):
                    if next(g, 1) == 1:
                        active.remove(g)
                yield

        accs = Slots([0, 1])
        misc = Slots([4, 5, 6, 7])
        PT = Slots([0, 1])

        order = []

        def plan(name, first, n):
            order.extend((name, i) for i in range(first, first + n))

        plan("w_in_a", 8, 24)
        plan("w_in_a", 0, 8)
        plan("w_in_b", 0, 1)
        plan("w_q_b", 0, 6)
        plan("w_kv_b", 0, 4)
        plan("w_out", 0, 32)
        if stage >= 2:
            plan("peer_w_q", 0, 32)
            plan("sub_keys", 0, 2)
            plan("peer_u", 0, 256)
            plan("peer_v", 0, 256)
        if stage >= 3:
            plan("w_in_2", 0, 160)
            for j in range(4):
                plan("w_branch_a", 4 * j, 4)
                plan("w_branch_b", 4 * j, 4)
            plan("w_out_2", 0, 32)
            done_up = 0
            for s in range(9):
                if s < 8:
                    plan("w_up", 16 * s, 16)
                if s >= 1:
                    plan("w_down", 16 * (s - 1), 16)

        s_raw = [sem(f"s_raw{i}") for i in range(NR)]
        loaded, split, used = [], [], []
        at = [0]

        def ensure_split(i):
            while len(split) <= min(i, len(order) - 1):
                n = len(split)
                while len(loaded) <= min(n + NR - 1, len(order) - 1):
                    m = len(loaded)
                    name, k = order[m]
                    loaded.append(S.dma(P(nc.sync.dma_start, raw[:, m % NR, :], D[name][k, :, :]),
                                        s_raw[m % NR], 16 * (m // NR + 1),
                                        split[m - NR] if m >= NR else None))
                free = used[n - NH] if n >= NH else None
                h = A.do(P(nc.scalar.activation, whi[:, n % NH, :], raw[:, n % NR, :], ACT.Copy),
                         loaded[n], free)
                split.append(V.do(P(nc.vector.tensor_tensor, wlo[:, n % NH, :], raw[:, n % NR, :],
                                    bf(whi[:, n % NH, :]), ALU.subtract), h))

        def piece(name, k):
            i = at[0]
            assert order[i] == (name, k), (order[i], name, k)
            ensure_split(i + NH - 1 if i + NH - 1 < len(used) + NH else i)
            at[0] += 1
            return i % NH, split[i]

        def used_up(tok):
            used.append(tok)
            if at[0] < len(order):
                ensure_split(at[0] + NH - 2)

        def gemm(name, first, kts, lh, ll, ltok, step_idle=1):
            pair, free = take(accs)
            b = [banks[2 * pair], banks[2 * pair + 1]]
            n = kts // 2
            for c in range(n):
                slot, tok = piece(name, first + c)
                T.wait([tok, ltok, free])
                for kk in range(2):
                    kt = 2 * c + kk
                    w = slice(512 * kk, 512 * kk + 512)
                    for t in range(2):
                        a = slice(128 * t, 128 * t + 128)
                        first_mm, last_mm = kt == 0, kt == kts - 1
                        T.quiet(P(nc.tensor.matmul, b[t][:, :], lh[:, kt, a], whi[:, slot, w], start=first_mm, stop=False))
                        T.quiet(P(nc.tensor.matmul, b[t][:, :], lh[:, kt, a], wlo[:, slot, w], start=False, stop=False))
                        f = P(nc.tensor.matmul, b[t][:, :], ll[:, kt, a], whi[:, slot, w], start=False, stop=last_mm)
                        if kk == 1 and t == 1:
                            last = T.do(f)
                        else:
                            T.quiet(f)
                used_up(last)
                if c < n - 1:
                    step(step_idle)
            return pair, b, last

        def transposed(srcs, bank, *toks):
            T.wait(toks)
            for n, s in enumerate(srcs):
                f = P(nc.tensor.transpose, banks[bank][:, 128 * n:128 * n + 128], s, ident)
                if n == len(srcs) - 1:
                    return T.do(f)
                T.quiet(f)

        def trans_split(src, kts, hi, lo, gcol, toks, free, done, pause=True):
            for k0 in range(0, kts, 2):
                bank, bfree = yield from wait_for(misc)
                tk = transposed([src(k0 + i, t) for i in range(2) for t in range(2)], bank, toks, bfree)
                if pause:
                    yield
                b = banks[bank][:, :].rearrange("p (k n) -> p k n", k=2)
                if gcol is None:
                    h = A.do(P(nc.scalar.activation, hi(k0, 2), b, ACT.Copy), tk, free)
                    low = V.do(P(nc.vector.tensor_tensor, lo(k0, 2), b, bf(hi(k0, 2)), ALU.subtract), h, free)
                else:
                    for i in range(2):
                        h = A.do(P(nc.scalar.activation, hi(k0 + i, 1), b[:, i:i + 1, :], ACT.Copy,
                                   scale=gcol(k0 + i)), tk, free)
                    for i in range(2):
                        low = V.do(P(nc.vector.scalar_tensor_tensor, out=lo(k0 + i, 1), in0=b[:, i:i + 1, :],
                                     scalar=gcol(k0 + i), in1=bf(hi(k0 + i, 1)), op0=ALU.mult,
                                     op1=ALU.subtract), h, free)
                misc.give(bank, low)
                done.append(low)

        def run(gen):
            for _ in gen:
                step(0)

        def rstd(ss, n, F, toks, mul=1.0):
            m, q, r = stat(n), stat(n), stat(n)
            t1 = V.do(P(nc.vector.tensor_scalar, m, ss, 1.0 / F, 1e-6, ALU.mult, ALU.add), toks)
            t2 = A.do(P(nc.scalar.activation, q, m, ACT.Sqrt), t1)
            t3 = V.do(P(nc.vector.reciprocal, r, q), t2)
            if mul != 1.0:
                t3 = V.do(P(nc.vector.tensor_scalar, r, r, mul, None, ALU.mult), t3)
            return r, t3

        def sum_squares(src, junk, F, toks):
            ss = stat(2)
            t0 = A.do(P(nc.scalar.activation, junk(0), src(0), ACT.Square, accum_out=ss[:, 0:1]), toks)
            t1 = V.do(P(nc.vector.tensor_tensor_reduce, out=junk(1), in0=src(1), in1=src(1), scale=1.0,
                        scalar=0.0, op0=ALU.mult, op1=ALU.add, accum_out=ss[:, 1:2]), toks)
            return rstd(ss, 2, F, [t0, t1])

        def norm_T(src, F, g0, hi, lo, junk, dst, toks, free):
            r, tr = sum_squares(src, junk, F, toks)
            t0 = A.do(P(nc.scalar.activation, dst(0), src(0), ACT.Copy, scale=r[:, 0:1]), tr)
            t1 = V.do(P(nc.vector.tensor_scalar, dst(1), src(1), r[:, 1:2], None, ALU.mult), tr)
            done = []
            run(trans_split(lambda kt, t: dst(t)[:, 128 * kt:128 * kt + 128], F // 128, hi, lo,
                            lambda kt: GC[:, g0 + kt:g0 + kt + 1], [t0, t1], free, done, pause=False))
            return done

        def hl(buf, k0=0):
            return lambda kt, n: buf[:, k0 + kt:k0 + kt + n, :]

        def head_norm(x, U, L, gain, mul, tmp, toks):
            t1 = V.do(P(nc.vector.tensor_tensor, tmp, x, x, ALU.mult), toks)
            ss = stat(U)
            t2 = V.do(P(nc.vector.tensor_reduce, ss, tmp, AX.X, ALU.add), t1)
            r, t3 = rstd(ss, U, L, t2, mul)
            t4 = V.do(P(nc.vector.tensor_tensor, x, x, r.unsqueeze(2).to_broadcast([128, U, L]), ALU.mult), t3)
            return V.do(P(nc.vector.tensor_tensor, x, x, gain.unsqueeze(1).to_broadcast([128, U, L]), ALU.mult), t4)

        def rope(x, U, H, c, s, toks):
            n = U * 2 * H
            a = TMP[:, 0:n].rearrange("p (u c h) -> p u c h", u=U, c=2)
            b = TMP[:, 512:512 + n].rearrange("p (u c h) -> p u c h", u=U, c=2)
            cb = c.unsqueeze(1).to_broadcast([128, U, H])
            sn = s.unsqueeze(1).to_broadcast([128, U, H])
            w = [toks, V.now()]
            t = []
            for i in range(2):
                t.append(V.do(P(nc.vector.tensor_tensor, a[:, :, i, :], x[:, :, i, :], cb, ALU.mult), w))
                t.append(V.do(P(nc.vector.tensor_tensor, b[:, :, i, :], x[:, :, 1 - i, :], sn, ALU.mult), w))
            V.do(P(nc.vector.tensor_tensor, x[:, :, 0, :], a[:, :, 0, :], b[:, :, 0, :], ALU.subtract), t)
            return V.do(P(nc.vector.tensor_tensor, x[:, :, 1, :], a[:, :, 1, :], b[:, :, 1, :], ALU.add), t)

        def attend(scores, U, nk, scale, sink, pslots, blocks, pv, out_cols, finish, combine=None):
            bank, bfree = yield from wait_for(misc)
            tk = scores(bank, bfree)
            yield
            sv = banks[bank][:, 0:U * nk].rearrange("p (u k) -> p u k", u=U)
            m, nm, sm, ri = stat(U), stat(U), stat(U), stat(U)
            t1 = V.do(P(nc.vector.tensor_reduce, m, sv, AX.X, ALU.max), tk)
            if sink is not None:
                t1 = V.do(P(nc.vector.tensor_tensor, m, m, sink, ALU.max), t1)
            t2 = V.do(P(nc.vector.tensor_scalar, nm, m, -scale, None, ALU.mult), t1)
            ps, pfree = yield from wait_for(pslots)
            for u in range(U):
                te = A.do(P(nc.scalar.activation, ps[:, u * nk:(u + 1) * nk], sv[:, u, :], ACT.Exp,
                            bias=nm[:, u:u + 1], scale=scale, accum_out=sm[:, u:u + 1]), t2, pfree)
            misc.give(bank, te, t1)
            ts = te
            if sink is not None:
                es, ee = stat(U), stat(U)
                t3 = V.do(P(nc.vector.tensor_tensor, es, sink, m, ALU.subtract), t1)
                t4 = A.do(P(nc.scalar.activation, ee, es, ACT.Exp), t3)
                ts = V.do(P(nc.vector.tensor_tensor, sm, sm, ee, ALU.add), t4, te)
            tr = V.do(P(nc.vector.reciprocal, ri, sm), ts)
            if combine is not None:
                te = combine(ps, ri, [te, tr])
            yield
            bank, bfree = yield from wait_for(misc)
            tk = transposed([ps[:, 128 * n:128 * n + 128] for n in range(blocks)], bank, te, bfree)
            pslots.give(ps, tk)
            yield
            pt, tfree = yield from wait_for(PT)
            eng = alt[0]
            alt[0] = 1 - eng
            if eng:
                tc = A.do(P(nc.scalar.activation, PTb[:, pt, 0:128 * blocks], banks[bank][:, 0:128 * blocks],
                            ACT.Copy), tk, tfree)
            else:
                tc = V.do(P(nc.vector.tensor_copy, PTb[:, pt, 0:128 * blocks], banks[bank][:, 0:128 * blocks]),
                          tk, tfree)
            misc.give(bank, tc)
            yield
            bank, bfree = yield from wait_for(misc)
            tk = pv(bank, PTb[:, pt, :], [tc, bfree])
            PT.give(pt, tk)
            yield
            tf = finish(banks[bank][:, 0:out_cols], ri, [tk, tr])
            misc.give(bank, tf)

        alt = [0]

        def mm(outp, l, r, start, stop):
            return P(nc.tensor.matmul, outp, l, r, start=start, stop=stop)

        t_x = load(R[:, :, :], D["x"].rearrange("(t p) n -> p t n", p=128), q=S)
        t_c = load(C[:, :], D["consts"], q=S)
        t_gc = load(GC[:, :], D["gain_cols"])
        t_pos = load(POS[:, :], D["pos"])
        t_gr = load(GR[:, :], D["gain_rows"])
        BD = stat(64)
        t_bd = load(BD, D["table"])
        consts = [t_c, t_gc]

        for q in (T, A, V):
            q.wait(consts)

        nA = norm_T(lambda t: R[:, t, :], 2048, 0, hl(AH), hl(AL), lambda t: Y[:, t, :], lambda t: Y[:, t, :],
                    [t_x], None)
        x_read = everyone()

        bias = M[:, 0:6144].rearrange("p (h s k) -> p h s k", h=16, s=3)
        dist = M[:, 6144:8192].rearrange("p (a k q) -> p a k q", a=2, k=8)
        dist_i = dist.bitcast(i32)
        OHm = Y[:, :, :].rearrange("p t (a k q) -> p t a k q", a=2, k=8)
        bias_done = []

        def bias_gen():
            free = {0: x_read, 1: x_read}
            dfree = {0: x_read, 1: x_read}
            n = 0
            for pair, (qb, kb) in enumerate([(0, 0), (1, 0), (1, 1)]):
                for c in range(4):
                    i = n % 2
                    n += 1
                    pq = POS[:, 128 * qb:128 * qb + 128].unsqueeze(1).to_broadcast([128, 8, 128])
                    pk = POS[:, 256 + 32 * kb + 8 * c:256 + 32 * kb + 8 * c + 8].unsqueeze(2).to_broadcast([128, 8, 128])
                    td = G.do(P(nc.gpsimd.tensor_tensor, dist_i[:, i], pq, pk, ALU.subtract), t_pos, dfree[i])
                    yield
                    t1 = V.do(P(nc.vector.tensor_scalar, OHm[:, 0, i], dist_i[:, i], C[:, 512:513], None, ALU.is_ge),
                              td, free[i])
                    t2 = V.do(P(nc.vector.scalar_tensor_tensor, out=OHm[:, 1, i], in0=dist_i[:, i],
                                scalar=C[:, 513:514], in1=OHm[:, 0, i], op0=ALU.is_lt, op1=ALU.mult), t1)
                    dfree[i] = [t2]
                    yield
                    bank, bfree = yield from wait_for(misc)
                    T.wait([t2, t_bd, bfree])
                    for k in range(8):
                        f = mm(banks[bank][:, 64 * k:64 * k + 64], OHm[:, 1, i, k, :], BD, True, True)
                        if k < 7:
                            T.quiet(f)
                    tk = T.do(f)
                    free[i] = [tk]
                    yield
                    mask = upper if pair == 1 else causal
                    bv = banks[bank][:, :].rearrange("p (k g h) -> p g h k", k=8, g=4)
                    for g in range(4):
                        o = 32 * g + 8 * c
                        tb = V.do(P(nc.vector.tensor_tensor, bias[:, :, pair, o:o + 8], bv[:, g],
                                    mask[:, o:o + 8].unsqueeze(1).to_broadcast([128, 16, 8]), ALU.add), tk)
                    misc.give(bank, tb)
                    bias_done.append(tb)
                    yield

        idle.append(bias_gen())

        cs = TMP[:, 0:0 + 1]
        CS = stat(128).rearrange("p (c t j) -> p c t j", c=2, t=2)

        def rope_tables():
            pf = stat(2)
            ang, nn, r, ab = [TMP[:, 64 * i:64 * i + 64].rearrange("p (t j) -> p t j", t=2) for i in range(4)]
            t = V.do(P(nc.vector.tensor_copy, pf, POS[:, 320:322]), t_pos)
            for i in range(2):
                last = V.do(P(nc.vector.tensor_scalar, ang[:, i, :], C[:, 834:866], pf[:, i:i + 1], None, ALU.mult), t)
            t = last
            t = V.do(P(nc.vector.tensor_scalar, nn, ang, 1.0 / (2 * math.pi), 12582912.0, ALU.mult, ALU.add), t)
            t = V.do(P(nc.vector.tensor_scalar, nn, nn, -12582912.0, None, ALU.add), t)
            rest = 2 * math.pi
            src = ang
            for bits in (8, 19, 30, None):
                if bits is None:
                    part = rest
                else:
                    part = math.floor(rest * 2.0 ** (bits - 3)) / 2.0 ** (bits - 3)
                rest -= part
                t = V.do(P(nc.vector.scalar_tensor_tensor, out=r, in0=nn, scalar=-part, in1=src, op0=ALU.mult,
                           op1=ALU.add), t)
                src = r
            t = V.do(P(nc.vector.tensor_scalar, r, r, 3.1415925, -3.1415925, ALU.min, ALU.max), t)
            t1 = V.do(P(nc.vector.scalar_tensor_tensor, out=ab, in0=r, scalar=-1.0, in1=r, op0=ALU.mult, op1=ALU.min), t)
            t1 = V.do(P(nc.vector.tensor_scalar, ab, ab, math.pi / 2, None, ALU.add), t1)
            A.do(P(nc.scalar.activation, CS[:, 0], ab, ACT.Sin), t1)
            return A.do(P(nc.scalar.activation, CS[:, 1], r, ACT.Sin), t)

        t_rope = rope_tables()

        swa_k = M[:, 8192:9216].rearrange("p (t n) -> p t n", t=2)
        qswT = M[:, 9728:11776].rearrange("p (k n) -> p k n", k=8)
        kswT = M[:, 11776:12288].rearrange("p (k n) -> p k n", k=2)
        kdup = M[:, 9216:9728].rearrange("p (t k d n) -> p t k d n", t=2, k=2, d=2)
        qlat = Rf[:, 0:1024].rearrange("p (t n) -> p t n", t=2)
        kpe = Rf[:, 3584:3712].rearrange("p (t n) -> p t n", t=2)
        qsw = Rf[:, 1024:2048].rearrange("p (t n) -> p t n", t=2)
        ktmp = Rf[:, 0:1024].rearrange("p (t n) -> p t n", t=2)
        gq, gk = GR[:, 0:192], GR[:, 192:384]
        gsq, gsk, sinks = GR[:, 384:448], GR[:, 448:512], GR[:, 512:528]
        qsw_t = []

        def evac2(pair, b, last, dst, *toks):
            t0 = A.do(P(nc.scalar.activation, dst(0), b[0][:, :], ACT.Copy), last, toks)
            t1 = V.do(P(nc.vector.tensor_copy, dst(1), b[1][:, :]), last, toks)
            accs.give(pair, t0, t1)
            return [t0, t1]

        free = [x_read]
        for j in range(2):
            pair, b, last = gemm("w_in_a", 16 + 8 * j - 8 * 0, 16, AH, AL, nA) if False else gemm("w_in_a", 8 + 8 * j, 16, AH, AL, nA)
            te = evac2(pair, b, last, lambda t: qsw[:, t, :], free)
            for t in range(2):
                xv = qsw[:, t, :].rearrange("p (u l) -> p u l", u=8)
                tn = head_norm(xv, 8, 64, gsq, 0.125, TMP[:, 512 * t:512 * t + 512].rearrange("p (u l) -> p u l", u=8),
                               [te, t_gr, V.now(), A.now()])
            free = []
            for k0 in range(0, 4, 2):
                bank, bfree = take(misc)
                tk = transposed([qsw[:, t, 128 * (k0 + i):128 * (k0 + i) + 128] for i in range(2) for t in range(2)],
                                bank, tn, bfree)
                tc = A.do(P(nc.scalar.activation, qswT[:, 4 * j + k0:4 * j + k0 + 2, :],
                            banks[bank][:, :].rearrange("p (k n) -> p k n", k=2), ACT.Copy), tk, x_read)
                misc.give(bank, tc)
                qsw_t.append(tc)
                free.append(tk)

        pair, b, last = gemm("w_in_a", 24, 16, AH, AL, nA)
        te = evac2(pair, b, last, lambda t: swa_k[:, t, :], x_read)
        for t in range(2):
            kv = swa_k[:, t, 256:384].rearrange("p (u l) -> p u l", u=2)
            tn = head_norm(kv, 2, 64, gsk, 1.0, TMP[:, 128 * t:128 * t + 128].rearrange("p (u l) -> p u l", u=2),
                           [te, t_gr, V.now(), A.now()])
            for d in range(2):
                tn = V.do(P(nc.vector.tensor_copy, kdup[:, t, :, d, :], kv), tn)
        bank, bfree = take(misc)
        tk = transposed([kdup[:, t, k].rearrange("p d n -> p (d n)") for k in range(2) for t in range(2)],
                        bank, tn, bfree)
        tc = A.do(P(nc.scalar.activation, kswT, banks[bank][:, :].rearrange("p (k n) -> p k n", k=2), ACT.Copy), tk)
        misc.give(bank, tc)
        t_ksw = tc

        nKV = norm_T(lambda t: swa_k[:, t, 0:256], 256, 20, hl(BH, 4), hl(BL, 4), lambda t: ktmp[:, t, 0:256],
                     lambda t: ktmp[:, t, 256:512], [te], None)
        kv_read = [T.now()]
        finish_idle()

        OM = Y[:, :, 0:1024]
        OS = Y[:, :, 1024:2048]
        psw = Slots([Rf[:, 2048 + 512 * i:2048 + 512 * i + 512] for i in range(3)], [x_read])
        y_free = everyone()
        os_done = []

        def swa_unit(t, h0):
            U = 2 if t else 4
            nk = 256 if t else 128

            def scores(bank, bfree):
                T.wait([qsw_t, t_ksw, bias_done[-1], bfree])
                for u in range(U):
                    h = h0 + 2 * u
                    p0 = 64 * (h % 2)
                    o = banks[bank][:, u * nk:(u + 1) * nk]
                    bs = bias[:, h, 1:3, :].rearrange("p s k -> p (s k)") if t else bias[:, h, 0, :]
                    T.quiet(mm(o, ident, bs, True, False))
                    f = mm(o, qswT[p0:p0 + 64, h // 2, 128 * t:128 * t + 128], kswT[p0:p0 + 64, h // 8, 0:nk],
                           False, True)
                    tk = T.do(f)
                return tk

            def pv(bank, pt, toks):
                T.wait(toks)
                for u in range(U):
                    kvh = h0 // 8
                    for kb in range(nk // 128):
                        f = mm(banks[bank][:, 64 * u:64 * u + 64], pt[:, u * nk + 128 * kb:u * nk + 128 * kb + 128],
                               swa_k[:, kb, 384 + 64 * kvh:448 + 64 * kvh], kb == 0, kb == nk // 128 - 1)
                        tk = T.do(f)
                return tk

            def finish(o, ri, toks):
                tf = V.do(P(nc.vector.tensor_tensor,
                            OS[:, t, :].rearrange("p (u l) -> p u l", u=16)[:, h0:h0 + 2 * U - 1:2, :],
                            o.rearrange("p (u l) -> p u l", u=U), ri.unsqueeze(2).to_broadcast([128, U, 64]),
                            ALU.mult), toks, y_free)
                os_done.append(tf)
                return tf

            return attend(scores, U, nk, 1.0, sinks[:, h0:h0 + 2 * U - 1:2], psw, 4, pv, 64 * U, finish)

        idle.append(pipelined([swa_unit(0, h) for h in (0, 1, 8, 9)] + [swa_unit(1, h) for h in (0, 1, 4, 5, 8, 9, 12, 13)], 3))

        pair, b, last = gemm("w_in_a", 0, 16, AH, AL, nA, 2)
        te = evac2(pair, b, last, lambda t: qlat[:, t, :], kv_read, x_read)
        slot, tok = piece("w_in_b", 0)
        pair, free = take(accs)
        T.wait([tok, nA, free])
        for t in range(2):
            for kt in range(16):
                w = slice(64 * kt, 64 * kt + 64)
                a = slice(128 * t, 128 * t + 128)
                o = banks[2 * pair + t][:, 0:64]
                T.quiet(mm(o, AH[:, kt, a], whi[:, slot, w], kt == 0, False))
                T.quiet(mm(o, AH[:, kt, a], wlo[:, slot, w], False, False))
                last = T.do(mm(o, AL[:, kt, a], whi[:, slot, w], False, kt == 15))
        used_up(last)
        t0 = A.do(P(nc.scalar.activation, kpe[:, 0, :], banks[2 * pair][:, 0:64], ACT.Copy), last)
        t1 = V.do(P(nc.vector.tensor_copy, kpe[:, 1, :], banks[2 * pair + 1][:, 0:64]), last)
        accs.give(pair, t0, t1)
        t_kpe = [t0, t1]
        qtmp = Rf[:, 1024:2048].rearrange("p (t n) -> p t n", t=2)
        nQ = norm_T(lambda t: qlat[:, t, :], 512, 16, hl(BH), hl(BL), lambda t: qtmp[:, t, :],
                    lambda t: qtmp[:, t, :], [te], None)
        finish_idle()
        everything = everyone()

        qall = M[:, 0:3072].rearrange("p (t n) -> p t n", t=2)
        kvall = M[:, 3072:7168].rearrange("p (t n) -> p t n", t=2)
        kall = M[:, 7168:10240].rearrange("p (t h n) -> p t h n", t=2, h=8)
        kTn = M[:, 10240:12288].rearrange("p (h n) -> p h n", h=8)
        kTr = Rf[:, 2560:3584].rearrange("p (h n) -> p h n", h=4)
        qTn = Rf[:, 0:2048].rearrange("p (h n) -> p h n", h=8)
        qTr_ = [Rf[:, 2048:2560].rearrange("p (h n) -> p h n", h=2), TMP[:, 512:1024].rearrange("p (h n) -> p h n", h=2)]
        tq = []
        for j in range(3):
            pair, b, last = gemm("w_q_b", 2 * j, 4, BH, BL, nQ)
            tq += evac2(pair, b, last, lambda t: qall[:, t, 512 * j:512 * j + 512], everything)
        tkv = []
        for j in range(4):
            pair, b, last = gemm("w_kv_b", j, 2, BH[:, 4:6, :], BL[:, 4:6, :], nKV)
            tkv += evac2(pair, b, last, lambda t: kvall[:, t, 512 * j:512 * j + 512], everything)
        sq = OM_sq = Y[:, :, 0:1024]
        qh = qall.rearrange("p t (h n) -> p t h n", h=8)
        tn = []
        for t in range(2):
            tmp = Rf[:, 0:1536].rearrange("p (u l) -> p u l", u=8)
            a = head_norm(qh[:, t], 8, 192, gq, 1.0, tmp, [tq, V.now(), T.now()])
            tn.append(rope(qh[:, t, :, 128:192].rearrange("p u (c h) -> p u c h", c=2), 8, 32, CS[:, 0, t], CS[:, 1, t], [a, t_rope]))
            kv4 = kvall[:, t, :].rearrange("p (h n) -> p h n", h=8)
            c1 = A.do(P(nc.scalar.activation, kall[:, t, :, 0:128], kv4[:, :, 0:128], ACT.Copy), tkv, everything)
            c2 = V.do(P(nc.vector.tensor_copy, kall[:, t, :, 128:192],
                        kpe[:, t, :].unsqueeze(1).to_broadcast([128, 8, 64])), t_kpe, everything)
            a = head_norm(kall[:, t], 8, 192, gk, 1.0, tmp, [c1, c2, V.now()])
            tn.append(rope(kall[:, t, :, 128:192].rearrange("p u (c h) -> p u c h", c=2), 8, 32, CS[:, 0, t], CS[:, 1, t], [a, t_rope]))
        tT = []

        def turn(srcs, dst, toks):
            bank, bfree = take(misc)
            tk = transposed(srcs, bank, toks, bfree)
            o = banks[bank][:, :].rearrange("p (k n) -> p k n", k=2)
            if alt[0]:
                tc = A.do(P(nc.scalar.activation, dst, o, ACT.Copy), tk, tn)
            else:
                tc = V.do(P(nc.vector.tensor_copy, dst, o), tk, tn)
            alt[0] = 1 - alt[0]
            misc.give(bank, tc)
            tT.append(tc)

        rp = M[:, 3072 + 0:3072 + 0]
        pk_q = Y[:, :, 0:512]
        pk_k = Y[:, :, 512:1024]
        tp = []
        for t in range(2):
            tp.append(A.do(P(nc.scalar.activation, pk_q[:, t, :].rearrange("p (h n) -> p h n", h=8), qh[:, t, :, 128:192],
                             ACT.Copy), tn, y_free))
            tp.append(A.do(P(nc.scalar.activation, pk_k[:, t, :].rearrange("p (h n) -> p h n", h=8),
                             kall[:, t, :, 128:192], ACT.Copy), tn, y_free))
        for h in range(0, 8, 2):
            turn([qh[:, t, h + i, 0:128] for i in range(2) for t in range(2)], qTn[:, h:h + 2, :], tn)
            turn([kall[:, t, h + i, 0:128] for i in range(2) for t in range(2)], kTn[:, h:h + 2, :], tn)
        for h in range(0, 4, 2):
            turn([pk_q[:, t, 128 * (h + i):128 * (h + i) + 128] for i in range(2) for t in range(2)],
                 qTr_[h // 2], tp)
            turn([pk_k[:, t, 128 * (h + i):128 * (h + i) + 128] for i in range(2) for t in range(2)],
                 kTr[:, h:h + 2, :], tp)
        pml = Slots([M[:, 7168 + 512 * i:7168 + 512 * i + 512] for i in range(4)], [T.now(), A.now()])
        om_done = []

        def mla_unit(t, h0):
            U = 2 if t else 4
            nk = 256 if t else 128

            def scores(bank, bfree):
                T.wait([tT, bfree])
                for u in range(U):
                    h = h0 + 2 * u
                    p0 = 64 * (h % 2)
                    o = banks[bank][:, u * nk:(u + 1) * nk]
                    T.quiet(mm(o, qTn[:, h, 128 * t:128 * t + 128], kTn[:, h, 0:nk], True, False))
                    T.quiet(mm(o, qTr_[h // 4][p0:p0 + 64, (h // 2) % 2, 128 * t:128 * t + 128],
                               kTr[p0:p0 + 64, h // 2, 0:nk], False, False))
                    tk = T.do(mm(banks[bank][:, u * nk + 128 * t:u * nk + 128 * t + 128], ident, causal, False, True))
                return tk

            def pv(bank, pt, toks):
                T.wait(toks)
                for u in range(U):
                    v0 = 256 * (h0 + 2 * u) + 128
                    for kb in range(nk // 128):
                        tk = T.do(mm(banks[bank][:, 128 * u:128 * u + 128],
                                     pt[:, u * nk + 128 * kb:u * nk + 128 * kb + 128],
                                     kvall[:, kb, v0:v0 + 128], kb == 0, kb == nk // 128 - 1))
                return tk

            def finish(o, ri, toks):
                tf = V.do(P(nc.vector.tensor_tensor,
                            OM[:, t, :].rearrange("p (u l) -> p u l", u=8)[:, h0:h0 + 2 * U - 1:2, :],
                            o.rearrange("p (u l) -> p u l", u=U), ri.unsqueeze(2).to_broadcast([128, U, 128]),
                            ALU.mult), toks, tT, y_free)
                om_done.append(tf)
                return tf

            return attend(scores, U, nk, 192 ** -0.5, None, pml, 4, pv, 128 * U, finish)

        idle.append(pipelined([mla_unit(0, 0), mla_unit(0, 1)] + [mla_unit(1, h) for h in (0, 1, 4, 5)], 4))
        finish_idle()
        everything = everyone()
        t_x = load(R[:, :, :], D["x"].rearrange("(t p) n -> p t n", p=128), everything)

        nM = []
        for g, O in ((0, OM), (1, OS)):
            junk = M[:, 4096:6144].rearrange("p (t n) -> p t n", t=2)
            dst = M[:, 2048 * g:2048 * g + 2048].rearrange("p (t n) -> p t n", t=2)
            nM += norm_T(lambda t: O[:, t, :], 1024, 22 + 8 * g, hl(AH, 8 * g), hl(AL, 8 * g),
                         lambda t: junk[:, t, :], lambda t: dst[:, t, :], [om_done, os_done, everything, V.now(), A.now()],
                         everything)
        t_R = [t_x]
        for j in range(4):
            pair, b, last = gemm("w_out", 8 * j, 16, AH, AL, nM)
            for t in range(2):
                c = slice(512 * j, 512 * j + 512)
                t_R.append(V.do(P(nc.vector.tensor_tensor, R[:, t, c], R[:, t, c], b[t][:, :], ALU.add), last, t_x))
            accs.give(pair, t_R[-1])

        tok_items = None
        if stage >= 2:
            everything = everyone()
            nA = norm_T(lambda t: R[:, t, :], 2048, 38, hl(AH), hl(AL), lambda t: Y[:, t, :], lambda t: Y[:, t, :],
                        [t_R, everything], [T.now()])
            norm_read = everyone()
            toks_ = Slots([M[:, 1024 * i:1024 * i + 1024].rearrange("p (t n) -> p t n", t=2) for i in range(2)],
                          everything)
            nB = []

            def q_post(pair, b, last, j):
                ts, free = take(toks_)
                te = evac2(pair, b, last, lambda t: ts[:, t, :], free)

                def later():
                    yield
                    yield from trans_split(lambda kt, t: ts[:, t, 128 * kt:128 * kt + 128], 4, hl(BH, 4 * j),
                                           hl(BL, 4 * j), None, te, everything, nB)
                    toks_.give(ts, T.now())
                tasks.append(later())

            for j in range(4):
                pair, b, last = gemm("peer_w_q", 8 * j, 16, AH, AL, nA)
                q_post(pair, b, last, j)
            finish_tasks()
            SC = Y[:, :, :].rearrange("p t (h n) -> p t h n", h=16)
            t_sc = []
            for c in range(2):
                slot, tok = piece("sub_keys", c)
                T.wait([tok, nB])
                for q4 in range(2):
                    for t in range(2):
                        bank, bfree = take(misc)
                        T.wait([bfree])
                        for i in range(4):
                            hp = 8 * c + 4 * q4 + i
                            w = slice(128 * (4 * q4 + i), 128 * (4 * q4 + i) + 128)
                            a = slice(128 * t, 128 * t + 128)
                            o = banks[bank][:, 128 * i:128 * i + 128]
                            T.quiet(mm(o, BH[:, hp, a], whi[:, slot, w], True, False))
                            T.quiet(mm(o, BH[:, hp, a], wlo[:, slot, w], False, False))
                            last = T.do(mm(o, BL[:, hp, a], whi[:, slot, w], False, True))
                        h0 = 8 * c + 4 * q4
                        te = A.do(P(nc.scalar.activation, SC[:, t, h0:h0 + 4, :],
                                    banks[bank][:, :].rearrange("p (h n) -> p h n", h=4), ACT.Copy), last, norm_read)
                        misc.give(bank, te)
                        t_sc.append(te)
                used_up(last)

            V16 = M[:, 4096:4608].rearrange("p (t h k) -> p t h k", t=2, h=16)
            I16 = M[:, 4608:5120].rearrange("p (t h k) -> p t h k", t=2, h=16)
            I16u = I16.bitcast(u32)
            cand = M[:, 5120:7168].rearrange("p (h a b) -> p h a b", h=8, a=16)
            cmp_ = M[:, 7168:9216].rearrange("p (h k r) -> p h k r", h=8, k=16)
            W2 = M[:, 9216:9344].rearrange("p (h k) -> p h k", h=8)
            P2 = M[:, 9344:9472].rearrange("p (h k) -> p h k", h=8)
            P2u = P2.bitcast(u32)
            pij = [M[:, 9472 + 128 * i:9600 + 128 * i] for i in range(2)]
            idg = [M[:, 9728 + 128 * i:9856 + 128 * i] for i in range(3)]
            IDT = M[:, 10240:11008].rearrange("p (a t) -> p a t", a=3)
            OA = M[:, 8192:9216].rearrange("p (s t n) -> p s t n", s=2, t=4)
            OB = M[:, 9216:10240].rearrange("p (s t n) -> p s t n", s=2, t=4)
            stg = [Yf[:, 0:4096].rearrange("p (i t) -> p i t", t=32),
                   M[:, 4096:8192].rearrange("p (i t) -> p i t", t=32)]
            s_g = [sem(f"s_gw{i}") for i in range(2)]
            g_written = []

            def top8(vals, outv, outi, toks):
                t1 = V.do(P(nc.vector.max, outv[:, 0:8], vals), toks)
                V.do(P(nc.vector.max_index, outi[:, 0:8], outv[:, 0:8], vals), t1)
                t2 = V.do(P(nc.vector.match_replace, vals, outv[:, 0:8], vals, -3.0e38), V.now())
                t3 = V.do(P(nc.vector.max, outv[:, 8:16], vals), t2)
                return V.do(P(nc.vector.max_index, outi[:, 8:16], outv[:, 8:16], vals), t3)

            def routing():
                t_id = []
                for t in range(2):
                    for hp in range(16):
                        last = top8(SC[:, t, hp, :], V16[:, t, hp, :], I16u[:, t, hp, :], [t_sc, everything])
                        yield
                last = V.do(P(nc.vector.tensor_copy, I16, I16u), last)
                for t in range(2):
                    v4 = V16[:, t].rearrange("p (h q) k -> p h q k", q=2)
                    for h in range(8):
                        last = V.do(P(nc.vector.tensor_tensor, cand[:, h],
                                      v4[:, h, 0, :].unsqueeze(2).to_broadcast([128, 16, 16]),
                                      v4[:, h, 1, :].unsqueeze(1).to_broadcast([128, 16, 16]), ALU.add), last)
                    yield
                    for h in range(8):
                        last = top8(cand[:, h].rearrange("p a b -> p (a b)"), W2[:, h, :], P2u[:, h, :], last)
                        yield
                    w3 = idg[2].rearrange("p (h k) -> p h k", h=8)
                    sm, ri = stat(8), stat(8)
                    a = V.do(P(nc.vector.tensor_tensor, w3, W2, W2[:, :, 0:1].to_broadcast([128, 8, 16]), ALU.subtract),
                             last, t_id)
                    a = A.do(P(nc.scalar.activation, idg[2], idg[2], ACT.Exp), a)
                    a = V.do(P(nc.vector.tensor_reduce, sm, w3, AX.X, ALU.add), a)
                    a = V.do(P(nc.vector.reciprocal, ri, sm), a)
                    tg = V.do(P(nc.vector.tensor_tensor, w3, w3, ri.unsqueeze(2).to_broadcast([128, 8, 16]), ALU.mult), a)
                    yield
                    pu = [x.bitcast(u32) for x in pij]
                    flatp = P2u.rearrange("p h k -> p (h k)")
                    a1 = V.do(P(nc.vector.tensor_single_scalar, pu[0], flatp, 4, ALU.logical_shift_right), last)
                    a2 = V.do(P(nc.vector.tensor_single_scalar, pu[1], flatp, 15, ALU.bitwise_and), last)
                    a1 = V.do(P(nc.vector.tensor_copy, pij[0], pu[0]), a1)
                    a2 = V.do(P(nc.vector.tensor_copy, pij[1], pu[1]), a2)
                    i4 = I16[:, t].rearrange("p (h q) k -> p h q k", q=2)
                    for q in range(2):
                        pv_ = pij[q].rearrange("p (h k) -> p h k", h=8).unsqueeze(3).to_broadcast([128, 8, 16, 16])
                        io = iota16.unsqueeze(1).unsqueeze(1).to_broadcast([128, 8, 16, 16])
                        last = V.do(P(nc.vector.tensor_tensor, cmp_, pv_, io, ALU.is_equal), a2, V.now())
                        yield
                        last = V.do(P(nc.vector.tensor_tensor, cmp_, cmp_,
                                      i4[:, :, q, :].unsqueeze(2).to_broadcast([128, 8, 16, 16]), ALU.mult), last)
                        yield
                        last = V.do(P(nc.vector.tensor_reduce, idg[q].rearrange("p (h k) -> p h k", h=8), cmp_, AX.X,
                                      ALU.add), last, t_id)
                        yield
                    bank, bfree = yield from wait_for(misc)
                    tk = transposed(idg, bank, last, tg, bfree)
                    t_id = [tk]
                    tc = A.do(P(nc.scalar.activation, IDT[:, :, 128 * t:128 * t + 128],
                                banks[bank][:, 0:384].rearrange("p (a t) -> p a t", a=3), ACT.Copy), tk, everything)
                    misc.give(bank, tc)
                    yield
                ready = [tc, V.now(), T.now()]
                ofree = [None, None]
                sfree = [None, None]
                tev = None
                for g in range(64):
                    i = g % 2
                    s = (g // 8) % 2
                    for k in range(4):
                        tt = 4 * g + k
                        V.do(P(nc.vector.tensor_scalar, OA[:, i, k, :], iota, IDT[:, 0, tt:tt + 1], None, ALU.is_equal),
                             ready, ofree[i])
                        tb = V.do(P(nc.vector.tensor_scalar, OB[:, i, k, :], iota, IDT[:, 1, tt:tt + 1],
                                    IDT[:, 2, tt:tt + 1], ALU.is_equal, ALU.mult), ready, ofree[i])
                        if k == 1:
                            yield
                    yield
                    bank, bfree = yield from wait_for(misc)
                    T.wait([tb, bfree])
                    for k in range(4):
                        tk = T.do(mm(banks[bank][:, 128 * k:128 * k + 128], OB[:, i, k, :], OA[:, i, k, :], True, True))
                    ofree[i] = tk
                    yield
                    tev = A.do(P(nc.scalar.activation, stg[s][:, :, 4 * (g % 8):4 * (g % 8) + 4],
                                 banks[bank][:, :].rearrange("p (t i) -> p i t", t=4), ACT.Copy), tk, sfree[s], ready)
                    misc.give(bank, tev)
                    if g % 8 == 7:
                        c = g // 8
                        w = G.dma(P(nc.gpsimd.dma_start, D["scr_g"][c, :, :],
                                    stg[s].rearrange("p i t -> p (i t)")), s_g[s], 16 * (c // 2 + 1), tev)
                        sfree[s] = w
                        g_written.append(w)
                    yield

            gls = Slots([(i, M[:, 2048 + 1024 * i:3072 + 1024 * i].rearrange("p (k n) -> p k n", k=4)) for i in range(2)],
                        everything)
            s_a = [sem(f"s_aw{i}") for i in range(2)]
            na = [0, 0]
            a_written = {}

            def u_post(pair, b, last, j):
                ts, free = take(toks_)
                te = evac2(pair, b, last, lambda t: ts[:, t, :], free)

                def later():
                    (gi, gl), gfree = yield from wait_for(gls)
                    for k0 in (0, 2):
                        yield
                        bank, bfree = yield from wait_for(misc)
                        tk = transposed([ts[:, t, 128 * (k0 + i):128 * (k0 + i) + 128] for i in range(2) for t in range(2)],
                                        bank, te, bfree)
                        yield
                        tg = A.do(P(nc.scalar.activation, gl[:, k0:k0 + 2, :],
                                    banks[bank][:, :].rearrange("p (k n) -> p k n", k=2), ACT.Gelu_apprx_tanh), tk, gfree)
                        misc.give(bank, tg)
                    toks_.give(ts, tk)
                    na[gi] += 16
                    h = j % 2
                    w = G.dma(P(nc.gpsimd.dma_start, D["scr_a"][j // 2, :, 1024 * h:1024 * h + 1024],
                                gl.rearrange("p k n -> p (k n)")), s_a[gi], na[gi], tg)
                    a_written[j] = w
                    gls.give((gi, gl), w)
                tasks.append(later())

            idle.append(routing())
            for j in range(32):
                pair, b, last = gemm("peer_u", 8 * j, 16, AH, AL, nA)
                u_post(pair, b, last, j)
            finish_idle()

            s_la = [sem(f"s_la{i}") for i in range(2)]
            s_lg = [sem(f"s_lg{i}") for i in range(2)]
            glt = [M[:, 4096 * (1 + i):4096 * (1 + i) + 2048] for i in range(2)]
            gtt = [M[:, 4096 * (1 + i) + 2048:4096 * (1 + i) + 4096] for i in range(2)]
            bar = everyone()
            lt = {}
            wB = {}
            vdone = {}
            tw_free = {}

            def fetch(sc):
                i = sc % 2
                w = bar if sc < 2 else tw_free[sc - 2]
                l1 = G.dma(P(nc.gpsimd.dma_start, glt[i], D["scr_a"][sc, :, :]), s_la[i], 16 * (sc // 2 + 1),
                           w, a_written[2 * sc], a_written[2 * sc + 1])
                l2 = G.dma(P(nc.gpsimd.dma_start, gtt[i].rearrange("p (c n) -> p c n", c=8),
                             D["scr_g"][:, :, 256 * sc:256 * sc + 256].rearrange("c p n -> p c n")),
                           s_lg[i], 16 * (sc // 2 + 1), w, g_written)
                lt[sc] = [l1, l2]

            def prepare(sc):
                i = sc % 2
                a = glt[i].rearrange("p (k c t) -> p k c t", k=8, c=8)
                g = gtt[i].rearrange("p (c k t) -> p k c t", k=8, c=8)
                free = vdone.get(sc - 2)
                done = []
                for k0 in range(0, 8, 2):
                    t1 = None
                    for k in (k0, k0 + 1):
                        t1 = V.do(P(nc.vector.tensor_tensor, a[:, k], a[:, k], g[:, k], ALU.mult), lt[sc])
                    src = glt[i][:, 256 * k0:256 * k0 + 512].rearrange("p (k n) -> p k n", k=2)
                    o = 8 * i + k0
                    h = A.do(P(nc.scalar.activation, BH[:, o:o + 2, :], src, ACT.Copy), t1, free, bar)
                    done.append(V.do(P(nc.vector.tensor_tensor, BL[:, o:o + 2, :], src, bf(BH[:, o:o + 2, :]), ALU.subtract), h))
                    yield
                wB[sc] = done
                tw_free[sc] = [done[-1]]
                if sc + 2 < 16:
                    fetch(sc + 2)

            fetch(0)
            fetch(1)
            run(prepare(0))
            lastR = t_R
            for sc in range(16):
                if sc + 1 < 16:
                    tasks.append(prepare(sc + 1))
                o = 8 * (sc % 2)
                for j in range(4):
                    pair, b, last = gemm("peer_v", 16 * sc + 4 * j, 8, BH[:, o:o + 8, :], BL[:, o:o + 8, :], wB[sc])
                    c = slice(512 * j, 512 * j + 512)
                    for t in range(2):
                        lr = V.do(P(nc.vector.tensor_tensor, R[:, t, c], R[:, t, c], b[t][:, :], ALU.add), last, lastR)
                    accs.give(pair, lr)
                lastR = [lr]
                vdone[sc] = [last]
                finish_tasks()
            t_R = [lr]

        if stage >= 3:
            everything = everyone()
            nA = norm_T(lambda t: R[:, t, :], 2048, 54, hl(AH), hl(AL), lambda t: Y[:, t, :], lambda t: Y[:, t, :],
                        [t_R, everything], [T.now()])
            y_free = everyone()
            QA = M[:, 0:2048].rearrange("p (k n) -> p k n", k=8)
            KA = M[:, 2048:4096].rearrange("p (k n) -> p k n", k=8)
            VA = M[:, 4096:6144].rearrange("p (t n) -> p t n", t=2)
            VN = M[:, 6144:8192].rearrange("p (t n) -> p t n", t=2)
            QN = Yf[:, 0:2048].rearrange("p (k n) -> p k n", k=8)
            KN = Yf[:, 2048:4096].rearrange("p (k n) -> p k n", k=8)
            toks_ = Slots([M[:, 8192 + 1024 * i:9216 + 1024 * i].rearrange("p (t n) -> p t n", t=2) for i in range(2)],
                          everything)
            pslots = Slots([M[:, 10240 + 512 * i:10752 + 512 * i] for i in range(2)], everything)
            nbs = [M[:, 11264 + 512 * i:11776 + 512 * i] for i in range(2)]

            lamb = TMP[:, 0:512]
            t_l = load(lamb, D["lam"], everything)
            ls, le, lam = stat(2), stat(2), stat(1)
            for i in range(2):
                t1 = V.do(P(nc.vector.tensor_tensor_reduce, out=TMP[:, 512 + 128 * i:640 + 128 * i],
                            in0=TMP[:, 256 * i:256 * i + 128], in1=TMP[:, 256 * i + 128:256 * i + 256], scale=1.0,
                            scalar=0.0, op0=ALU.mult, op1=ALU.add, accum_out=ls[:, i:i + 1]), t_l, everything)
            t2 = A.do(P(nc.scalar.activation, le, ls, ACT.Exp), t1)
            t3 = V.do(P(nc.vector.tensor_tensor, lam, le[:, 0:1], le[:, 1:2], ALU.subtract), t2)
            t_lam = V.do(P(nc.vector.tensor_scalar, lam, lam, 0.8 - 0.6 * float(np.exp(-0.0)), None, ALU.add), t3)

            tdone = {"QA": [], "KA": [], "QN": [], "KN": [], "VA": [], "VN": []}

            def qk_post(pair, b, last, name, dst, j, do_rope, mul):
                ts, free = take(toks_)
                if mul == 1.0:
                    te = evac2(pair, b, last, lambda t: ts[:, t, :], free)
                else:
                    t0 = A.do(P(nc.scalar.activation, ts[:, 0, :], b[0][:, :], ACT.Copy, scale=mul), last, free)
                    t1 = V.do(P(nc.vector.tensor_scalar, ts[:, 1, :], b[1][:, :], mul, None, ALU.mult), last, free)
                    accs.give(pair, t0, t1)
                    te = [t0, t1]

                def later():
                    tt = te
                    yield
                    if do_rope:
                        tt = []
                        for t in range(2):
                            tt.append(rope(ts[:, t, :].rearrange("p (u c h) -> p u c h", u=4, c=2), 4, 64,
                                           cos2[:, t], sin2[:, t], [te, t_lam]))
                            yield
                    for k0 in (0, 2):
                        bank, bfree = yield from wait_for(misc)
                        tk = transposed([ts[:, t, 128 * (k0 + i):128 * (k0 + i) + 128] for i in range(2) for t in range(2)],
                                        bank, tt, bfree)
                        yield
                        tc = A.do(P(nc.scalar.activation, dst[:, 4 * j + k0:4 * j + k0 + 2, :],
                                    banks[bank][:, :].rearrange("p (k n) -> p k n", k=2), ACT.Copy), tk, everything, y_free)
                        misc.give(bank, tc)
                        tdone[name].append(tc)
                    toks_.give(ts, tk)
                tasks.append(later())

            def da_unit(h, t):
                def scores(bank, bfree):
                    T.wait([tdone["QA"], tdone["KA"], bfree])
                    for c in range(2):
                        tk = T.do(mm(banks[bank][:, 256 * c:256 * c + 256], QA[:, 2 * h + c, 128 * t:128 * t + 128],
                                     KA[:, 2 * h + c, :], True, True))
                    return tk

                def combine(ps, ri, toks):
                    rl = stat(1)
                    a = V.do(P(nc.vector.tensor_tensor, rl, ri[:, 1:2], lam, ALU.mult), toks, t_lam)
                    a = V.do(P(nc.vector.tensor_scalar, ps[:, 256:512], ps[:, 256:512], rl, None, ALU.mult), a)
                    return V.do(P(nc.vector.scalar_tensor_tensor, out=ps[:, 0:256], in0=ps[:, 0:256],
                                  scalar=ri[:, 0:1], in1=ps[:, 256:512], op0=ALU.mult, op1=ALU.subtract), a)

                def pv(bank, pt, toks):
                    T.wait([toks, tdone["VA"]])
                    for kb in range(2):
                        tk = T.do(mm(banks[bank][:, 0:256], pt[:, 128 * kb:128 * kb + 128],
                                     VA[:, kb, 256 * h:256 * h + 256], kb == 0, kb == 1))
                    return tk

                def finish(o, ri, toks):
                    tf = A.do(P(nc.scalar.activation, QA[:, 2 * h:2 * h + 2, 128 * t:128 * t + 128],
                                o.rearrange("p (c n) -> p c n", c=2), ACT.Copy), toks)
                    oa_done.append(tf)
                    return tf

                return attend(scores, 2, 256, 128 ** -0.5, None, pslots, 2, pv, 256, finish, combine)

            s_nb = [sem(f"s_nb{i}") for i in range(2)]
            nb_t, nb_free = {}, {}

            def nb_fetch(h):
                i = h % 2
                nb_t[h] = G.dma(P(nc.gpsimd.dma_start, nbs[i], D["na_bias"][h, :, :]), s_nb[i], 16 * (h // 2 + 1),
                                nb_free.get(h - 2, everything))

            def na_unit(h):
                i = h % 2

                def scores(bank, bfree):
                    v = nbs[i].rearrange("p (r c) -> p r c", c=64)
                    tb = V.do(P(nc.vector.tensor_tensor, v, v, namask.unsqueeze(1).to_broadcast([128, 8, 64]), ALU.add),
                              nb_t[h])
                    T.wait([tdone["QN"], tdone["KN"], bfree, tb])
                    for t in range(2):
                        o = banks[bank][:, 256 * t:256 * t + 256]
                        T.quiet(mm(o, QN[:, h, 128 * t:128 * t + 128], KN[:, h, :], True, False))
                        tk = T.do(mm(o, ident, nbs[i][:, 256 * t:256 * t + 256], False, True))
                    nb_free[h] = [tk]
                    if h + 2 < 8:
                        nb_fetch(h + 2)
                    return tk

                def pv(bank, pt, toks):
                    T.wait([toks, tdone["VN"]])
                    for t in range(2):
                        for kb in range(2):
                            tk = T.do(mm(banks[bank][:, 128 * t:128 * t + 128],
                                         pt[:, 256 * t + 128 * kb:256 * t + 128 * kb + 128],
                                         VN[:, kb, 128 * h:128 * h + 128], kb == 0, kb == 1))
                    return tk

                def finish(o, ri, toks):
                    tf = V.do(P(nc.vector.tensor_tensor, QN[:, h, :].rearrange("p (t n) -> p t n", t=2),
                                o.rearrange("p (t n) -> p t n", t=2), ri.unsqueeze(2).to_broadcast([128, 2, 128]),
                                ALU.mult), toks)
                    on_done.append(tf)
                    return tf

                return attend(scores, 2, 256, 1.0, None, pslots, 4, pv, 256, finish)

            oa_done, on_done, nBa, nBb = [], [], [], []

            def branch_a():
                yield from pipelined([da_unit(h, t) for h in range(4) for t in range(2)], 2)
                tt = []
                for t in range(2):
                    v = QA[:, :, 128 * t:128 * t + 128]
                    t8 = TMP[:, 0:1024].rearrange("p (k n) -> p k n", k=8)
                    a = V.do(P(nc.vector.tensor_tensor, t8, v, v, ALU.mult), oa_done, V.now())
                    yield
                    s8, s4 = stat(8), stat(4)
                    a = V.do(P(nc.vector.tensor_reduce, s8, t8, AX.X, ALU.add), a)
                    s82 = s8.rearrange("p (h c) -> p h c", c=2)
                    a = V.do(P(nc.vector.tensor_tensor, s4.unsqueeze(2), s82[:, :, 0:1], s82[:, :, 1:2], ALU.add), a)
                    r, a = rstd(s4, 4, 256, a, 1.0 - (0.8 - 0.6 * float(np.exp(-0.0))))
                    v4 = v.rearrange("p (h c) n -> p h c n", c=2)
                    for c in range(2):
                        tt.append(V.do(P(nc.vector.tensor_tensor, v4[:, :, c, :], v4[:, :, c, :],
                                         r.unsqueeze(2).to_broadcast([128, 4, 128]), ALU.mult), a))
                    yield
                yield from trans_split(lambda kt, t: QA[:, kt, 128 * t:128 * t + 128], 8, hl(BH, 0), hl(BL, 0),
                                       lambda kt: GC[:, 86 + kt % 2:87 + kt % 2], tt, everything, nBa)

            def branch_b():
                yield from pipelined([na_unit(h) for h in range(8)], 2)
                yield from trans_split(lambda kt, t: QN[:, kt, 128 * t:128 * t + 128], 8, hl(BH, 8), hl(BL, 8),
                                       None, on_done, everything, nBb)

            nb_fetch(0)
            nb_fetch(1)
            for n, (name, dst, rp_, mul) in enumerate((("QA", QA, True, 1.0), ("KA", KA, True, 1.0), ("VA", VA, None, 1.0),
                                                       ("QN", QN, False, 128 ** -0.5), ("KN", KN, False, 1.0), ("VN", VN, None, 1.0))):
                for j in range(2):
                    pair, b, last = gemm("w_in_2", 16 * n + 8 * j, 16, AH, AL, nA, 2)
                    if rp_ is None:
                        tdone[name] += evac2(pair, b, last, lambda t: dst[:, t, 512 * j:512 * j + 512], everything)
                    else:
                        qk_post(pair, b, last, name, dst, j, rp_, mul)
                if name == "VA":
                    finish_tasks()
                    idle.append(branch_a())
            finish_idle()
            a_over = everyone()
            idle.append(branch_b())
            gate = [M[:, 2048 + 1024 * j:3072 + 1024 * j] for j in range(4)] + \
                   [Yf[:, 2048:3072], Yf[:, 3072:4096], M[:, 0:1024], M[:, 1024:2048]]
            gate = [g.rearrange("p (t n) -> p t n", t=2) for g in gate]
            t_gate = {}
            for j in range(8):
                pair, b, last = gemm("w_in_2", 96 + 8 * j, 16, AH, AL, nA, 2)
                if j == 4:
                    finish_idle()
                    b_over = everyone()
                w = a_over if j < 4 else b_over
                for t in range(2):
                    t_gate[j, t] = A.do(P(nc.scalar.activation, gate[j][:, t, :], b[t][:, :], ACT.Sigmoid), last, w)
                accs.give(pair, t_gate[j, 1])
            tm = []
            for j in range(4):
                pair, b, last = gemm("w_branch_a", 4 * j, 8, BH[:, 0:8, :], BL[:, 0:8, :], nBa)
                for t in range(2):
                    ta = V.do(P(nc.vector.tensor_tensor, gate[j][:, t, :], gate[j][:, t, :], b[t][:, :], ALU.mult),
                              last, t_gate[j, t])
                accs.give(pair, ta)
                pair, b, last = gemm("w_branch_b", 4 * j, 8, BH[:, 8:16, :], BL[:, 8:16, :], nBb)
                for t in range(2):
                    tb = V.do(P(nc.vector.tensor_tensor, gate[4 + j][:, t, :], gate[4 + j][:, t, :], b[t][:, :],
                                ALU.mult), last, t_gate[4 + j, t])
                    tm.append(V.do(P(nc.vector.tensor_tensor, gate[j][:, t, :], gate[j][:, t, :], gate[4 + j][:, t, :],
                                     ALU.add), tb, ta))
                accs.give(pair, tb)
                nC = [] if j == 0 else nC
                tasks.append(trans_split(lambda kt, t, j=j: gate[j][:, t, 128 * kt:128 * kt + 128], 4, hl(AH, 4 * j),
                                         hl(AL, 4 * j), None, [tm[-1], tm[-2]], [t_gate[7, 1]], nC))
            finish_tasks()
            everything = everyone()
            grow = M[:, 8192:10240]
            t_gw = load(grow, D["post_mix"].partition_broadcast(128), everything)
            ty = []
            for j in range(4):
                pair, b, last = gemm("w_out_2", 8 * j, 16, AH, AL, nC)
                ty += evac2(pair, b, last, lambda t: Y[:, t, 512 * j:512 * j + 512], everything)

            def residual(ty, t_gw, lastR):
                junk = M[:, 0:4096].rearrange("p (t n) -> p t n", t=2)
                r, tr = sum_squares(lambda t: Y[:, t, :], lambda t: junk[:, t, :], 2048, [ty, everything])
                ends = []
                for t in range(2):
                    a = V.do(P(nc.vector.scalar_tensor_tensor, out=Y[:, t, :], in0=Y[:, t, :], scalar=r[:, t:t + 1],
                               in1=grow, op0=ALU.mult, op1=ALU.mult), tr, t_gw)
                    ends.append(V.do(P(nc.vector.tensor_tensor, R[:, t, :], R[:, t, :], Y[:, t, :], ALU.add), a, lastR))
                return ends

            t_R = residual(ty, t_gw, t_R)
            everything = everyone()
            t_gw = load(grow, D["post_mlp"].partition_broadcast(128), everything)
            nA = norm_T(lambda t: R[:, t, :], 2048, 70, hl(AH), hl(AL), lambda t: Y[:, t, :], lambda t: Y[:, t, :],
                        [t_R, everything], [T.now()])
            y_free = everyone()
            toks_ = Slots([M[:, 4096 + 1024 * i:5120 + 1024 * i].rearrange("p (t n) -> p t n", t=2) for i in range(2)],
                          everything)
            wB, vdone = {s: [] for s in range(8)}, {}

            def up(s):
                for j in range(2):
                    pair, b, last = gemm("w_up", 16 * s + 8 * j, 16, AH, AL, nA)
                    ts, free = take(toks_)
                    te = []
                    for t in range(2):
                        a = A.do(P(nc.scalar.activation, ts[:, t, :], b[t][:, :], ACT.Relu), last, free)
                        te.append(V.do(P(nc.vector.tensor_tensor, ts[:, t, :], ts[:, t, :], ts[:, t, :], ALU.mult), a))
                    accs.give(pair, a)

                    def later(ts=ts, te=te, j=j):
                        o = 8 * (s % 2) + 4 * j
                        yield
                        yield from trans_split(lambda kt, t: ts[:, t, 128 * kt:128 * kt + 128], 4, hl(BH, o), hl(BL, o),
                                               None, te, [everything, vdone.get(s - 2)], wB[s])
                        toks_.give(ts, T.now())
                    tasks.append(later())

            ty = {}
            for s in range(9):
                if s < 8:
                    up(s)
                if s == 0:
                    continue
                d = s - 1
                while len(wB[d]) < 4:
                    step(0)
                o = 8 * (d % 2)
                for j in range(4):
                    pair, b, last = gemm("w_down", 16 * d + 4 * j, 8, BH[:, o:o + 8, :], BL[:, o:o + 8, :], wB[d])
                    c = slice(512 * j, 512 * j + 512)
                    if d == 0:
                        ty[j] = evac2(pair, b, last, lambda t: Y[:, t, c], y_free)
                    else:
                        for t in range(2):
                            a = V.do(P(nc.vector.tensor_tensor, Y[:, t, c], Y[:, t, c], b[t][:, :], ALU.add), last, ty[j])
                        ty[j] = [a]
                        accs.give(pair, a)
                vdone[d] = [last]
            t_R = residual(list(ty.values()), t_gw, t_R)

        finish_idle()
        assert at[0] == len(order)
        last = load(out.rearrange("(t p) n -> p t n", p=128), R[:, :, :], t_R, q=S)
        S.wait([last])
        if stage >= 2:
            S.wait([g_written, list(a_written.values())])

        block = ctx.enter_context(nc.Block())

        @block.sync
        def _(e):
            for f in S.q:
                f()

        @block.gpsimd
        def _(e):
            for f in G.q:
                f()

        @block.scalar
        def _(e):
            for f in A.q:
                f()

        @block.vector
        def _(e):
            for f in V.q:
                f()

        @block.tensor
        def _(e):
            for f in T.q:
                f()


def cut(w):
    K, N = w.shape
    v = w.reshape(K // 256, 2, 128, N // 512, 512).transpose(3, 0, 2, 1, 4)
    return np.ascontiguousarray(v).reshape(-1, 128, NPIECE)


def cut_down(w):
    return np.concatenate([cut(w[k:k + 1024]) for k in range(0, w.shape[0], 1024)])


def columns(g):
    return g.reshape(-1, 128).T


def spread(g):
    return np.broadcast_to(g.reshape(1, -1), (128, g.size))


def kernel(STAGE=9, **inputs):
    import numpy as np
    import concourse.bacc as bacc
    from concourse import mybir
    from concourse.bass_utils import run_bass_kernel_spmd as run

    I = {k: np.asarray(v) for k, v in inputs.items()}
    w_in = I["w_in"][0]
    lat, kvl, pe, qs, ks, vs = np.split(w_in, [512, 768, 832, 1856, 1984], axis=1)
    A = {}
    A["x"] = I["x"][0]
    A["consts"] = constants()
    A["gain_cols"] = np.concatenate(
        [columns(I[n][0]) for n in ("norm1_gain", "q_a_gain", "kv_a_gain", "group_out_gain", "norm2_gain",
                                    "norm_mix_pre_2", "norm_mlp_pre_2", "subln_w_2")], axis=1)
    A["gain_rows"] = np.concatenate(
        [spread(I[n][0]) for n in ("mla_q_gain", "mla_k_gain", "swa_q_gain", "swa_k_gain", "swa_sinks")], axis=1)
    pos = I["positions"][0]
    p = np.arange(128)
    kidx = 128 * np.arange(2)[None, :, None] + 32 * (p // 32)[:, None, None] + np.arange(32)[None, None, :]
    A["pos"] = np.concatenate([spread(pos), pos[kidx].reshape(128, 64), pos.reshape(2, 128).T], axis=1)
    table = np.zeros((4, 32, 4, 16), np.float32)
    for g in range(4):
        table[g, :, g, :] = I["rel_bias_table"]
    A["table"] = table.reshape(128, 64)
    A["w_in_a"] = cut(np.concatenate([lat, qs, kvl, ks, vs], axis=1))
    A["w_in_b"] = pe.reshape(16, 128, 64).transpose(1, 0, 2).reshape(1, 128, NPIECE)
    for n in ("w_q_b", "w_kv_b", "w_out", "peer_w_q"):
        A[n] = cut(I[n][0])
    A["sub_keys"] = I["peer_sub_keys"][0].reshape(2, 8, 128, 128).transpose(0, 3, 1, 2).reshape(2, 128, NPIECE)
    A["peer_u"] = cut(I["peer_u"][0].T)
    A["peer_v"] = cut_down(I["peer_v"][0])
    A["w_in_2"] = cut(I["w_in_2"][0])
    A["w_branch_a"] = cut(I["w_branch_a_2"][0])
    A["w_branch_b"] = cut(I["w_branch_b_2"][0])
    A["w_out_2"] = cut(I["w_out_2"][0])
    A["w_up"] = cut(I["w_up_2"][0])
    A["w_down"] = cut_down(I["w_down_2"][0])
    A["lam"] = np.concatenate([spread(I[n][0]) for n in ("lam_q1_2", "lam_k1_2", "lam_q2_2", "lam_k2_2")], axis=1)
    A["post_mix"] = I["norm_mix_post_2"][0]
    A["post_mlp"] = I["norm_mlp_post_2"][0]
    q = np.arange(256)
    dr = q[None, :] // 64 - q[:, None] // 64 + 7
    dc = np.clip(q[None, :] % 64 - q[:, None] % 64 + 15, 0, 30)
    nb = I["na_rpb_2"][0][:, dr, dc]
    A["na_bias"] = nb.reshape(8, 2, 128, 256).transpose(0, 2, 1, 3).reshape(8, 128, 512)

    nc = bacc.Bacc("TRN2", target_bir_lowering=False, num_devices=1)
    arrays, D = {}, {}
    for n, a in A.items():
        a = np.ascontiguousarray(a)
        arrays["in_" + n] = a
        D[n] = nc.dram_tensor("in_" + n, a.shape, mybir.dt.from_np(a.dtype), kind="ExternalInput").ap()
    D["scr_g"] = nc.dram_tensor("scr_g", (8, 128, 4096), mybir.dt.float32, kind="Internal").ap()
    D["scr_a"] = nc.dram_tensor("scr_a", (16, 128, 2048), mybir.dt.float32, kind="Internal").ap()
    o = nc.dram_tensor("out_0", (256, 2048), mybir.dt.float32, kind="ExternalOutput").ap()
    build(nc, D, o, STAGE)
    r = run(nc, [arrays], core_ids=[0])
    return r.results[0]["out_0"].reshape(1, 256, 2048)
```

```python
import numpy as np

NPIECE = 1024


def threshold_rows():
    import math
    thr = [float(b) for b in range(17)]
    for j in range(1, 16):
        thr.append(float(math.ceil(16.0 * 8.0 ** (j / 16.0) - 1e-9)))
    thr[0] = -3.0e38
    return np.array(thr + [3.0e38], np.float32)


def constants():
    p = np.arange(128)
    c = np.zeros((128, 882), np.float32)
    c[:, 0:128] = np.eye(128)
    c[:, 128:256] = np.where(p[None, :] <= p[:, None], 0.0, -1e30)
    c[:, 256:384] = np.where(p[None, :] > p[:, None], 0.0, -1e30)
    c[:, 384:512] = p[None, :]
    thr = threshold_rows()
    c[:, 512] = thr[p % 32]
    c[:, 513] = thr[p % 32 + 1]
    qc = p % 64
    start = np.clip(qc - 8, 0, 48)
    kc = np.arange(64)
    c[:, 514:578] = np.where((kc[None] >= start[:, None]) & (kc[None] < start[:, None] + 16), 0.0, -1e30)
    inv = (1.0 / (np.float32(10000.0) ** (np.arange(0, 128, 2, dtype=np.float32) / np.float32(128)))).astype(np.float32)
    ang = np.arange(256, dtype=np.float32)[:, None] * inv[None]
    c[:, 578:706] = np.cos(ang).astype(np.float32).reshape(2, 128, 64).transpose(1, 0, 2).reshape(128, 128)
    c[:, 706:834] = np.sin(ang).astype(np.float32).reshape(2, 128, 64).transpose(1, 0, 2).reshape(128, 128)
    c[:, 834:866] = (np.float32(10000.0) ** (-np.arange(32, dtype=np.float32) / np.float32(32)))[None]
    c[:, 866:882] = np.arange(16)[None]
    return c


def build(nc, D, out, stage=9):
    import math
    import concourse.bass as bass
    from concourse import mybir
    from contextlib import ExitStack
    from functools import partial as P

    f32, f32r = mybir.dt.float32, mybir.dt.float32r
    i32, u32 = mybir.dt.int32, mybir.dt.uint32
    ALU, ACT, AX = mybir.AluOpType, mybir.ActivationFunctionType, mybir.AxisListType
    NR, NH = 5, 3

    with ExitStack() as ctx:
        def sb(name, shape, dt=f32):
            return ctx.enter_context(nc.sbuf_tensor(name, shape, dt))

        def sem(name):
            return ctx.enter_context(nc.semaphore(name))

        raw = sb("raw", [128, NR, NPIECE])
        whi = sb("whi", [128, NH, NPIECE], f32r)
        wlo = sb("wlo", [128, NH, NPIECE], f32r)
        AH = sb("AH", [128, 16, 256], f32r)
        AL = sb("AL", [128, 16, 256], f32r)
        BH = sb("BH", [128, 16, 256], f32r)
        BL = sb("BL", [128, 16, 256], f32r)
        R = sb("R", [128, 2, 2048])
        Y = sb("Y", [128, 2, 2048])
        M = sb("M", [128, 12288])
        PTb = sb("PTb", [128, 2, 512])
        TMP = sb("TMP", [128, 1024])
        C = sb("C", [128, 882])
        GC = sb("GC", [128, 90])
        GR = sb("GR", [128, 528])
        POS = sb("POS", [128, 322], i32)
        ST = sb("ST", [128, 1150])
        banks = [ctx.enter_context(nc.psum_tensor(f"bank{i}", [128, 512], f32)) for i in range(8)]

        ident, causal, upper, iota = C[:, 0:128], C[:, 128:256], C[:, 256:384], C[:, 384:512]
        namask = C[:, 514:578]
        cos2 = C[:, 578:706].rearrange("p (t j) -> p t j", t=2)
        sin2 = C[:, 706:834].rearrange("p (t j) -> p t j", t=2)
        iota16 = C[:, 866:882]
        Yf = Y[:, :, :].rearrange("p t n -> p (t n)")
        Rf = R[:, :, :].rearrange("p t n -> p (t n)")

        def mv(a, n, src=None):
            return (M[:, a:a + n] if src is None else src[:, a:a + n])

        def bf(ap):
            return ap.bitcast(f32)

        class Queue:
            def __init__(self, wait, name):
                self.wait_ge, self.sem, self.n, self.q, self.seen = wait, sem(name), 0, [], {}

            def wait(self, toks):
                need = {}
                for tok in flat(toks):
                    s, v = tok
                    if need.get(s.name, (s, 0))[1] < v:
                        need[s.name] = (s, v)
                for name, (s, v) in need.items():
                    if self.seen.get(name, 0) < v:
                        self.seen[name] = v
                        self.q.append(P(self.wait_ge, s, v))

            def do(self, fn, *toks):
                self.wait(toks)
                self.n += 1
                self.q.append(P(signalled, fn, self.sem, 1))
                return (self.sem, self.n)

            def quiet(self, fn, *toks):
                self.wait(toks)
                self.q.append(fn)

            def dma(self, fn, s, count, *toks):
                self.wait(toks)
                self.q.append(P(signalled, fn, s, 16))
                return (s, count)

            def now(self):
                return (self.sem, self.n)

        def signalled(fn, s, n):
            fn().then_inc(s, n)

        def flat(toks):
            for t in toks:
                if t is None:
                    continue
                if isinstance(t, tuple) and len(t) == 2 and isinstance(t[1], int):
                    yield t
                else:
                    yield from flat(t)

        T = Queue(nc.tensor.wait_ge, "q_pe")
        A = Queue(nc.scalar.wait_ge, "q_act")
        V = Queue(nc.vector.wait_ge, "q_dve")
        G = Queue(nc.gpsimd.wait_ge, "q_pool")
        S = Queue(nc.sync.wait_ge, "q_sp")

        def everyone():
            return [q.now() for q in (T, A, V, G)]

        n_aux = [0]

        def load(dst, src, *toks, q=None):
            n_aux[0] += 1
            q = q or G
            e = nc.gpsimd if q is G else nc.sync
            return q.dma(P(e.dma_start, dst, src), sem(f"s_aux{n_aux[0]}"), 16, *toks)

        n_st = [0]

        def stat(n):
            a = n_st[0]
            n_st[0] += n
            assert n_st[0] <= 1150, n_st
            return ST[:, a:a + n]

        class Slots:
            def __init__(self, items, toks=()):
                self.free = [(i, list(toks)) for i in items]

            def give(self, item, *toks):
                self.free.append((item, list(toks)))

        tasks, idle = [], []

        def step(n_idle=1):
            for g in list(tasks):
                if next(g, 1) == 1:
                    tasks.remove(g)
            for _ in range(n_idle):
                if idle and next(idle[0], 1) == 1:
                    idle.pop(0)

        def take(slots):
            while not slots.free:
                step()
            return slots.free.pop(0)

        def wait_for(slots):
            while not slots.free:
                yield
            return slots.free.pop(0)

        def finish_tasks():
            while tasks:
                step(0)

        def finish_idle():
            while idle:
                step()
            finish_tasks()

        def pipelined(units, depth):
            active = []
            units = list(units)
            while units or active:
                if units and len(active) < depth:
                    active.append(units.pop(0))
                for g in list(active):
                    if next(g, 1) == 1:
                        active.remove(g)
                yield

        accs = Slots([0, 1])
        misc = Slots([4, 5, 6, 7])
        PT = Slots([0, 1])

        def lend_banks():
            for _ in range(2):
                pair, free = take(accs)
                misc.give(2 * pair, free)
                misc.give(2 * pair + 1, free)

        def return_banks():
            free = {b: f for b, f in misc.free}
            assert len(free) == 8
            misc.free[:] = [(b, f) for b, f in misc.free if b >= 4]
            for pair in range(2):
                accs.give(pair, free[2 * pair], free[2 * pair + 1])

        order = []

        def plan(name, first, n):
            order.extend((name, i) for i in range(first, first + n))

        plan("w_in_a", 0, 16)
        plan("w_in_b", 0, 1)
        plan("w_in_a", 16, 16)
        plan("w_q_b", 0, 6)
        plan("w_kv_b", 0, 4)
        plan("w_out", 0, 32)
        if stage >= 2:
            plan("peer_w_q", 0, 32)
            plan("peer_u", 0, 8)
            plan("sub_keys", 0, 2)
            plan("peer_u", 8, 248)
            plan("peer_v", 0, 256)
        if stage >= 3:
            plan("w_in_2", 0, 160)
            for j in range(4):
                plan("w_branch_a", 4 * j, 4)
                plan("w_branch_b", 4 * j, 4)
            plan("w_out_2", 0, 32)
            done_up = 0
            for s in range(9):
                if s < 8:
                    plan("w_up", 16 * s, 16)
                if s >= 1:
                    plan("w_down", 16 * (s - 1), 16)

        s_raw = [sem(f"s_raw{i}") for i in range(NR)]
        loaded, split, used = [], [], []
        at = [0]

        def ensure_split(i):
            while len(split) <= min(i, len(order) - 1):
                n = len(split)
                while len(loaded) <= min(n + NR - 1, len(order) - 1):
                    m = len(loaded)
                    name, k = order[m]
                    loaded.append(S.dma(P(nc.sync.dma_start, raw[:, m % NR, :], D[name][k, :, :]),
                                        s_raw[m % NR], 16 * (m // NR + 1),
                                        split[m - NR] if m >= NR else None))
                free = used[n - NH] if n >= NH else None
                h = A.do(P(nc.scalar.activation, whi[:, n % NH, :], raw[:, n % NR, :], ACT.Copy),
                         loaded[n], free)
                split.append(V.do(P(nc.vector.tensor_tensor, wlo[:, n % NH, :], raw[:, n % NR, :],
                                    bf(whi[:, n % NH, :]), ALU.subtract), h))

        def piece(name, k):
            i = at[0]
            assert order[i] == (name, k), (order[i], name, k)
            ensure_split(i + NH - 1 if i + NH - 1 < len(used) + NH else i)
            at[0] += 1
            return i % NH, split[i]

        def used_up(tok):
            used.append(tok)
            if at[0] < len(order):
                ensure_split(at[0] + NH - 2)

        def gemm(name, first, kts, lh, ll, ltok, step_idle=1):
            pair, free = take(accs)
            b = [banks[2 * pair], banks[2 * pair + 1]]
            n = kts // 2
            for c in range(n):
                while len(ltok) < min(c + 2, n):
                    step(0)
                slot, tok = piece(name, first + c)
                T.wait([tok, ltok[c], free])
                for kk in range(2):
                    kt = 2 * c + kk
                    w = slice(512 * kk, 512 * kk + 512)
                    for t in range(2):
                        a = slice(128 * t, 128 * t + 128)
                        first_mm, last_mm = kt == 0, kt == kts - 1
                        T.quiet(P(nc.tensor.matmul, b[t][:, :], lh[:, kt, a], whi[:, slot, w], start=first_mm, stop=False))
                        T.quiet(P(nc.tensor.matmul, b[t][:, :], lh[:, kt, a], wlo[:, slot, w], start=False, stop=False))
                        f = P(nc.tensor.matmul, b[t][:, :], ll[:, kt, a], whi[:, slot, w], start=False, stop=last_mm)
                        if kk == 1 and t == 1:
                            last = T.do(f)
                        else:
                            T.quiet(f)
                used_up(last)
                if c < n - 1:
                    step(step_idle)
            return pair, b, last

        def transposed(srcs, bank, *toks):
            T.wait(toks)
            for n, s in enumerate(srcs):
                f = P(nc.tensor.transpose, banks[bank][:, 128 * n:128 * n + 128], s, ident)
                if n == len(srcs) - 1:
                    return T.do(f)
                T.quiet(f)

        def trans_split(src, kts, hi, lo, gcol, toks, free, done, pause=True):
            for k0 in range(0, kts, 2):
                bank, bfree = yield from wait_for(misc)
                tk = transposed([src(k0 + i, t) for i in range(2) for t in range(2)], bank, toks, bfree)
                if pause:
                    yield
                b = banks[bank][:, :].rearrange("p (k n) -> p k n", k=2)
                if gcol is None:
                    h = A.do(P(nc.scalar.activation, hi(k0, 2), b, ACT.Copy), tk, free)
                    low = V.do(P(nc.vector.tensor_tensor, lo(k0, 2), b, bf(hi(k0, 2)), ALU.subtract), h, free)
                else:
                    for i in range(2):
                        h = A.do(P(nc.scalar.activation, hi(k0 + i, 1), b[:, i:i + 1, :], ACT.Copy,
                                   scale=gcol(k0 + i)), tk, free)
                    for i in range(2):
                        low = V.do(P(nc.vector.scalar_tensor_tensor, out=lo(k0 + i, 1), in0=b[:, i:i + 1, :],
                                     scalar=gcol(k0 + i), in1=bf(hi(k0 + i, 1)), op0=ALU.mult,
                                     op1=ALU.subtract), h, free)
                misc.give(bank, low)
                done.append(low)
                yield

        def run(gen):
            for _ in gen:
                step(0)

        def rstd(ss, n, F, toks, mul=1.0):
            m, q, r = stat(n), stat(n), stat(n)
            t1 = V.do(P(nc.vector.tensor_scalar, m, ss, 1.0 / F, 1e-6, ALU.mult, ALU.add), toks)
            t2 = A.do(P(nc.scalar.activation, q, m, ACT.Sqrt), t1)
            t3 = V.do(P(nc.vector.reciprocal, r, q), t2)
            if mul != 1.0:
                t3 = V.do(P(nc.vector.tensor_scalar, r, r, mul, None, ALU.mult), t3)
            return r, t3

        def sum_squares(src, junk, F, toks):
            ss = stat(2)
            t0 = A.do(P(nc.scalar.activation, junk(0), src(0), ACT.Square, accum_out=ss[:, 0:1]), toks)
            t1 = V.do(P(nc.vector.tensor_tensor_reduce, out=junk(1), in0=src(1), in1=src(1), scale=1.0,
                        scalar=0.0, op0=ALU.mult, op1=ALU.add, accum_out=ss[:, 1:2]), toks)
            return rstd(ss, 2, F, [t0, t1])

        def norm_T(src, F, g0, hi, lo, dst, toks, free, ssp=None, done=None):
            if ssp is None:
                r, tr = sum_squares(src, dst, F, [toks, free])
            else:
                ss = stat(2)
                t = V.do(P(nc.vector.tensor_reduce, ss, ssp, AX.X, ALU.add), toks)
                r, tr = rstd(ss, 2, F, t)
            queue = done is None
            done = [] if queue else done

            def later():
                n = min(F, 512)
                for c in range(0, F, n):
                    t0 = A.do(P(nc.scalar.activation, dst(0)[:, c:c + n], src(0)[:, c:c + n], ACT.Copy,
                                scale=r[:, 0:1]), tr, free)
                    t1 = V.do(P(nc.vector.tensor_scalar, dst(1)[:, c:c + n], src(1)[:, c:c + n], r[:, 1:2], None,
                                ALU.mult), tr, free)
                    k = c // 128
                    yield from trans_split(lambda kt, t: dst(t)[:, c + 128 * kt:c + 128 * kt + 128], n // 128,
                                           lambda kt, m: hi(k + kt, m), lambda kt, m: lo(k + kt, m),
                                           lambda kt: GC[:, g0 + k + kt:g0 + k + kt + 1], [t0, t1], free, done,
                                           pause=False)
            if not queue:
                return later()
            tasks.append(later())
            return done

        def chained(gens):
            for g in gens:
                yield from g

        def hl(buf, k0=0):
            return lambda kt, n: buf[:, k0 + kt:k0 + kt + n, :]

        def head_norm(x, U, L, gain, mul, tmp, toks):
            t1 = A.do(P(nc.scalar.activation, tmp, x, ACT.Square), toks)
            ss = stat(U)
            t2 = V.do(P(nc.vector.tensor_reduce, ss, tmp, AX.X, ALU.add), t1)
            r, t3 = rstd(ss, U, L, t2, mul)
            t4 = V.do(P(nc.vector.tensor_tensor, x, x, r.unsqueeze(2).to_broadcast([128, U, L]), ALU.mult), t3)
            return V.do(P(nc.vector.tensor_tensor, x, x, gain.unsqueeze(1).to_broadcast([128, U, L]), ALU.mult), t4)

        def rope(x, U, H, c, s, toks):
            n = U * 2 * H
            a = TMP[:, 0:n].rearrange("p (u c h) -> p u c h", u=U, c=2)
            b = TMP[:, 512:512 + n].rearrange("p (u c h) -> p u c h", u=U, c=2)
            cb = c.unsqueeze(1).to_broadcast([128, U, H])
            sn = s.unsqueeze(1).to_broadcast([128, U, H])
            w = [toks, V.now()]
            t = []
            for i in range(2):
                t.append(V.do(P(nc.vector.tensor_tensor, a[:, :, i, :], x[:, :, i, :], cb, ALU.mult), w))
                t.append(V.do(P(nc.vector.tensor_tensor, b[:, :, i, :], x[:, :, 1 - i, :], sn, ALU.mult), w))
            V.do(P(nc.vector.tensor_tensor, x[:, :, 0, :], a[:, :, 0, :], b[:, :, 0, :], ALU.subtract), t)
            return V.do(P(nc.vector.tensor_tensor, x[:, :, 1, :], a[:, :, 1, :], b[:, :, 1, :], ALU.add), t)

        def attend(scores, U, nk, scale, sink, pslots, blocks, pv, out_cols, finish, combine=None, per_head=None,
                   slack=False):
            bank, bfree = yield from wait_for(misc)
            tk = scores(bank, bfree)
            yield
            sv = banks[bank][:, 0:U * nk].rearrange("p (u k) -> p u k", u=U)
            m, nm, sm, ri = stat(U), stat(U), stat(U), stat(U)
            t1 = V.do(P(nc.vector.tensor_reduce, m, sv, AX.X, ALU.max), tk)
            if sink is not None:
                t1 = V.do(P(nc.vector.tensor_tensor, m, m, sink, ALU.max), t1)
            if per_head is None:
                t2 = V.do(P(nc.vector.tensor_scalar, nm, m, -scale, None, ALU.mult), t1)
            else:
                t2 = V.do(P(nc.vector.scalar_tensor_tensor, out=nm, in0=m, scalar=-1.0, in1=per_head, op0=ALU.mult,
                            op1=ALU.mult), t1)
            ps, pfree = yield from wait_for(pslots)
            for u in range(U):
                te = A.do(P(nc.scalar.activation, ps[:, u * nk:(u + 1) * nk], sv[:, u, :], ACT.Exp,
                            bias=nm[:, u:u + 1], scale=scale if per_head is None else per_head[:, u:u + 1], accum_out=sm[:, u:u + 1]), t2, pfree)
            misc.give(bank, te, t1)
            ts = te
            if sink is not None:
                es, ee = stat(U), stat(U)
                t3 = V.do(P(nc.vector.tensor_tensor, es, sink, m, ALU.subtract), t1)
                t4 = A.do(P(nc.scalar.activation, ee, es, ACT.Exp), t3)
                ts = V.do(P(nc.vector.tensor_tensor, sm, sm, ee, ALU.add), t4, te)
            tr = V.do(P(nc.vector.reciprocal, ri, sm), ts)
            if combine is not None:
                te = combine(ps, ri, [te, tr])
            yield
            if slack:
                yield
            bank, bfree = yield from wait_for(misc)
            tk = transposed([ps[:, 128 * n:128 * n + 128] for n in range(blocks)], bank, te, bfree)
            pslots.give(ps, tk)
            yield
            pt, tfree = yield from wait_for(PT)
            eng = alt[0]
            alt[0] = 1 - eng
            if eng:
                tc = A.do(P(nc.scalar.activation, PTb[:, pt, 0:128 * blocks], banks[bank][:, 0:128 * blocks],
                            ACT.Copy), tk, tfree)
            else:
                tc = V.do(P(nc.vector.tensor_copy, PTb[:, pt, 0:128 * blocks], banks[bank][:, 0:128 * blocks]),
                          tk, tfree)
            misc.give(bank, tc)
            yield
            bank, bfree = yield from wait_for(misc)
            tk = pv(bank, PTb[:, pt, :], [tc, bfree])
            PT.give(pt, tk)
            yield
            tf = finish(banks[bank][:, 0:out_cols], ri, [tk, tr])
            misc.give(bank, tf)

        alt = [0]

        def mm(outp, l, r, start, stop):
            return P(nc.tensor.matmul, outp, l, r, start=start, stop=stop)

        t_x = load(R[:, :, :], D["x"].rearrange("(t p) n -> p t n", p=128), q=S)
        t_c = load(C[:, :], D["consts"], q=S)
        t_gc = load(GC[:, :], D["gain_cols"])
        t_pos = load(POS[:, :], D["pos"])
        t_gr = load(GR[:, :], D["gain_rows"])
        BD = stat(64)
        t_bd = load(BD, D["table"])
        consts = [t_c, t_gc]

        for q in (T, A, V):
            q.wait(consts)

        nA = norm_T(lambda t: R[:, t, :], 2048, 0, hl(AH), hl(AL), lambda t: Y[:, t, :], [t_x], None)

        bias = M[:, 0:6144].rearrange("p (h s k) -> p h s k", h=16, s=3)
        OH = [Y[:, i, 0:1024].rearrange("p (k q) -> p k q", k=8) for i in range(2)]
        dist = [Y[:, i, 1024:2048].bitcast(i32).rearrange("p (k q) -> p k q", k=8) for i in range(2)]
        bias_done = []

        def bias_gen():
            chunks = [(pair, qb, kb, c) for pair, (qb, kb) in enumerate([(0, 0), (1, 0), (1, 1)]) for c in range(4)]
            td, t2, tk = {}, {}, {}

            def sub(n):
                pair, qb, kb, c = chunks[n]
                pq = POS[:, 128 * qb:128 * qb + 128].unsqueeze(1).to_broadcast([128, 8, 128])
                pk = POS[:, 256 + 32 * kb + 8 * c:256 + 32 * kb + 8 * c + 8].unsqueeze(2).to_broadcast([128, 8, 128])
                td[n] = G.do(P(nc.gpsimd.tensor_tensor, dist[n % 2], pq, pk, ALU.subtract), t_pos,
                             t2[n - 2] if n >= 2 else x_read)

            def hot(n):
                i = n % 2
                t1 = V.do(P(nc.vector.tensor_scalar, OH[i], dist[i], C[:, 512:513], None, ALU.is_ge), td[n],
                          tk[n - 2] if n >= 2 else x_read)
                t2[n] = V.do(P(nc.vector.scalar_tensor_tensor, out=OH[i], in0=dist[i], scalar=C[:, 513:514],
                               in1=OH[i], op0=ALU.is_lt, op1=ALU.mult), t1)

            sub(0)
            sub(1)
            yield
            for n in range(13):
                if n < 12:
                    hot(n)
                    if n + 2 < 12:
                        sub(n + 2)
                yield
                if n == 0:
                    continue
                m = n - 1
                pair, qb, kb, c = chunks[m]
                bank, bfree = yield from wait_for(misc)
                T.wait([t2[m], t_bd, bfree])
                for k in range(8):
                    f = mm(banks[bank][:, 64 * k:64 * k + 64], OH[m % 2][:, k, :], BD, True, True)
                    if k < 7:
                        T.quiet(f)
                tk[m] = T.do(f)
                mask = upper if pair == 1 else causal
                bv = banks[bank][:, :].rearrange("p (k g h) -> p g h k", k=8, g=4)
                for g in range(4):
                    o = 32 * g + 8 * c
                    tb = V.do(P(nc.vector.tensor_tensor, bias[:, :, pair, o:o + 8], bv[:, g],
                                mask[:, o:o + 8].unsqueeze(1).to_broadcast([128, 16, 8]), ALU.add), tk[m])
                misc.give(bank, tb)
                bias_done.append(tb)
                yield

        CS = stat(128).rearrange("p (c t j) -> p c t j", c=2, t=2)

        def rope_tables():
            pf = stat(2)
            ang, nn, r, ab = [TMP[:, 64 * i:64 * i + 64].rearrange("p (t j) -> p t j", t=2) for i in range(4)]
            t = V.do(P(nc.vector.tensor_copy, pf, POS[:, 320:322]), t_pos)
            for i in range(2):
                last = V.do(P(nc.vector.tensor_scalar, ang[:, i, :], C[:, 834:866], pf[:, i:i + 1], None, ALU.mult), t)
            t = last
            t = V.do(P(nc.vector.tensor_scalar, nn, ang, 1.0 / (2 * math.pi), 12582912.0, ALU.mult, ALU.add), t)
            t = V.do(P(nc.vector.tensor_scalar, nn, nn, -12582912.0, None, ALU.add), t)
            rest = 2 * math.pi
            src = ang
            for bits in (8, 19, 30, None):
                if bits is None:
                    part = rest
                else:
                    part = math.floor(rest * 2.0 ** (bits - 3)) / 2.0 ** (bits - 3)
                rest -= part
                t = V.do(P(nc.vector.scalar_tensor_tensor, out=r, in0=nn, scalar=-part, in1=src, op0=ALU.mult,
                           op1=ALU.add), t)
                src = r
            t = V.do(P(nc.vector.tensor_scalar, r, r, 3.1415925, -3.1415925, ALU.min, ALU.max), t)
            t1 = V.do(P(nc.vector.scalar_tensor_tensor, out=ab, in0=r, scalar=-1.0, in1=r, op0=ALU.mult, op1=ALU.min), t)
            t1 = V.do(P(nc.vector.tensor_scalar, ab, ab, math.pi / 2, None, ALU.add), t1)
            A.do(P(nc.scalar.activation, CS[:, 0], ab, ACT.Sin), t1)
            return A.do(P(nc.scalar.activation, CS[:, 1], r, ACT.Sin), t)

        def evac2(pair, b, last, dst, *toks):
            t0 = A.do(P(nc.scalar.activation, dst(0), b[0][:, :], ACT.Copy), last, toks)
            t1 = V.do(P(nc.vector.tensor_copy, dst(1), b[1][:, :]), last, toks)
            accs.give(pair, t0, t1)
            return [t0, t1]

        def row2(a, n, src):
            return src[:, a:a + n].rearrange("p (t n) -> p t n", t=2)

        swa_k = row2(8704, 1024, M)
        qswT = M[:, 6144:8192].rearrange("p (k n) -> p k n", k=8)
        kswT = M[:, 8192:8704].rearrange("p (k n) -> p k n", k=2)
        kdup = M[:, 11264:11776].rearrange("p (t k d n) -> p t k d n", t=2, k=2, d=2)
        kpe = row2(11776, 128, M)
        qlat, qtmp = row2(0, 1024, Rf), row2(1024, 1024, Rf)
        kvtmp = PTb[:, :, 0:256]
        gq, gk = GR[:, 0:192], GR[:, 192:384]
        gsq, gsk, sinks = GR[:, 384:448], GR[:, 448:512], GR[:, 512:528]

        pair, b, last = gemm("w_in_a", 0, 16, AH, AL, nA)
        finish_tasks()
        x_read = everyone()
        t_rope = rope_tables()
        te = evac2(pair, b, last, lambda t: qlat[:, t, :], x_read)
        nQ = norm_T(lambda t: qlat[:, t, :], 512, 16, hl(BH), hl(BL), lambda t: qtmp[:, t, :], te, x_read)
        toks_ = Slots([row2(2048 + 1024 * i, 1024, Rf) for i in range(2)], x_read)
        idle.append(bias_gen())
        pair, b, last = gemm("w_in_a", 8, 16, AH, AL, nA, 2)
        te = evac2(pair, b, last, lambda t: swa_k[:, t, :], x_read)
        nKV = norm_T(lambda t: swa_k[:, t, 0:256], 256, 20, hl(BH, 4), hl(BL, 4), lambda t: kvtmp[:, t, :], te, None)
        t_ksw, t_kpe = [], []

        def k_side(te=te):
            for t in range(2):
                kv = swa_k[:, t, 256:384].rearrange("p (u l) -> p u l", u=2)
                tn = head_norm(kv, 2, 64, gsk, 1.0, TMP[:, 128 * t:128 * t + 128].rearrange("p (u l) -> p u l", u=2),
                               [te, t_gr, t_rope, V.now()])
                for d in range(2):
                    tn = V.do(P(nc.vector.tensor_copy, kdup[:, t, :, d, :], kv), tn)
                yield
            bank, bfree = yield from wait_for(misc)
            tk = transposed([kdup[:, t, k].rearrange("p d n -> p (d n)") for k in range(2) for t in range(2)],
                            bank, tn, bfree)
            tc = A.do(P(nc.scalar.activation, kswT, banks[bank][:, :].rearrange("p (k n) -> p k n", k=2), ACT.Copy), tk)
            misc.give(bank, tc)
            t_ksw.append(tc)

        tasks.append(k_side())

        slot, tok = piece("w_in_b", 0)
        pair, free = take(accs)
        T.wait([tok, free])
        for t in range(2):
            for kt in range(16):
                w = slice(64 * kt, 64 * kt + 64)
                a = slice(128 * t, 128 * t + 128)
                o = banks[2 * pair + t][:, 0:64]
                T.quiet(mm(o, AH[:, kt, a], whi[:, slot, w], kt == 0, False))
                T.quiet(mm(o, AH[:, kt, a], wlo[:, slot, w], False, False))
                last = T.do(mm(o, AL[:, kt, a], whi[:, slot, w], False, kt == 15))
        used_up(last)
        t0 = A.do(P(nc.scalar.activation, kpe[:, 0, :], banks[2 * pair][:, 0:64], ACT.Copy), last)
        t1 = V.do(P(nc.vector.tensor_copy, kpe[:, 1, :], banks[2 * pair + 1][:, 0:64]), last)
        accs.give(pair, t0, t1)
        t_kpe = [t0, t1]
        step()

        qsw_t = []

        def q_side(ts, te, j):
            for t in range(2):
                xv = ts[:, t, :].rearrange("p (u l) -> p u l", u=8)
                tn = head_norm(xv, 8, 64, gsq, 0.125, TMP[:, 512 * t:512 * t + 512].rearrange("p (u l) -> p u l", u=8),
                               [te, t_gr, V.now(), A.now()])
                yield
            for k0 in (0, 2):
                bank, bfree = yield from wait_for(misc)
                tk = transposed([ts[:, t, 128 * (k0 + i):128 * (k0 + i) + 128] for i in range(2) for t in range(2)],
                                bank, tn, bfree)
                tc = A.do(P(nc.scalar.activation, qswT[:, 4 * j + k0:4 * j + k0 + 2, :],
                            banks[bank][:, :].rearrange("p (k n) -> p k n", k=2), ACT.Copy), tk)
                misc.give(bank, tc)
                qsw_t.append(tc)
            toks_.give(ts, tk)

        for j in range(2):
            pair, b, last = gemm("w_in_a", 16 + 8 * j, 16, AH, AL, nA, 2)
            ts, free = take(toks_)
            te = evac2(pair, b, last, lambda t: ts[:, t, :], free)
            tasks.append(q_side(ts, te, j))
        a_free = [last]

        OM, OS = Y[:, :, 0:1024], Y[:, :, 1024:2048]
        ps3 = [M[:, 9728 + 512 * i:9728 + 512 * i + 512] for i in range(3)]
        psw = Slots(ps3)
        os_done = []

        def swa_unit(t, h0):
            U = 2 if t else 4
            nk = 256 if t else 128

            def scores(bank, bfree):
                T.wait([qsw_t, t_ksw, bias_done[-1], bfree])
                for u in range(U):
                    h = h0 + 2 * u
                    p0 = 64 * (h % 2)
                    o = banks[bank][:, u * nk:(u + 1) * nk]
                    bs = bias[:, h, 1:3, :].rearrange("p s k -> p (s k)") if t else bias[:, h, 0, :]
                    T.quiet(mm(o, ident, bs, True, False))
                    f = mm(o, qswT[p0:p0 + 64, h // 2, 128 * t:128 * t + 128], kswT[p0:p0 + 64, h // 8, 0:nk],
                           False, True)
                    tk = T.do(f)
                return tk

            def pv(bank, pt, toks):
                T.wait(toks)
                for u in range(U):
                    kvh = h0 // 8
                    for kb in range(nk // 128):
                        f = mm(banks[bank][:, 64 * u:64 * u + 64], pt[:, u * nk + 128 * kb:u * nk + 128 * kb + 128],
                               swa_k[:, kb, 384 + 64 * kvh:448 + 64 * kvh], kb == 0, kb == nk // 128 - 1)
                        tk = T.do(f)
                return tk

            def finish(o, ri, toks):
                tf = V.do(P(nc.vector.tensor_tensor,
                            OS[:, t, :].rearrange("p (u l) -> p u l", u=16)[:, h0:h0 + 2 * U - 1:2, :],
                            o.rearrange("p (u l) -> p u l", u=U), ri.unsqueeze(2).to_broadcast([128, U, 64]),
                            ALU.mult), toks, bias_done[-1])
                os_done.append(tf)
                return tf

            return attend(scores, U, nk, 1.0, sinks[:, h0:h0 + 2 * U - 1:2], psw, 4, pv, 64 * U, finish)

        finish_idle()
        idle.append(pipelined([swa_unit(0, h) for h in (0, 1, 8, 9)] +
                              [swa_unit(1, h) for h in (0, 1, 4, 5, 8, 9, 12, 13)], 3))

        VM = row2(0, 2048, Rf)
        rq, rk = stat(16).rearrange("p (t h) -> p t h", t=2), stat(16).rearrange("p (t h) -> p t h", t=2)
        ssq, ssk = stat(32).rearrange("p (a t h) -> p a t h", a=2, t=2), stat(16).rearrange("p (t h) -> p t h", t=2)
        sspe = stat(2)
        t_ssq, qt_done, kt_done, t_rq, t_rk = [], [], [], [], []
        TM = [TMP[:, 512 * t:512 * t + 512] for t in range(2)]

        def squares(x, t, U, L, out, toks):
            tmp = TM[t][:, 0:U * L].rearrange("p (u l) -> p u l", u=U)
            a = A.do(P(nc.scalar.activation, tmp, x, ACT.Square), toks, V.now())
            return V.do(P(nc.vector.tensor_reduce, out, tmp, AX.X, ALU.add), a)

        def small_rsqrt(out, ss, toks, mul):
            a = V.do(P(nc.vector.tensor_scalar, out, ss, 1.0 / 192, 1e-6, ALU.mult, ALU.add), toks)
            a = A.do(P(nc.scalar.activation, out, out, ACT.Sqrt), a)
            a = V.do(P(nc.vector.reciprocal, out, out), a)
            if mul != 1.0:
                a = V.do(P(nc.vector.tensor_scalar, out, out, mul, None, ALU.mult), a)
            return a

        def q_nope(ts, te, j):
            for t in range(2):
                t_ssq.append(squares(ts[:, t, :].rearrange("p (u l) -> p u l", u=4), t, 4, 128,
                                     ssq[:, 0, t, 4 * j:4 * j + 4], te))
                yield
            yield from trans_split(lambda kt, t: ts[:, t, 128 * kt:128 * kt + 128], 4, hl(AH, 4 * j), hl(AL, 4 * j),
                                   lambda kt: GC[:, 88:89], te, a_free, qt_done)
            toks_.give(ts, t_ssq, T.now())

        def q_rope(ts, te, j):
            tr = []
            for t in range(2):
                x = ts[:, t, :].rearrange("p (u l) -> p u l", u=8)
                a = squares(x, t, 8, 64, ssq[:, 1, t, :], te)
                a = V.do(P(nc.vector.tensor_tensor, x, x, gq[:, 128:192].unsqueeze(1).to_broadcast([128, 8, 64]),
                           ALU.mult), a, t_gr)
                yield
                tr.append(rope(ts[:, t, :].rearrange("p (u c h) -> p u c h", u=8, c=2), 8, 32, CS[:, 0, t],
                               CS[:, 1, t], [a, t_rope]))
                yield
            a = V.do(P(nc.vector.tensor_tensor, rq, ssq[:, 0], ssq[:, 1], ALU.add), t_ssq, V.now())
            t_rq.append(small_rsqrt(rq, rq, a, 192 ** -0.5))
            yield from trans_split(lambda kt, t: ts[:, t, 128 * kt:128 * kt + 128], 4, hl(AH, 8), hl(AL, 8),
                                   None, tr, a_free, qt_done)
            toks_.give(ts, T.now())

        def k_nope(ts, te, j):
            h = slice(4 * j, 4 * j + 4)
            tn = []
            for t in range(2):
                x = ts[:, t, :].rearrange("p (u l) -> p u l", u=4)
                a = squares(x, t, 4, 128, ssk[:, t, h], te)
                if j == 0:
                    a2 = A.do(P(nc.scalar.activation, TM[t][:, 0:64], kpe[:, t, :], ACT.Square,
                                accum_out=sspe[:, t:t + 1]), t_kpe, a)
                    a = [a, a2]
                a = V.do(P(nc.vector.tensor_scalar, rk[:, t, h], ssk[:, t, h], sspe[:, t:t + 1], None, ALU.add), a)
                a = small_rsqrt(rk[:, t, h], rk[:, t, h], a, 1.0)
                t_rk.append(a)
                tn.append(V.do(P(nc.vector.tensor_tensor, x, x, rk[:, t, h].unsqueeze(2).to_broadcast([128, 4, 128]),
                                 ALU.mult), a))
                yield
            yield from trans_split(lambda kt, t: ts[:, t, 128 * kt:128 * kt + 128], 4, hl(BH, 6 + 4 * j),
                                   hl(BL, 6 + 4 * j), lambda kt: GC[:, 89:90], tn, None, kt_done)
            toks_.give(ts, T.now())

        def k_rope():
            ts, free = yield from wait_for(toks_)
            while len(t_rk) < 4:
                yield
            tr = []
            for t in range(2):
                a = V.do(P(nc.vector.tensor_tensor, kpe[:, t, :], kpe[:, t, :], gk[:, 128:192], ALU.mult), t_kpe, t_gr,
                         t_rk, A.now())
                a = rope(kpe[:, t, :].rearrange("p (u c h) -> p u c h", u=1, c=2), 1, 32, CS[:, 0, t], CS[:, 1, t],
                         [a, t_rope])
                tr.append(V.do(P(nc.vector.tensor_tensor, ts[:, t, :].rearrange("p (h n) -> p h n", h=8),
                                 kpe[:, t, :].unsqueeze(1).to_broadcast([128, 8, 64]),
                                 rk[:, t, :].unsqueeze(2).to_broadcast([128, 8, 64]), ALU.mult), a, free))
                yield
            yield from trans_split(lambda kt, t: ts[:, t, 128 * kt:128 * kt + 128], 4, hl(AH, 12), hl(AL, 12),
                                   None, tr, a_free, kt_done)
            toks_.give(ts, T.now())

        for j in range(3):
            pair, b, last = gemm("w_q_b", 2 * j, 4, BH, BL, nQ, 2)
            ts, free = take(toks_)
            te = evac2(pair, b, last, lambda t: ts[:, t, :], free)
            tasks.append(q_nope(ts, te, j) if j < 2 else q_rope(ts, te, j))
            step(2)
        t_v = []
        for j in range(4):
            pair, b, last = gemm("w_kv_b", j, 2, BH[:, 4:6, :], BL[:, 4:6, :], nKV, 2)
            if j < 2:
                ts, free = take(toks_)
                te = evac2(pair, b, last, lambda t: ts[:, t, :], free)
                tasks.append(k_nope(ts, te, j))
                step(2)
            else:
                t_v += evac2(pair, b, last, lambda t: VM[:, t, 512 * (j - 2):512 * (j - 2) + 512], x_read, T.now())
        tasks.append(k_rope())
        lend_banks()
        finish_idle()
        pml = Slots(ps3 + [M[:, 11264:11776], M[:, 0:512], M[:, 512:1024]], everyone())
        om_free = everyone()
        om_done = []

        def mla_unit(t, h0):
            U = 2 if t else 4
            nk = 256 if t else 128

            def scores(bank, bfree):
                T.wait([qt_done, kt_done, bfree])
                a = slice(128 * t, 128 * t + 128)
                for u in range(U):
                    h = h0 + 2 * u
                    p = slice(64 * (h % 2), 64 * (h % 2) + 64)
                    o = banks[bank][:, u * nk:(u + 1) * nk]
                    r, q = 8 + h // 2, 12 + h // 2
                    for i, (ql, kl) in enumerate(((AH, BH), (AH, BL), (AL, BH))):
                        T.quiet(mm(o, ql[:, h, a], kl[:, 6 + h, 0:nk], i == 0, False))
                    for ql, kl in ((AH, AH), (AH, AL), (AL, AH)):
                        T.quiet(mm(o, ql[p, r, a], kl[p, q, 0:nk], False, False))
                    tk = T.do(mm(banks[bank][:, u * nk + 128 * t:u * nk + 128 * t + 128], ident, causal, False, True))
                return tk

            def pv(bank, pt, toks):
                T.wait([toks, t_v])
                for u in range(U):
                    v0 = 128 * (h0 + 2 * u)
                    for kb in range(nk // 128):
                        tk = T.do(mm(banks[bank][:, 128 * u:128 * u + 128],
                                     pt[:, u * nk + 128 * kb:u * nk + 128 * kb + 128],
                                     VM[:, kb, v0:v0 + 128], kb == 0, kb == nk // 128 - 1))
                return tk

            def finish(o, ri, toks):
                tf = V.do(P(nc.vector.tensor_tensor,
                            OM[:, t, :].rearrange("p (u l) -> p u l", u=8)[:, h0:h0 + 2 * U - 1:2, :],
                            o.rearrange("p (u l) -> p u l", u=U), ri.unsqueeze(2).to_broadcast([128, U, 128]),
                            ALU.mult), toks, om_free)
                om_done.append(tf)
                return tf

            return attend(scores, U, nk, None, None, pml, 4, pv, 128 * U, finish,
                          per_head=rq[:, t, h0:h0 + 2 * U - 1:2])

        for q in (V, A):
            q.wait(t_rq)
        idle.append(pipelined([mla_unit(0, 0), mla_unit(0, 1)] + [mla_unit(1, h) for h in (0, 1, 4, 5)], 6))
        finish_idle()
        return_banks()
        everything = everyone()
        t_x = load(R[:, :, :], D["x"].rearrange("(t p) n -> p t n", p=128), everything, q=S)

        nM, gens = [], []
        for g, O in ((0, OM), (1, OS)):
            gens.append(norm_T(lambda t, O=O: O[:, t, :], 1024, 22 + 8 * g, hl(AH, 8 * g), hl(AL, 8 * g),
                               lambda t, g=g: row2(2048 * g, 2048, M)[:, t, :], everything, everything, done=nM))
        tasks.append(chained(gens))
        t_R = [t_x]
        ssr = stat(8).rearrange("p (t c) -> p t c", t=2)

        def add_residual(b, last, j, toks, final=True):
            c = slice(512 * j, 512 * j + 512)
            out = []
            for t in range(2):
                a = V.do(P(nc.vector.tensor_tensor, R[:, t, c], R[:, t, c], b[t][:, :], ALU.add), last, toks)
                out.append(a)
            if final:
                for t in range(2):
                    out.append(A.do(P(nc.scalar.activation, Y[:, t, c], R[:, t, c], ACT.Square,
                                      accum_out=ssr[:, t, j:j + 1]), out[t]))
            return out

        for j in range(4):
            pair, b, last = gemm("w_out", 8 * j, 16, AH, AL, nM)
            if j == 0:
                finish_tasks()
                for q in (V, A):
                    q.wait(everyone())
            t_R += add_residual(b, last, j, t_x)
            accs.give(pair, t_R[-1], t_R[-3])

        if stage >= 2:
            everything = everyone()
            nA = norm_T(lambda t: R[:, t, :], 2048, 38, hl(AH), hl(AL), lambda t: Y[:, t, :], everything,
                        everything, ssp=ssr)
            toks_ = Slots([M[:, 1024 * i:1024 * i + 1024].rearrange("p (t n) -> p t n", t=2) for i in range(2)],
                          everything)
            nB = []

            def q_post(pair, b, last, j):
                ts, free = take(toks_)
                te = evac2(pair, b, last, lambda t: ts[:, t, :], free)

                def later():
                    yield
                    yield from trans_split(lambda kt, t: ts[:, t, 128 * kt:128 * kt + 128], 4, hl(BH, 4 * j),
                                           hl(BL, 4 * j), None, te, everything, nB)
                    toks_.give(ts, T.now())
                tasks.append(later())

            for j in range(4):
                pair, b, last = gemm("peer_w_q", 8 * j, 16, AH, AL, nA)
                q_post(pair, b, last, j)
            norm_read = everyone()
            SC = Y[:, :, :].rearrange("p t (h n) -> p t h n", h=16)
            t_sc = []

            def sub_scores():
                for c in range(2):
                    slot, tok = piece("sub_keys", c)
                    T.wait([tok, nB])
                    for q4 in range(2):
                        for t in range(2):
                            bank, bfree = take(misc)
                            T.wait([bfree])
                            for i in range(4):
                                hp = 8 * c + 4 * q4 + i
                                w = slice(128 * (4 * q4 + i), 128 * (4 * q4 + i) + 128)
                                a = slice(128 * t, 128 * t + 128)
                                o = banks[bank][:, 128 * i:128 * i + 128]
                                T.quiet(mm(o, BH[:, hp, a], whi[:, slot, w], True, False))
                                T.quiet(mm(o, BH[:, hp, a], wlo[:, slot, w], False, False))
                                last = T.do(mm(o, BL[:, hp, a], whi[:, slot, w], False, True))
                            h0 = 8 * c + 4 * q4
                            te = A.do(P(nc.scalar.activation, SC[:, t, h0:h0 + 4, :],
                                        banks[bank][:, :].rearrange("p (h n) -> p h n", h=4), ACT.Copy), last, norm_read)
                            misc.give(bank, te)
                            t_sc.append(te)
                    used_up(last)

            V16 = M[:, 4096:4608].rearrange("p (t h k) -> p t h k", t=2, h=16)
            I16 = M[:, 4608:5120].rearrange("p (t h k) -> p t h k", t=2, h=16)
            I16u = I16.bitcast(u32)
            cand = M[:, 5120:7168].rearrange("p (h a b) -> p h a b", h=8, a=16)
            cmp_ = M[:, 7168:9216].rearrange("p (h k r) -> p h k r", h=8, k=16)
            W2 = M[:, 9216:9344].rearrange("p (h k) -> p h k", h=8)
            P2 = M[:, 9344:9472].rearrange("p (h k) -> p h k", h=8)
            P2u = P2.bitcast(u32)
            pij = [M[:, 9472 + 128 * i:9600 + 128 * i] for i in range(2)]
            idg = [M[:, 9728 + 128 * i:9856 + 128 * i] for i in range(3)]
            IDT = M[:, 10240:11008].rearrange("p (a t) -> p a t", a=3)
            OA = BH[:, 0:4, :].rearrange("p (s x) (y n) -> p s (x y) n", s=2, y=2)
            OBh = BH[:, 4:8, :].rearrange("p (s x) (y n) -> p s (x y) n", s=2, y=2)
            OBl = BH[:, 8:12, :].rearrange("p (s x) (y n) -> p s (x y) n", s=2, y=2)
            gh, gl_ = BH[:, 12, :], M[:, 11008:11264]
            stg = [Yf[:, 0:4096].rearrange("p (i t) -> p i t", t=32),
                   M[:, 4096:8192].rearrange("p (i t) -> p i t", t=32)]
            s_g = [sem(f"s_gw{i}") for i in range(2)]
            g_written = []

            def top8(vals, outv, outi, toks):
                t1 = V.do(P(nc.vector.max, outv[:, 0:8], vals), toks)
                V.do(P(nc.vector.max_index, outi[:, 0:8], outv[:, 0:8], vals), t1)
                t2 = V.do(P(nc.vector.match_replace, vals, outv[:, 0:8], vals, -3.0e38), V.now())
                t3 = V.do(P(nc.vector.max, outv[:, 8:16], vals), t2)
                return V.do(P(nc.vector.max_index, outi[:, 8:16], outv[:, 8:16], vals), t3)

            def routing():
                t_id = []
                for t in range(2):
                    for hp in range(16):
                        last = top8(SC[:, t, hp, :], V16[:, t, hp, :], I16u[:, t, hp, :], [t_sc, everything])
                        yield
                last = V.do(P(nc.vector.tensor_copy, I16, I16u), last)
                for t in range(2):
                    v4 = V16[:, t].rearrange("p (h q) k -> p h q k", q=2)
                    for h in range(8):
                        if h == 4:
                            yield
                        last = V.do(P(nc.vector.tensor_tensor, cand[:, h],
                                      v4[:, h, 0, :].unsqueeze(2).to_broadcast([128, 16, 16]),
                                      v4[:, h, 1, :].unsqueeze(1).to_broadcast([128, 16, 16]), ALU.add), last)
                    yield
                    for h in range(8):
                        last = top8(cand[:, h].rearrange("p a b -> p (a b)"), W2[:, h, :], P2u[:, h, :], last)
                        yield
                    w3 = idg[2].rearrange("p (h k) -> p h k", h=8)
                    sm, ri = stat(8), stat(8)
                    a = V.do(P(nc.vector.tensor_tensor, w3, W2, W2[:, :, 0:1].to_broadcast([128, 8, 16]), ALU.subtract),
                             last, t_id)
                    a = A.do(P(nc.scalar.activation, idg[2], idg[2], ACT.Exp), a)
                    a = V.do(P(nc.vector.tensor_reduce, sm, w3, AX.X, ALU.add), a)
                    a = V.do(P(nc.vector.reciprocal, ri, sm), a)
                    tg = V.do(P(nc.vector.tensor_tensor, w3, w3, ri.unsqueeze(2).to_broadcast([128, 8, 16]), ALU.mult), a)
                    yield
                    pu = [x.bitcast(u32) for x in pij]
                    flatp = P2u.rearrange("p h k -> p (h k)")
                    a1 = V.do(P(nc.vector.tensor_single_scalar, pu[0], flatp, 4, ALU.logical_shift_right), last)
                    a2 = V.do(P(nc.vector.tensor_single_scalar, pu[1], flatp, 15, ALU.bitwise_and), last)
                    a1 = V.do(P(nc.vector.tensor_copy, pij[0], pu[0]), a1)
                    a2 = V.do(P(nc.vector.tensor_copy, pij[1], pu[1]), a2)
                    i4 = I16[:, t].rearrange("p (h q) k -> p h q k", q=2)
                    for q in range(2):
                        parts = []
                        for h in (0, 4):
                            hs = slice(h, h + 4)
                            p_ = pij[q].rearrange("p (h k) -> p h k", h=8)[:, hs].unsqueeze(3).to_broadcast([128, 4, 16, 16])
                            io = iota16.unsqueeze(1).unsqueeze(1).to_broadcast([128, 4, 16, 16])
                            a = V.do(P(nc.vector.tensor_tensor, cmp_[:, hs], p_, io, ALU.is_equal), a2, V.now())
                            yield
                            a = V.do(P(nc.vector.tensor_tensor, cmp_[:, hs], cmp_[:, hs],
                                       i4[:, hs, q, :].unsqueeze(2).to_broadcast([128, 4, 16, 16]), ALU.mult), a)
                            yield
                            last = V.do(P(nc.vector.tensor_reduce, idg[q].rearrange("p (h k) -> p h k", h=8)[:, hs],
                                          cmp_[:, hs], AX.X, ALU.add), a, t_id)
                            yield
                    bank, bfree = yield from wait_for(misc)
                    tk = transposed(idg, bank, last, tg, bfree)
                    t_id = [tk]
                    tc = A.do(P(nc.scalar.activation, IDT[:, :, 128 * t:128 * t + 128],
                                banks[bank][:, 0:384].rearrange("p (a t) -> p a t", a=3), ACT.Copy), tk, everything)
                    misc.give(bank, tc)
                    yield
                th = A.do(P(nc.scalar.activation, gh, IDT[:, 2, :], ACT.Copy), tc, q_read)
                ready = V.do(P(nc.vector.tensor_tensor, gl_, IDT[:, 2, :], bf(gh), ALU.subtract), th)
                ready = [ready, T.now()]
                ofree, sfree, tb = {}, {}, {}

                def build(g, k):
                    i = g % 2
                    for k in (k, k + 1):
                        tt = 4 * g + k
                        w = [ready, ofree.get(g - 2), q_read]
                        V.do(P(nc.vector.tensor_scalar, OA[:, i, k, :], iota, IDT[:, 0, tt:tt + 1], None, ALU.is_equal), w)
                        for ob, gg in ((OBh, bf(gh)), (OBl, gl_)):
                            tb[g] = V.do(P(nc.vector.tensor_scalar, ob[:, i, k, :], iota, IDT[:, 1, tt:tt + 1],
                                           gg[:, tt:tt + 1], ALU.is_equal, ALU.mult), w)

                held = {}

                def multiply(g):
                    i = g % 2
                    bank, bfree = yield from wait_for(misc)
                    T.wait([tb[g], bfree])
                    for k in range(4):
                        o = banks[bank][:, 128 * k:128 * k + 128]
                        T.quiet(mm(o, OBh[:, i, k, :], OA[:, i, k, :], True, False))
                        tk = T.do(mm(o, OBl[:, i, k, :], OA[:, i, k, :], False, True))
                    ofree[g] = tk
                    held[g] = bank

                def keep(g):
                    s, bank, tk = (g // 8) % 2, held[g], ofree[g]
                    tev = A.do(P(nc.scalar.activation, stg[s][:, :, 4 * (g % 8):4 * (g % 8) + 4],
                                 banks[bank][:, :].rearrange("p (t i) -> p i t", t=4), ACT.Copy), tk,
                               sfree.get(g // 8 - 2), ready)
                    misc.give(bank, tev)
                    if g % 8 == 7:
                        c = g // 8
                        w = G.dma(P(nc.gpsimd.dma_start, D["scr_g"][c, :, :],
                                    stg[s].rearrange("p i t -> p (i t)")), s_g[s], 16 * (c // 2 + 1), tev)
                        sfree[c] = w
                        g_written.append(w)

                for g in range(65):
                    if g < 64:
                        build(g, 0)
                    if g > 0:
                        yield from multiply(g - 1)
                    yield
                    if g < 64:
                        build(g, 2)
                    if g > 0:
                        keep(g - 1)
                    yield
                bar.append(everyone())
                fetch(0)
                fetch(1)
                for _ in range(4):
                    yield
                yield from prepare(0)

            gls = Slots([(i, M[:, 2048 + 1024 * i:3072 + 1024 * i].rearrange("p (k n) -> p k n", k=4)) for i in range(2)],
                        everything)
            s_a = [sem(f"s_aw{i}") for i in range(2)]
            na = [0, 0]
            a_written = {}

            def u_post(pair, b, last, j):
                ts, free = take(toks_)
                te = evac2(pair, b, last, lambda t: ts[:, t, :], free)

                def later():
                    (gi, gl), gfree = yield from wait_for(gls)
                    for k0 in (0, 2):
                        yield
                        bank, bfree = yield from wait_for(misc)
                        tk = transposed([ts[:, t, 128 * (k0 + i):128 * (k0 + i) + 128] for i in range(2) for t in range(2)],
                                        bank, te, bfree)
                        yield
                        tg = A.do(P(nc.scalar.activation, gl[:, k0:k0 + 2, :],
                                    banks[bank][:, :].rearrange("p (k n) -> p k n", k=2), ACT.Gelu_apprx_tanh), tk, gfree)
                        misc.give(bank, tg)
                    toks_.give(ts, tk)
                    na[gi] += 16
                    h = j % 2
                    w = G.dma(P(nc.gpsimd.dma_start, D["scr_a"][j // 2, :, 1024 * h:1024 * h + 1024],
                                gl.rearrange("p k n -> p (k n)")), s_a[gi], na[gi], tg)
                    a_written[j] = w
                    gls.give((gi, gl), w)
                tasks.append(later())

            s_la = [sem(f"s_la{i}") for i in range(2)]
            s_lg = [sem(f"s_lg{i}") for i in range(2)]
            glt = [M[:, 4096 * (1 + i):4096 * (1 + i) + 2048] for i in range(2)]
            gtt = [M[:, 4096 * (1 + i) + 2048:4096 * (1 + i) + 4096] for i in range(2)]
            bar = []
            lt = {}
            wB = {}
            vdone = {}
            tw_free = {}

            def fetch(sc):
                i = sc % 2
                w = bar if sc < 2 else tw_free[sc - 2]
                l1 = G.dma(P(nc.gpsimd.dma_start, glt[i], D["scr_a"][sc, :, :]), s_la[i], 16 * (sc // 2 + 1),
                           w, a_written[2 * sc], a_written[2 * sc + 1])
                l2 = G.dma(P(nc.gpsimd.dma_start, gtt[i].rearrange("p (c n) -> p c n", c=8),
                             D["scr_g"][:, :, 256 * sc:256 * sc + 256].rearrange("c p n -> p c n")),
                           s_lg[i], 16 * (sc // 2 + 1), w, g_written)
                lt[sc] = [l1, l2]

            def prepare(sc):
                i = sc % 2
                a = glt[i].rearrange("p (k c t) -> p k c t", k=8, c=8)
                g = gtt[i].rearrange("p (c k t) -> p k c t", k=8, c=8)
                free = vdone.get(sc - 2)
                done = wB[sc] = []
                for k0 in range(0, 8, 2):
                    t1 = None
                    for k in (k0, k0 + 1):
                        t1 = V.do(P(nc.vector.tensor_tensor, a[:, k], a[:, k], g[:, k], ALU.mult), lt[sc])
                    src = glt[i][:, 256 * k0:256 * k0 + 512].rearrange("p (k n) -> p k n", k=2)
                    o = 8 * i + k0
                    h = A.do(P(nc.scalar.activation, BH[:, o:o + 2, :], src, ACT.Copy), t1, free, bar)
                    done.append(V.do(P(nc.vector.tensor_tensor, BL[:, o:o + 2, :], src, bf(BH[:, o:o + 2, :]), ALU.subtract), h))
                    yield
                tw_free[sc] = [done[-1]]
                if sc + 2 < 16:
                    fetch(sc + 2)

            for j in range(32):
                pair, b, last = gemm("peer_u", 8 * j, 16, AH, AL, nA)
                u_post(pair, b, last, j)
                if j == 0:
                    finish_tasks()
                    sub_scores()
                    q_read = T.now()
                    idle.append(routing())
            while len(wB.get(0, ())) < 4:
                step()
            lastR = t_R
            for sc in range(16):
                if sc + 1 < 16:
                    tasks.append(prepare(sc + 1))
                o = 8 * (sc % 2)
                for j in range(4):
                    pair, b, last = gemm("peer_v", 16 * sc + 4 * j, 8, BH[:, o:o + 8, :], BL[:, o:o + 8, :], wB[sc])
                    out_r = add_residual(b, last, j, lastR, sc == 15)
                    accs.give(pair, out_r)
                    if sc == 15:
                        t_R = t_R + out_r
                lastR = [V.now()]
                vdone[sc] = [last]
                finish_tasks()

        if stage >= 3:
            everything = everyone()
            nA = norm_T(lambda t: R[:, t, :], 2048, 54, hl(AH), hl(AL), lambda t: Y[:, t, :], everything,
                        everything, ssp=ssr)
            QA = M[:, 0:2048].rearrange("p (k n) -> p k n", k=8)
            KA = M[:, 2048:4096].rearrange("p (k n) -> p k n", k=8)
            VA = M[:, 4096:6144].rearrange("p (t n) -> p t n", t=2)
            VN = M[:, 6144:8192].rearrange("p (t n) -> p t n", t=2)
            QN = Yf[:, 0:2048].rearrange("p (k n) -> p k n", k=8)
            KN = Yf[:, 2048:4096].rearrange("p (k n) -> p k n", k=8)
            toks_ = Slots([M[:, 8192 + 1024 * i:9216 + 1024 * i].rearrange("p (t n) -> p t n", t=2) for i in range(2)],
                          everything)
            pslots = Slots([M[:, 10240 + 512 * i:10752 + 512 * i] for i in range(2)], everything)
            nbs = [M[:, 11264 + 512 * i:11776 + 512 * i] for i in range(2)]

            lamb = TMP[:, 0:512]
            t_l = load(lamb, D["lam"], everything)
            ls, le, lam = stat(2), stat(2), stat(1)
            for i in range(2):
                t1 = V.do(P(nc.vector.tensor_tensor_reduce, out=TMP[:, 512 + 128 * i:640 + 128 * i],
                            in0=TMP[:, 256 * i:256 * i + 128], in1=TMP[:, 256 * i + 128:256 * i + 256], scale=1.0,
                            scalar=0.0, op0=ALU.mult, op1=ALU.add, accum_out=ls[:, i:i + 1]), t_l, everything)
            t2 = A.do(P(nc.scalar.activation, le, ls, ACT.Exp), t1)
            t3 = V.do(P(nc.vector.tensor_tensor, lam, le[:, 0:1], le[:, 1:2], ALU.subtract), t2)
            t_lam = V.do(P(nc.vector.tensor_scalar, lam, lam, 0.8 - 0.6 * float(np.exp(-0.0)), None, ALU.add), t3)

            tdone = {"QA": [], "KA": [], "QN": [], "KN": [], "VA": [], "VN": []}

            def qk_post(pair, b, last, name, dst, j, do_rope, mul):
                ts, free = take(toks_)
                if mul == 1.0:
                    te = evac2(pair, b, last, lambda t: ts[:, t, :], free)
                else:
                    t0 = A.do(P(nc.scalar.activation, ts[:, 0, :], b[0][:, :], ACT.Copy, scale=mul), last, free)
                    t1 = V.do(P(nc.vector.tensor_scalar, ts[:, 1, :], b[1][:, :], mul, None, ALU.mult), last, free)
                    accs.give(pair, t0, t1)
                    te = [t0, t1]

                def later():
                    tt = te
                    yield
                    if do_rope:
                        tt = []
                        for t in range(2):
                            tt.append(rope(ts[:, t, :].rearrange("p (u c h) -> p u c h", u=4, c=2), 4, 64,
                                           cos2[:, t], sin2[:, t], [te, t_lam]))
                            yield
                    for k0 in (0, 2):
                        bank, bfree = yield from wait_for(misc)
                        tk = transposed([ts[:, t, 128 * (k0 + i):128 * (k0 + i) + 128] for i in range(2) for t in range(2)],
                                        bank, tt, bfree)
                        yield
                        tc = A.do(P(nc.scalar.activation, dst[:, 4 * j + k0:4 * j + k0 + 2, :],
                                    banks[bank][:, :].rearrange("p (k n) -> p k n", k=2), ACT.Copy), tk, everything, y_free)
                        misc.give(bank, tc)
                        tdone[name].append(tc)
                    toks_.give(ts, tk)
                tasks.append(later())

            def da_unit(h, t):
                def scores(bank, bfree):
                    T.wait([tdone["QA"], tdone["KA"], bfree])
                    for c in range(2):
                        tk = T.do(mm(banks[bank][:, 256 * c:256 * c + 256], QA[:, 2 * h + c, 128 * t:128 * t + 128],
                                     KA[:, 2 * h + c, :], True, True))
                    return tk

                def combine(ps, ri, toks):
                    rl = stat(1)
                    a = V.do(P(nc.vector.tensor_tensor, rl, ri[:, 1:2], lam, ALU.mult), toks, t_lam)
                    a = V.do(P(nc.vector.tensor_scalar, ps[:, 256:512], ps[:, 256:512], rl, None, ALU.mult), a)
                    return V.do(P(nc.vector.scalar_tensor_tensor, out=ps[:, 0:256], in0=ps[:, 0:256],
                                  scalar=ri[:, 0:1], in1=ps[:, 256:512], op0=ALU.mult, op1=ALU.subtract), a)

                def pv(bank, pt, toks):
                    T.wait([toks, tdone["VA"]])
                    for kb in range(2):
                        tk = T.do(mm(banks[bank][:, 0:256], pt[:, 128 * kb:128 * kb + 128],
                                     VA[:, kb, 256 * h:256 * h + 256], kb == 0, kb == 1))
                    return tk

                def finish(o, ri, toks):
                    tf = A.do(P(nc.scalar.activation, QA[:, 2 * h:2 * h + 2, 128 * t:128 * t + 128],
                                o.rearrange("p (c n) -> p c n", c=2), ACT.Copy), toks)
                    oa_done.append(tf)
                    return tf

                return attend(scores, 2, 256, 128 ** -0.5, None, pslots, 2, pv, 256, finish, combine)

            s_nb = [sem(f"s_nb{i}") for i in range(2)]
            nb_t, nb_free = {}, {}

            def nb_fetch(h):
                i = h % 2
                nb_t[h] = G.dma(P(nc.gpsimd.dma_start, nbs[i], D["na_bias"][h, :, :]), s_nb[i], 16 * (h // 2 + 1),
                                nb_free.get(h - 2, everything))

            def na_unit(h):
                i = h % 2

                def scores(bank, bfree):
                    v = nbs[i].rearrange("p (r c) -> p r c", c=64)
                    tb = V.do(P(nc.vector.tensor_tensor, v, v, namask.unsqueeze(1).to_broadcast([128, 8, 64]), ALU.add),
                              nb_t[h])
                    T.wait([tdone["QN"], tdone["KN"], bfree, tb])
                    for t in range(2):
                        o = banks[bank][:, 256 * t:256 * t + 256]
                        T.quiet(mm(o, QN[:, h, 128 * t:128 * t + 128], KN[:, h, :], True, False))
                        tk = T.do(mm(o, ident, nbs[i][:, 256 * t:256 * t + 256], False, True))
                    nb_free[h] = [tk]
                    if h + 2 < 8:
                        nb_fetch(h + 2)
                    return tk

                def pv(bank, pt, toks):
                    T.wait([toks, tdone["VN"]])
                    for t in range(2):
                        for kb in range(2):
                            tk = T.do(mm(banks[bank][:, 128 * t:128 * t + 128],
                                         pt[:, 256 * t + 128 * kb:256 * t + 128 * kb + 128],
                                         VN[:, kb, 128 * h:128 * h + 128], kb == 0, kb == 1))
                    return tk

                def finish(o, ri, toks):
                    tf = V.do(P(nc.vector.tensor_tensor, QN[:, h, :].rearrange("p (t n) -> p t n", t=2),
                                o.rearrange("p (t n) -> p t n", t=2), ri.unsqueeze(2).to_broadcast([128, 2, 128]),
                                ALU.mult), toks)
                    on_done.append(tf)
                    return tf

                return attend(scores, 2, 256, 1.0, None, pslots, 4, pv, 256, finish)

            oa_done, on_done, nBa, nBb = [], [], [], []

            def branch_a():
                yield from pipelined([da_unit(h, t) for h in range(4) for t in range(2)], 2)
                tt = []
                for t in range(2):
                    v = QA[:, :, 128 * t:128 * t + 128]
                    t8 = TMP[:, 0:1024].rearrange("p (k n) -> p k n", k=8)
                    a = V.do(P(nc.vector.tensor_tensor, t8, v, v, ALU.mult), oa_done, V.now())
                    yield
                    s8, s4 = stat(8), stat(4)
                    a = V.do(P(nc.vector.tensor_reduce, s8, t8, AX.X, ALU.add), a)
                    s82 = s8.rearrange("p (h c) -> p h c", c=2)
                    a = V.do(P(nc.vector.tensor_tensor, s4.unsqueeze(2), s82[:, :, 0:1], s82[:, :, 1:2], ALU.add), a)
                    r, a = rstd(s4, 4, 256, a, 1.0 - (0.8 - 0.6 * float(np.exp(-0.0))))
                    v4 = v.rearrange("p (h c) n -> p h c n", c=2)
                    for c in range(2):
                        tt.append(V.do(P(nc.vector.tensor_tensor, v4[:, :, c, :], v4[:, :, c, :],
                                         r.unsqueeze(2).to_broadcast([128, 4, 128]), ALU.mult), a))
                    yield
                yield from trans_split(lambda kt, t: QA[:, kt, 128 * t:128 * t + 128], 8, hl(BH, 0), hl(BL, 0),
                                       lambda kt: GC[:, 86 + kt % 2:87 + kt % 2], tt, everything, nBa)

            def branch_b():
                yield from pipelined([na_unit(h) for h in range(8)], 2)
                yield from trans_split(lambda kt, t: QN[:, kt, 128 * t:128 * t + 128], 8, hl(BH, 8), hl(BL, 8),
                                       None, on_done, everything, nBb)

            nb_fetch(0)
            nb_fetch(1)
            for n, (name, dst, rp_, mul) in enumerate((("QA", QA, True, 1.0), ("KA", KA, True, 1.0), ("VA", VA, None, 1.0),
                                                       ("QN", QN, False, 128 ** -0.5), ("KN", KN, False, 1.0), ("VN", VN, None, 1.0))):
                for j in range(2):
                    pair, b, last = gemm("w_in_2", 16 * n + 8 * j, 16, AH, AL, nA)
                    if n == 0 and j == 0:
                        finish_tasks()
                        y_free = everyone()
                    if rp_ is None:
                        tdone[name] += evac2(pair, b, last, lambda t: dst[:, t, 512 * j:512 * j + 512], everything)
                    else:
                        qk_post(pair, b, last, name, dst, j, rp_, mul)
                if name == "VA":
                    finish_tasks()
                    idle.append(branch_a())
            finish_idle()
            a_over = everyone()
            idle.append(branch_b())
            gate = [M[:, 2048 + 1024 * j:3072 + 1024 * j] for j in range(4)] + \
                   [Yf[:, 2048:3072], Yf[:, 3072:4096], M[:, 0:1024], M[:, 1024:2048]]
            gate = [g.rearrange("p (t n) -> p t n", t=2) for g in gate]
            t_gate = {}
            for j in range(8):
                pair, b, last = gemm("w_in_2", 96 + 8 * j, 16, AH, AL, nA)
                if j == 4:
                    finish_idle()
                    b_over = everyone()
                w = a_over if j < 4 else b_over
                for t in range(2):
                    t_gate[j, t] = A.do(P(nc.scalar.activation, gate[j][:, t, :], b[t][:, :], ACT.Sigmoid), last, w)
                accs.give(pair, t_gate[j, 1])
            tm = []
            for j in range(4):
                pair, b, last = gemm("w_branch_a", 4 * j, 8, BH[:, 0:8, :], BL[:, 0:8, :], nBa)
                for t in range(2):
                    ta = V.do(P(nc.vector.tensor_tensor, gate[j][:, t, :], gate[j][:, t, :], b[t][:, :], ALU.mult),
                              last, t_gate[j, t])
                accs.give(pair, ta)
                pair, b, last = gemm("w_branch_b", 4 * j, 8, BH[:, 8:16, :], BL[:, 8:16, :], nBb)
                for t in range(2):
                    tb = V.do(P(nc.vector.tensor_tensor, gate[4 + j][:, t, :], gate[4 + j][:, t, :], b[t][:, :],
                                ALU.mult), last, t_gate[4 + j, t])
                    tm.append(V.do(P(nc.vector.tensor_tensor, gate[j][:, t, :], gate[j][:, t, :], gate[4 + j][:, t, :],
                                     ALU.add), tb, ta))
                accs.give(pair, tb)
                nC = [] if j == 0 else nC
                tasks.append(trans_split(lambda kt, t, j=j: gate[j][:, t, 128 * kt:128 * kt + 128], 4, hl(AH, 4 * j),
                                         hl(AL, 4 * j), None, [tm[-1], tm[-2]], [t_gate[7, 1]], nC))
                if j < 3:
                    finish_tasks()
            finish_tasks()
            everything = everyone()
            grow = M[:, 8192:10240]
            t_gw = load(grow, D["post_mix"].partition_broadcast(128), everything)
            junks = [M[:, 10240 + 512 * i:10752 + 512 * i] for i in range(4)]
            squared = [None] * 4

            def square(x, acc, toks):
                squared.append(A.do(P(nc.scalar.activation, junks[len(squared) % 4], x, ACT.Square, accum_out=acc),
                                    toks, squared[-4]))
                return squared[-1]

            def weigh(j, ty, t_gw, ssy):
                c = slice(512 * j, 512 * j + 512)
                for t in range(2):
                    a = square(Y[:, t, c], ssy[:, t, j:j + 1], [ty, everything])
                    a = V.do(P(nc.vector.tensor_tensor, Y[:, t, c], Y[:, t, c], grow[:, c], ALU.mult), a, t_gw)
                return a

            def residual(ssy, toks, lastR, store):
                ss = stat(2)
                a = V.do(P(nc.vector.tensor_reduce, ss, ssy, AX.X, ALU.add), toks, A.now())
                r, tr = rstd(ss, 2, 2048, a)
                ends = []
                for j in range(4):
                    c = slice(512 * j, 512 * j + 512)
                    for t in range(2):
                        a = V.do(P(nc.vector.scalar_tensor_tensor, out=R[:, t, c], in0=Y[:, t, c], scalar=r[:, t:t + 1],
                                   in1=R[:, t, c], op0=ALU.mult, op1=ALU.add), tr, toks, lastR)
                        if store is None:
                            a = square(R[:, t, c], ssr[:, t, j:j + 1], a)
                        else:
                            a = store(j, t, a)
                        ends.append(a)
                return ends

            ssy = stat(8).rearrange("p (t c) -> p t c", t=2)
            for j in range(4):
                pair, b, last = gemm("w_out_2", 8 * j, 16, AH, AL, nC)
                ty = evac2(pair, b, last, lambda t: Y[:, t, 512 * j:512 * j + 512], everything)
                ty = weigh(j, ty, t_gw, ssy)
            t_R = residual(ssy, ty, t_R, None)
            everything = everyone()
            t_gw = load(grow, D["post_mlp"].partition_broadcast(128), everything)
            nA = norm_T(lambda t: R[:, t, :], 2048, 70, hl(AH), hl(AL), lambda t: Y[:, t, :], [t_R, everything],
                        everything, ssp=ssr)
            y_free = None
            toks_ = Slots([M[:, 4096 + 1024 * i:5120 + 1024 * i].rearrange("p (t n) -> p t n", t=2) for i in range(2)],
                          everything)
            wB, vdone = {s: [] for s in range(8)}, {}

            def up(s):
                for j in range(2):
                    pair, b, last = gemm("w_up", 16 * s + 8 * j, 16, AH, AL, nA)
                    ts, free = take(toks_)
                    te = []
                    for t in range(2):
                        a = A.do(P(nc.scalar.activation, ts[:, t, :], b[t][:, :], ACT.Relu), last, free)
                        te.append(V.do(P(nc.vector.tensor_tensor, ts[:, t, :], ts[:, t, :], ts[:, t, :], ALU.mult), a))
                    accs.give(pair, a)

                    def later(ts=ts, te=te, j=j):
                        o = 8 * (s % 2) + 4 * j
                        yield from trans_split(lambda kt, t: ts[:, t, 128 * kt:128 * kt + 128], 4, hl(BH, o), hl(BL, o),
                                               None, te, [everything, vdone.get(s - 2)], wB[s])
                        toks_.give(ts, T.now())
                    tasks.append(later())

            ty = {}
            for s in range(9):
                if s < 8:
                    up(s)
                if s == 0:
                    continue
                d = s - 1
                o = 8 * (d % 2)
                if d == 0:
                    finish_tasks()
                    y_free = everyone()
                for j in range(4):
                    pair, b, last = gemm("w_down", 16 * d + 4 * j, 8, BH[:, o:o + 8, :], BL[:, o:o + 8, :], wB[d])
                    c = slice(512 * j, 512 * j + 512)
                    if d == 0:
                        ty[j] = evac2(pair, b, last, lambda t: Y[:, t, c], y_free)
                    else:
                        for t in range(2):
                            a = V.do(P(nc.vector.tensor_tensor, Y[:, t, c], Y[:, t, c], b[t][:, :], ALU.add), last, ty[j])
                        ty[j] = [a]
                        accs.give(pair, a)
                    if d == 7:
                        ty[j] = weigh(j, ty[j], t_gw, ssy)
                vdone[d] = [last]
            s_out = [sem(f"s_out{i}") for i in range(8)]
            out_v = out.rearrange("(t p) n -> p t n", p=128)

            def store(j, t, a):
                c = slice(512 * j, 512 * j + 512)
                return S.dma(P(nc.sync.dma_start, out_v[:, t, c], R[:, t, c]), s_out[2 * j + t], 16, a)

            stored = residual(ssy, list(ty.values()), t_R, store)

        finish_idle()
        assert at[0] == len(order)
        if stage < 3:
            stored = [load(out.rearrange("(t p) n -> p t n", p=128), R[:, :, :], t_R, q=S)]
        S.wait(stored)
        if stage >= 2:
            S.wait([g_written, list(a_written.values())])

        block = ctx.enter_context(nc.Block())

        @block.sync
        def _(e):
            for f in S.q:
                f()

        @block.gpsimd
        def _(e):
            for f in G.q:
                f()

        @block.scalar
        def _(e):
            for f in A.q:
                f()

        @block.vector
        def _(e):
            for f in V.q:
                f()

        @block.tensor
        def _(e):
            for f in T.q:
                f()


def cut(w):
    K, N = w.shape
    v = w.reshape(K // 256, 2, 128, N // 512, 512).transpose(3, 0, 2, 1, 4)
    return np.ascontiguousarray(v).reshape(-1, 128, NPIECE)


def cut_down(w):
    return np.concatenate([cut(w[k:k + 1024]) for k in range(0, w.shape[0], 1024)])


def columns(g):
    return g.reshape(-1, 128).T


def spread(g):
    return np.broadcast_to(g.reshape(1, -1), (128, g.size))


def kernel(STAGE=9, **inputs):
    import numpy as np
    import concourse.bacc as bacc
    from concourse import mybir
    from concourse.bass_utils import run_bass_kernel_spmd as run

    I = {k: np.asarray(v) for k, v in inputs.items()}
    w_in = I["w_in"][0]
    lat, kvl, pe, qs, ks, vs = np.split(w_in, [512, 768, 832, 1856, 1984], axis=1)
    A = {}
    A["x"] = I["x"][0]
    A["consts"] = constants()
    A["gain_cols"] = np.concatenate(
        [columns(I[n][0]) for n in ("norm1_gain", "q_a_gain", "kv_a_gain", "group_out_gain", "norm2_gain",
                                    "norm_mix_pre_2", "norm_mlp_pre_2", "subln_w_2")] +
        [columns(I[n][0, :128]) for n in ("mla_q_gain", "mla_k_gain")], axis=1)
    A["gain_rows"] = np.concatenate(
        [spread(I[n][0]) for n in ("mla_q_gain", "mla_k_gain", "swa_q_gain", "swa_k_gain", "swa_sinks")], axis=1)
    pos = I["positions"][0]
    p = np.arange(128)
    kidx = 128 * np.arange(2)[None, :, None] + 32 * (p // 32)[:, None, None] + np.arange(32)[None, None, :]
    A["pos"] = np.concatenate([spread(pos), pos[kidx].reshape(128, 64), pos.reshape(2, 128).T], axis=1)
    table = np.zeros((4, 32, 4, 16), np.float32)
    for g in range(4):
        table[g, :, g, :] = I["rel_bias_table"]
    A["table"] = table.reshape(128, 64)
    A["w_in_a"] = cut(np.concatenate([lat, kvl, ks, vs, qs], axis=1))
    A["w_in_b"] = pe.reshape(16, 128, 64).transpose(1, 0, 2).reshape(1, 128, NPIECE)
    for n, per in (("w_q_b", 192), ("w_kv_b", 256)):
        w = I[n][0].reshape(-1, 8, per)
        A[n] = cut(np.concatenate([w[:, :, :128].reshape(-1, 1024), w[:, :, 128:].reshape(w.shape[0], -1)], axis=1))
    for n in ("w_out", "peer_w_q"):
        A[n] = cut(I[n][0])
    A["sub_keys"] = I["peer_sub_keys"][0].reshape(2, 8, 128, 128).transpose(0, 3, 1, 2).reshape(2, 128, NPIECE)
    A["peer_u"] = cut(I["peer_u"][0].T)
    A["peer_v"] = cut_down(I["peer_v"][0])
    A["w_in_2"] = cut(I["w_in_2"][0])
    A["w_branch_a"] = cut(I["w_branch_a_2"][0])
    A["w_branch_b"] = cut(I["w_branch_b_2"][0])
    A["w_out_2"] = cut(I["w_out_2"][0])
    A["w_up"] = cut(I["w_up_2"][0])
    A["w_down"] = cut_down(I["w_down_2"][0])
    A["lam"] = np.concatenate([spread(I[n][0]) for n in ("lam_q1_2", "lam_k1_2", "lam_q2_2", "lam_k2_2")], axis=1)
    A["post_mix"] = I["norm_mix_post_2"][0]
    A["post_mlp"] = I["norm_mlp_post_2"][0]
    q = np.arange(256)
    dr = q[None, :] // 64 - q[:, None] // 64 + 7
    dc = np.clip(q[None, :] % 64 - q[:, None] % 64 + 15, 0, 30)
    nb = I["na_rpb_2"][0][:, dr, dc]
    A["na_bias"] = nb.reshape(8, 2, 128, 256).transpose(0, 2, 1, 3).reshape(8, 128, 512)

    nc = bacc.Bacc("TRN2", target_bir_lowering=False, num_devices=1)
    arrays, D = {}, {}
    for n, a in A.items():
        a = np.ascontiguousarray(a)
        arrays["in_" + n] = a
        D[n] = nc.dram_tensor("in_" + n, a.shape, mybir.dt.from_np(a.dtype), kind="ExternalInput").ap()
    D["scr_g"] = nc.dram_tensor("scr_g", (8, 128, 4096), mybir.dt.float32, kind="Internal").ap()
    D["scr_a"] = nc.dram_tensor("scr_a", (16, 128, 2048), mybir.dt.float32, kind="Internal").ap()
    o = nc.dram_tensor("out_0", (256, 2048), mybir.dt.float32, kind="ExternalOutput").ap()
    build(nc, D, o, STAGE)
    r = run(nc, [arrays], core_ids=[0])
    return r.results[0]["out_0"].reshape(1, 256, 2048)
```

```python
import numpy as np

NPIECE = 1024


def threshold_rows():
    import math
    thr = [float(b) for b in range(17)]
    for j in range(1, 16):
        thr.append(float(math.ceil(16.0 * 8.0 ** (j / 16.0) - 1e-9)))
    thr[0] = -3.0e38
    return np.array(thr + [3.0e38], np.float32)


def constants():
    p = np.arange(128)
    c = np.zeros((128, 882), np.float32)
    c[:, 0:128] = np.eye(128)
    c[:, 128:256] = np.where(p[None, :] <= p[:, None], 0.0, -1e30)
    c[:, 256:384] = np.where(p[None, :] > p[:, None], 0.0, -1e30)
    c[:, 384:512] = p[None, :]
    thr = threshold_rows()
    c[:, 512] = thr[p % 32]
    c[:, 513] = thr[p % 32 + 1]
    qc = p % 64
    start = np.clip(qc - 8, 0, 48)
    kc = np.arange(64)
    c[:, 514:578] = np.where((kc[None] >= start[:, None]) & (kc[None] < start[:, None] + 16), 0.0, -1e30)
    inv = (1.0 / (np.float32(10000.0) ** (np.arange(0, 128, 2, dtype=np.float32) / np.float32(128)))).astype(np.float32)
    ang = np.arange(256, dtype=np.float32)[:, None] * inv[None]
    c[:, 578:706] = np.cos(ang).astype(np.float32).reshape(2, 128, 64).transpose(1, 0, 2).reshape(128, 128)
    c[:, 706:834] = np.sin(ang).astype(np.float32).reshape(2, 128, 64).transpose(1, 0, 2).reshape(128, 128)
    c[:, 834:866] = (np.float32(10000.0) ** (-np.arange(32, dtype=np.float32) / np.float32(32)))[None]
    c[:, 866:882] = np.arange(16)[None]
    return c


def build(nc, D, out):
    import math
    import concourse.bass as bass
    from concourse import mybir
    from contextlib import ExitStack
    from functools import partial as P

    f32, f32r = mybir.dt.float32, mybir.dt.float32r
    i32, u32 = mybir.dt.int32, mybir.dt.uint32
    ALU, ACT, AX = mybir.AluOpType, mybir.ActivationFunctionType, mybir.AxisListType
    LEAD, LEADT = 3, 4
    NR, NH, NST = 5, 3, 1080

    with ExitStack() as ctx:
        def sb(name, shape, dt=f32):
            return ctx.enter_context(nc.sbuf_tensor(name, shape, dt))

        def sem(name):
            return ctx.enter_context(nc.semaphore(name))

        raw = sb("raw", [128, NR, NPIECE])
        whi = sb("whi", [128, NH, NPIECE], f32r)
        wlo = sb("wlo", [128, NH, NPIECE], f32r)
        AH = sb("AH", [128, 16, 256], f32r)
        AL = sb("AL", [128, 16, 256], f32r)
        BH = sb("BH", [128, 16, 256], f32r)
        BL = sb("BL", [128, 16, 256], f32r)
        R = sb("R", [128, 2, 2048])
        Y = sb("Y", [128, 2, 2048])
        M = sb("M", [128, 12288])
        PTb = sb("PTb", [128, 2, 512])
        TMP = sb("TMP", [128, 1024])
        C = sb("C", [128, 882])
        GC = sb("GC", [128, 92])
        GR = sb("GR", [128, 400])
        POS = sb("POS", [128, 322], i32)
        ST = sb("ST", [128, NST])
        RT = sb("RT", [128, 2, 48])
        banks = [ctx.enter_context(nc.psum_tensor(f"bank{i}", [128, 512], f32)) for i in range(8)]

        ident, causal, upper, iota = C[:, 0:128], C[:, 128:256], C[:, 256:384], C[:, 384:512]
        namask = C[:, 514:578]
        cos2 = C[:, 578:706].rearrange("p (t j) -> p t j", t=2)
        sin2 = C[:, 706:834].rearrange("p (t j) -> p t j", t=2)
        iota16 = C[:, 866:882]
        Yf = Y[:, :, :].rearrange("p t n -> p (t n)")
        Rf = R[:, :, :].rearrange("p t n -> p (t n)")

        def bf(ap):
            return ap.bitcast(f32)

        class Queue:
            def __init__(self, wait, name):
                self.wait_ge, self.sem, self.n, self.q, self.seen = wait, sem(name), 0, [], {}

            def wait(self, toks):
                need = {}
                for tok in flat(toks):
                    s, v = tok
                    if need.get(s.name, (s, 0))[1] < v:
                        need[s.name] = (s, v)
                for name, (s, v) in need.items():
                    if self.seen.get(name, 0) < v:
                        self.seen[name] = v
                        self.q.append(P(self.wait_ge, s, v))

            def do(self, fn, *toks):
                self.wait(toks)
                self.n += 1
                self.q.append(P(signalled, fn, self.sem, 1))
                return (self.sem, self.n)

            def quiet(self, fn, *toks):
                self.wait(toks)
                self.q.append(fn)

            def dma(self, fn, s, count, *toks):
                self.wait(toks)
                self.q.append(P(signalled, fn, s, 16))
                return (s, count)

            def now(self):
                return (self.sem, self.n)

        def signalled(fn, s, n):
            fn().then_inc(s, n)

        def flat(toks):
            for t in toks:
                if t is None:
                    continue
                if isinstance(t, tuple) and len(t) == 2 and isinstance(t[1], int):
                    yield t
                else:
                    yield from flat(t)

        T = Queue(nc.tensor.wait_ge, "q_pe")
        A = Queue(nc.scalar.wait_ge, "q_act")
        V = Queue(nc.vector.wait_ge, "q_dve")
        G = Queue(nc.gpsimd.wait_ge, "q_pool")
        S = Queue(nc.sync.wait_ge, "q_sp")

        def everyone():
            return [q.now() for q in (T, A, V, G)]

        n_aux = [0]

        def load(dst, src, *toks, q=None):
            n_aux[0] += 1
            q = q or G
            e = nc.gpsimd if q is G else nc.sync
            return q.dma(P(e.dma_start, dst, src), sem(f"s_aux{n_aux[0]}"), 16, *toks)

        n_st = [0]

        def stat(n):
            a = n_st[0]
            n_st[0] += n
            assert n_st[0] <= NST, n_st
            return ST[:, a:a + n]

        class Slots:
            def __init__(self, items, toks=()):
                self.free = [(i, list(toks)) for i in items]

            def give(self, item, *toks):
                self.free.append((item, list(toks)))

        tasks, idle = [], []

        def step(n_idle=1):
            for g in list(tasks):
                if next(g, 1) == 1:
                    tasks.remove(g)
            for _ in range(n_idle):
                if idle and next(idle[0], 1) == 1:
                    idle.pop(0)

        def take(slots):
            while not slots.free:
                step()
            return slots.free.pop(0)

        def wait_for(slots):
            while not slots.free:
                yield
            return slots.free.pop(0)

        def finish_tasks():
            while tasks:
                step(0)

        def finish_idle():
            while idle:
                step()
            finish_tasks()

        def pipelined(units, depth, at_once=1):
            active = []
            units = list(units)
            while units or active:
                for _ in range(min(at_once, len(units), depth - len(active))):
                    active.append(units.pop(0))
                for g in list(active):
                    if next(g, 1) == 1:
                        active.remove(g)
                yield

        accs = Slots([0, 1])
        misc = Slots([4, 5, 6, 7])
        PT = Slots([0, 1])
        roots = Slots([0, 1])

        def lend_banks():
            for _ in range(2):
                pair, free = take(accs)
                misc.give(2 * pair, free)
                misc.give(2 * pair + 1, free)

        def return_banks():
            free = {b: f for b, f in misc.free}
            assert len(free) == 8
            misc.free[:] = [(b, f) for b, f in misc.free if b >= 4]
            for pair in range(2):
                accs.give(pair, free[2 * pair], free[2 * pair + 1])

        order = []

        def plan(name, first, n):
            order.extend((name, i) for i in range(first, first + n))

        plan("w_in_a", 0, 16)
        plan("w_in_b", 0, 1)
        plan("w_in_a", 16, 16)
        plan("w_kv_b", 0, 4)
        plan("w_q_b", 4, 2)
        plan("w_q_b", 0, 4)
        plan("w_out", 0, 32)
        plan("peer_w_q", 0, 32)
        plan("peer_u", 0, 8)
        plan("sub_keys", 0, 2)
        plan("peer_u", 8, 248)
        plan("peer_v", 0, 256)
        plan("w_in_2", 0, 160)
        for j in range(4):
            plan("w_branch_a", 4 * j, 4)
            plan("w_branch_b", 4 * j, 4)
        plan("w_out_2", 0, 32)
        for s in range(9):
            if s < 8:
                plan("w_up", 16 * s, 16)
            if s >= 1:
                plan("w_down", 16 * (s - 1), 16)

        s_raw = [sem(f"s_raw{i}") for i in range(NR)]
        loaded, split, used = [], [], []
        at = [0]

        def ensure_split(i):
            while len(split) <= min(i, len(order) - 1):
                n = len(split)
                while len(loaded) <= min(n + NR - 1, len(order) - 1):
                    m = len(loaded)
                    name, k = order[m]
                    loaded.append(S.dma(P(nc.sync.dma_start, raw[:, m % NR, :], D[name][k, :, :]),
                                        s_raw[m % NR], 16 * (m // NR + 1),
                                        split[m - NR] if m >= NR else None))
                free = used[n - NH] if n >= NH else None
                h = A.do(P(nc.scalar.activation, whi[:, n % NH, :], raw[:, n % NR, :], ACT.Copy),
                         loaded[n], free)
                split.append(V.do(P(nc.vector.tensor_tensor, wlo[:, n % NH, :], raw[:, n % NR, :],
                                    bf(whi[:, n % NH, :]), ALU.subtract), h))

        def piece(name, k):
            i = at[0]
            assert order[i] == (name, k), (order[i], name, k)
            ensure_split(i + NH - 1 if i + NH - 1 < len(used) + NH else i)
            at[0] += 1
            return i % NH, split[i]

        def used_up(tok):
            used.append(tok)
            if at[0] < len(order):
                ensure_split(at[0] + NH - 2)

        def gemm(name, first, kts, lh, ll, ltok, step_idle=1, hold=0):
            pair, free = take(accs)
            b = [banks[2 * pair], banks[2 * pair + 1]]
            n = kts // 2
            for c in range(n):
                while len(ltok) < (min(c + LEAD, n) if c >= hold else c + 1):
                    step(0)
                slot, tok = piece(name, first + c)
                T.wait([tok, ltok[c], free])
                for kk in range(2):
                    kt = 2 * c + kk
                    w = slice(512 * kk, 512 * kk + 512)
                    for t in range(2):
                        a = slice(128 * t, 128 * t + 128)
                        first_mm, last_mm = kt == 0, kt == kts - 1
                        T.quiet(P(nc.tensor.matmul, b[t][:, :], lh[:, kt, a], whi[:, slot, w], start=first_mm, stop=False))
                        T.quiet(P(nc.tensor.matmul, b[t][:, :], lh[:, kt, a], wlo[:, slot, w], start=False, stop=False))
                        f = P(nc.tensor.matmul, b[t][:, :], ll[:, kt, a], whi[:, slot, w], start=False, stop=last_mm)
                        if kk == 1 and t == 1:
                            last = T.do(f)
                        else:
                            T.quiet(f)
                used_up(last)
                if c < n - 1:
                    step(step_idle)
            return pair, b, last

        def gemm_t(name, first, kts, rh, rl, rtok, step_idle=1):
            pair, free = take(accs)
            b = [banks[2 * pair], banks[2 * pair + 1]]
            n = kts // 4
            for half in range(2):
                for c in range(n):
                    while len(rtok) < min(2 * c + LEADT, kts // 2):
                        step(0)
                    slot, tok = piece(name, first + n * half + c)
                    T.wait([tok, rtok[2 * c:2 * c + 2], free])
                    for kk in range(4):
                        kt = 4 * c + kk
                        for i in range(2):
                            o = b[i][:, 256 * half:256 * half + 256]
                            w = slice(256 * kk + 128 * i, 256 * kk + 128 * i + 128)
                            T.quiet(P(nc.tensor.matmul, o, whi[:, slot, w], rh[:, kt, :], start=kt == 0, stop=False))
                            T.quiet(P(nc.tensor.matmul, o, whi[:, slot, w], rl[:, kt, :], start=False, stop=False))
                            f = P(nc.tensor.matmul, o, wlo[:, slot, w], rh[:, kt, :], start=False, stop=kt == kts - 1)
                            if kk == 3 and i == 1:
                                last = T.do(f)
                            else:
                                T.quiet(f)
                    used_up(last)
                    if half == 0 or c < n - 1:
                        step(step_idle)
            return pair, b, last

        def transposed(srcs, bank, *toks):
            T.wait(toks)
            for n, s in enumerate(srcs):
                f = P(nc.tensor.transpose, banks[bank][:, 128 * n:128 * n + 128], s, ident)
                if n == len(srcs) - 1:
                    return T.do(f)
                T.quiet(f)

        def trans_split(src, kts, hi, lo, gcol, toks, free, done, pause=True):
            for k0 in range(0, kts, 2):
                bank, bfree = yield from wait_for(misc)
                tk = transposed([src(k0 + i, t) for i in range(2) for t in range(2)], bank, toks, bfree)
                if pause:
                    yield
                b = banks[bank][:, :].rearrange("p (k n) -> p k n", k=2)
                if gcol is None:
                    h = A.do(P(nc.scalar.activation, hi(k0, 2), b, ACT.Copy), tk, free)
                    low = V.do(P(nc.vector.tensor_tensor, lo(k0, 2), b, bf(hi(k0, 2)), ALU.subtract), h, free)
                else:
                    for i in range(2):
                        h = A.do(P(nc.scalar.activation, hi(k0 + i, 1), b[:, i:i + 1, :], ACT.Copy,
                                   scale=gcol(k0 + i)), tk, free)
                    for i in range(2):
                        low = V.do(P(nc.vector.scalar_tensor_tensor, out=lo(k0 + i, 1), in0=b[:, i:i + 1, :],
                                     scalar=gcol(k0 + i), in1=bf(hi(k0 + i, 1)), op0=ALU.mult,
                                     op1=ALU.subtract), h, free)
                misc.give(bank, low)
                done.append(low)
                yield

        def rstd(ss, n, F, toks, mul=1.0, out=None):
            slot, free = roots.free.pop(0)
            w = RT[:, slot, 0:3 * n].rearrange("p (a n) -> p a n", a=3)
            toks = [toks, free]
            y = stat(n) if out is None else out
            x, a, b = [w[:, i, :] for i in range(3)]
            t = V.do(P(nc.vector.tensor_scalar, x, ss, 1.0 / F, 1e-6, ALU.mult, ALU.add), toks)
            t = V.do(P(nc.vector.tensor_single_scalar, a.bitcast(i32), x.bitcast(i32), 1, ALU.logical_shift_right), t)
            t = V.do(P(nc.vector.tensor_scalar, y.bitcast(i32), a.bitcast(i32), -1.0, 1597463007.0, ALU.mult, ALU.add), t)
            for _ in range(3):
                t = V.do(P(nc.vector.tensor_tensor, a, y, y, ALU.mult), t)
                t = V.do(P(nc.vector.scalar_tensor_tensor, out=b, in0=a, scalar=-0.5, in1=x, op0=ALU.mult,
                           op1=ALU.mult), t)
                t = V.do(P(nc.vector.scalar_tensor_tensor, out=y, in0=b, scalar=1.5, in1=y, op0=ALU.add,
                           op1=ALU.mult), t)
            if mul != 1.0:
                t = V.do(P(nc.vector.tensor_scalar, y, y, mul, None, ALU.mult), t)
            roots.give(slot, t)
            return y, t

        def sum_squares(src, junk, F, toks):
            ss = stat(2)
            t0 = A.do(P(nc.scalar.activation, junk(0), src(0), ACT.Square, accum_out=ss[:, 0:1]), toks)
            t1 = V.do(P(nc.vector.tensor_tensor_reduce, out=junk(1), in0=src(1), in1=src(1), scale=1.0,
                        scalar=0.0, op0=ALU.mult, op1=ALU.add, accum_out=ss[:, 1:2]), toks)
            return rstd(ss, 2, F, [t0, t1])

        def norm_T(src, F, g0, hi, lo, dst, toks, free, ssp=None, done=None, delay=0):
            if ssp is None:
                r, tr = sum_squares(src, dst, F, [toks, None if delay else free])
            else:
                ss = stat(2)
                t = V.do(P(nc.vector.tensor_reduce, ss, ssp, AX.X, ALU.add), toks)
                r, tr = rstd(ss, 2, F, t)
            queue = done is None
            done = [] if queue else done

            def later():
                for _ in range(delay):
                    yield
                n = min(F, 512)
                ts = {}

                def scaled(c):
                    if c < F:
                        t0 = A.do(P(nc.scalar.activation, dst(0)[:, c:c + n], src(0)[:, c:c + n], ACT.Copy,
                                    scale=r[:, 0:1]), tr, free)
                        t1 = V.do(P(nc.vector.tensor_scalar, dst(1)[:, c:c + n], src(1)[:, c:c + n], r[:, 1:2], None,
                                    ALU.mult), tr, free)
                        ts[c] = [t0, t1]

                scaled(0)
                for c in range(0, F, n):
                    scaled(c + n)
                    k = c // 128
                    yield from trans_split(lambda kt, t: dst(t)[:, c + 128 * kt:c + 128 * kt + 128], n // 128,
                                           lambda kt, m: hi(k + kt, m), lambda kt, m: lo(k + kt, m),
                                           lambda kt: GC[:, g0 + k + kt:g0 + k + kt + 1], ts[c], free, done,
                                           pause=False)
            if not queue:
                return later()
            tasks.append(later())
            return done

        def hl(buf, k0=0):
            return lambda kt, n: buf[:, k0 + kt:k0 + kt + n, :]

        halves = Slots([TMP[:, 0:512], TMP[:, 512:1024]])

        def head_norm(x, U, L, mul, toks, box):
            while len(halves.free) < 2:
                yield
            t1 = [f for _, f in halves.free]
            halves.free.clear()
            tmp = TMP[:, 0:2 * U * L].rearrange("p (t u l) -> p t u l", t=2, u=U)
            t1 = A.do(P(nc.scalar.activation, tmp, x, ACT.Square), toks, t1)
            yield
            ss = stat(2 * U)
            t2 = V.do(P(nc.vector.tensor_reduce, ss.rearrange("p (t u) -> p t u", t=2), tmp, AX.X, ALU.add), t1)
            halves.give(TMP[:, 0:512], t2)
            halves.give(TMP[:, 512:1024], t2)
            r, t3 = rstd(ss, 2 * U, L, t2, mul)
            r = r.rearrange("p (t u) -> p t u", t=2).unsqueeze(3).to_broadcast([128, 2, U, L])
            box.append(V.do(P(nc.vector.tensor_tensor, x, x, r, ALU.mult), t3))

        def rope(x, U, H, c, s, toks):
            n = U * 2 * H
            a = TMP[:, 0:n].rearrange("p (u c h) -> p u c h", u=U, c=2)
            b = TMP[:, 512:512 + n].rearrange("p (u c h) -> p u c h", u=U, c=2)
            cb = c.unsqueeze(1).to_broadcast([128, U, H])
            sn = s.unsqueeze(1).to_broadcast([128, U, H])
            w = [toks, V.now()]
            t = []
            for i in range(2):
                t.append(V.do(P(nc.vector.tensor_tensor, a[:, :, i, :], x[:, :, i, :], cb, ALU.mult), w))
                t.append(V.do(P(nc.vector.tensor_tensor, b[:, :, i, :], x[:, :, 1 - i, :], sn, ALU.mult), w))
            V.do(P(nc.vector.tensor_tensor, x[:, :, 0, :], a[:, :, 0, :], b[:, :, 0, :], ALU.subtract), t)
            return V.do(P(nc.vector.tensor_tensor, x[:, :, 1, :], a[:, :, 1, :], b[:, :, 1, :], ALU.add), t)

        def attend(scores, U, nk, scale, sink, pslots, blocks, pv, out_cols, finish, combine=None, per_head=None):
            bank, bfree = yield from wait_for(misc)
            tk = scores(bank, bfree)
            yield
            sv = banks[bank][:, 0:U * nk].rearrange("p (u k) -> p u k", u=U)
            m, nm, sm, ri = stat(U), stat(U), stat(U), stat(U)
            t1 = V.do(P(nc.vector.tensor_reduce, m, sv, AX.X, ALU.max), tk)
            if sink is not None:
                t1 = V.do(P(nc.vector.tensor_tensor, m, m, sink, ALU.max), t1)
            if per_head is None:
                t2 = V.do(P(nc.vector.tensor_scalar, nm, m, -scale, None, ALU.mult), t1)
            else:
                t2 = V.do(P(nc.vector.scalar_tensor_tensor, out=nm, in0=m, scalar=-1.0, in1=per_head, op0=ALU.mult,
                            op1=ALU.mult), t1)
            ps, pfree = yield from wait_for(pslots)
            for u in range(U):
                te = A.do(P(nc.scalar.activation, ps[:, u * nk:(u + 1) * nk], sv[:, u, :], ACT.Exp,
                            bias=nm[:, u:u + 1], scale=scale if per_head is None else per_head[:, u:u + 1], accum_out=sm[:, u:u + 1]), t2, pfree)
            misc.give(bank, te, t1)
            ts = te
            if sink is not None:
                es, ee = stat(U), stat(U)
                t3 = V.do(P(nc.vector.tensor_tensor, es, sink, m, ALU.subtract), t1)
                t4 = A.do(P(nc.scalar.activation, ee, es, ACT.Exp), t3)
                ts = V.do(P(nc.vector.tensor_tensor, sm, sm, ee, ALU.add), t4, te)
            tr = V.do(P(nc.vector.reciprocal, ri, sm), ts)
            if combine is not None:
                te = combine(ps, ri, [te, tr])
            yield
            bank, bfree = yield from wait_for(misc)
            tk = transposed([ps[:, 128 * n:128 * n + 128] for n in range(blocks)], bank, te, bfree)
            pslots.give(ps, tk)
            yield
            pt, tfree = yield from wait_for(PT)
            eng = alt[0]
            alt[0] = 1 - eng
            if eng:
                tc = A.do(P(nc.scalar.activation, PTb[:, pt, 0:128 * blocks], banks[bank][:, 0:128 * blocks],
                            ACT.Copy), tk, tfree)
            else:
                tc = V.do(P(nc.vector.tensor_copy, PTb[:, pt, 0:128 * blocks], banks[bank][:, 0:128 * blocks]),
                          tk, tfree)
            misc.give(bank, tc)
            yield
            bank, bfree = yield from wait_for(misc)
            tk = pv(bank, PTb[:, pt, :], [tc, bfree])
            PT.give(pt, tk)
            yield
            tf = finish(banks[bank][:, 0:out_cols], ri, [tk, tr])
            misc.give(bank, tf)

        alt = [0]

        def mm(outp, l, r, start, stop):
            return P(nc.tensor.matmul, outp, l, r, start=start, stop=stop)

        x_v = D["x"].rearrange("(t p) n -> p t n", p=128)
        t_x = [load(R[:, :, 512 * j:512 * j + 512], x_v[:, :, 512 * j:512 * j + 512], q=S) for j in range(4)]
        t_c = load(C[:, :], D["consts"], q=S)
        t_gc = load(GC[:, :], D["gain_cols"])
        t_pos = load(POS[:, :], D["pos"])
        t_gr = load(GR[:, :], D["gain_rows"])
        BD = stat(64)
        t_bd = load(BD, D["table"])
        consts = [t_c, t_gc]

        ssx = stat(8).rearrange("p (t c) -> p t c", t=2)
        x_sq = []
        for j in range(4):
            c = slice(512 * j, 512 * j + 512)
            x_sq.append(A.do(P(nc.scalar.activation, Y[:, 0, c], R[:, 0, c], ACT.Square, accum_out=ssx[:, 0, j:j + 1]),
                             t_x[j]))
            x_sq.append(V.do(P(nc.vector.tensor_tensor_reduce, out=Y[:, 1, c], in0=R[:, 1, c], in1=R[:, 1, c], scale=1.0,
                               scalar=0.0, op0=ALU.mult, op1=ALU.add, accum_out=ssx[:, 1, j:j + 1]), t_x[j]))
        for q in (T, A, V):
            q.wait(consts)

        nA = norm_T(lambda t: R[:, t, :], 2048, 0, hl(AH), hl(AL), lambda t: Y[:, t, :], x_sq, x_sq, ssp=ssx)

        bias = M[:, 0:6144].rearrange("p (h s k) -> p h s k", h=16, s=3)
        OH = [Y[:, i, 0:1024].rearrange("p (k q) -> p k q", k=8) for i in range(2)]
        dist = [Y[:, i, 1024:2048].bitcast(i32).rearrange("p (k q) -> p k q", k=8) for i in range(2)]
        bias_done = []

        def bias_gen():
            chunks = [(pair, qb, kb, c) for pair, (qb, kb) in enumerate([(0, 0), (1, 0), (1, 1)]) for c in range(4)]
            td, t2, tk = {}, {}, {}

            def sub(n):
                pair, qb, kb, c = chunks[n]
                pq = POS[:, 128 * qb:128 * qb + 128].unsqueeze(1).to_broadcast([128, 8, 128])
                pk = POS[:, 256 + 32 * kb + 8 * c:256 + 32 * kb + 8 * c + 8].unsqueeze(2).to_broadcast([128, 8, 128])
                td[n] = G.do(P(nc.gpsimd.tensor_tensor, dist[n % 2], pq, pk, ALU.subtract), t_pos,
                             t2[n - 2] if n >= 2 else x_read)

            def hot(n):
                i = n % 2
                t1 = V.do(P(nc.vector.tensor_scalar, OH[i], dist[i], C[:, 512:513], None, ALU.is_ge), td[n],
                          tk[n - 2] if n >= 2 else x_read)
                t2[n] = V.do(P(nc.vector.scalar_tensor_tensor, out=OH[i], in0=dist[i], scalar=C[:, 513:514],
                               in1=OH[i], op0=ALU.is_lt, op1=ALU.mult), t1)

            sub(0)
            sub(1)
            yield
            for n in range(13):
                if n < 12:
                    hot(n)
                    if n + 2 < 12:
                        sub(n + 2)
                yield
                if n == 0:
                    continue
                m = n - 1
                pair, qb, kb, c = chunks[m]
                bank, bfree = yield from wait_for(misc)
                T.wait([t2[m], t_bd, bfree])
                for k in range(8):
                    f = mm(banks[bank][:, 64 * k:64 * k + 64], OH[m % 2][:, k, :], BD, True, True)
                    if k < 7:
                        T.quiet(f)
                tk[m] = T.do(f)
                mask = upper if pair == 1 else causal
                bv = banks[bank][:, :].rearrange("p (k g h) -> p h g k", k=8, g=4)
                bo = bias[:, :, pair, :].rearrange("p h (g x) -> p h g x", g=4)[:, :, :, 8 * c:8 * c + 8]
                mv = mask.rearrange("p (g x) -> p g x", g=4)[:, :, 8 * c:8 * c + 8]
                tb = V.do(P(nc.vector.tensor_tensor, bo, bv, mv.unsqueeze(1).to_broadcast([128, 16, 4, 8]), ALU.add), tk[m])
                misc.give(bank, tb)
                bias_done.append(tb)
                yield

        CS = stat(128).rearrange("p (c t j) -> p c t j", c=2, t=2)

        def rope_tables():
            pf = stat(2)
            ang, nn, r, ab = [TMP[:, 64 * i:64 * i + 64].rearrange("p (t j) -> p t j", t=2) for i in range(4)]
            t = V.do(P(nc.vector.tensor_copy, pf, POS[:, 320:322]), t_pos)
            for i in range(2):
                last = V.do(P(nc.vector.tensor_scalar, ang[:, i, :], C[:, 834:866], pf[:, i:i + 1], None, ALU.mult), t)
            t = last
            t = V.do(P(nc.vector.tensor_scalar, nn, ang, 1.0 / (2 * math.pi), 12582912.0, ALU.mult, ALU.add), t)
            t = V.do(P(nc.vector.tensor_scalar, nn, nn, -12582912.0, None, ALU.add), t)
            rest = 2 * math.pi
            src = ang
            for bits in (8, 19, 30, None):
                if bits is None:
                    part = rest
                else:
                    part = math.floor(rest * 2.0 ** (bits - 3)) / 2.0 ** (bits - 3)
                rest -= part
                t = V.do(P(nc.vector.scalar_tensor_tensor, out=r, in0=nn, scalar=-part, in1=src, op0=ALU.mult,
                           op1=ALU.add), t)
                src = r
            t = V.do(P(nc.vector.tensor_scalar, r, r, 3.1415925, -3.1415925, ALU.min, ALU.max), t)
            t1 = V.do(P(nc.vector.scalar_tensor_tensor, out=ab, in0=r, scalar=-1.0, in1=r, op0=ALU.mult, op1=ALU.min), t)
            t1 = V.do(P(nc.vector.tensor_scalar, ab, ab, math.pi / 2, None, ALU.add), t1)
            A.do(P(nc.scalar.activation, CS[:, 0], ab, ACT.Sin), t1)
            return A.do(P(nc.scalar.activation, CS[:, 1], r, ACT.Sin), t)

        def evac2(pair, b, last, dst, *toks):
            t0 = A.do(P(nc.scalar.activation, dst(0), b[0][:, :], ACT.Copy), last, toks)
            t1 = V.do(P(nc.vector.tensor_copy, dst(1), b[1][:, :]), last, toks)
            accs.give(pair, t0, t1)
            return [t0, t1]

        def row2(a, n, src):
            return src[:, a:a + n].rearrange("p (t n) -> p t n", t=2)

        swa_k = row2(9216, 1024, M)
        qswT = M[:, 6144:8192].rearrange("p (k n) -> p k n", k=8)
        kswT = M[:, 8192:9216].rearrange("p (k n) -> p k n", k=4)
        kpe = row2(11776, 128, M)
        qlat, qtmp = row2(0, 1024, Rf), row2(1024, 1024, Rf)
        kvtmp = PTb[:, :, 0:256]
        gq, gk = GR[:, 0:192], GR[:, 192:384]
        sinks = GR[:, 384:400]

        pair, b, last = gemm("w_in_a", 0, 16, AH, AL, nA)
        finish_tasks()
        x_read = everyone()
        te = evac2(pair, b, last, lambda t: qlat[:, t, :], x_read)
        nQ = norm_T(lambda t: qlat[:, t, :], 512, 16, hl(BH), hl(BL), lambda t: qtmp[:, t, :], te, x_read)
        toks_ = Slots([row2(2048 + 1024 * i, 1024, Rf) for i in range(2)], x_read)
        idle.append(bias_gen())
        pair, b, last = gemm("w_in_a", 8, 16, AH, AL, nA, 2)
        te = evac2(pair, b, last, lambda t: swa_k[:, t, :], x_read)
        nKV = norm_T(lambda t: swa_k[:, t, 0:256], 256, 20, hl(BH, 4), hl(BL, 4), lambda t: kvtmp[:, t, :], te, None)
        t_ksw, t_kpe = [], []
        t_rope = rope_tables()

        def k_side(te=te):
            ts, free = yield from wait_for(toks_)
            pad = ts.rearrange("p t (k d n) -> p t k d n", k=2, d=2)
            tz = G.do(P(nc.gpsimd.memset, ts, 0.0), free)
            tn, box = [], []
            kv = swa_k[:, :, 256:384].rearrange("p t (u l) -> p t u l", u=2)
            yield from head_norm(kv, 2, 64, 1.0, [te, t_rope], box)
            for d in range(2):
                for t in range(2):
                    tn.append(V.do(P(nc.vector.tensor_copy, pad[:, t, :, d, 64 * d:64 * d + 64], kv[:, t]), box, tz))
            yield
            for k in range(2):
                bank, bfree = yield from wait_for(misc)
                tk = transposed([pad[:, t, k, d] for d in range(2) for t in range(2)], bank, tn, bfree)
                tc = A.do(P(nc.scalar.activation, kswT[:, 2 * k:2 * k + 2, :],
                            banks[bank][:, :].rearrange("p (k n) -> p k n", k=2), ACT.Copy, scale=GC[:, 91:92]), tk)
                misc.give(bank, tc)
                t_ksw.append(tc)
            toks_.give(ts, tk)

        tasks.append(k_side())

        slot, tok = piece("w_in_b", 0)
        bank, free = take(misc)
        T.wait([tok, free])
        kpeT = banks[bank][0:64, 0:256]
        for kt in range(16):
            w = slice(64 * kt, 64 * kt + 64)
            T.quiet(mm(kpeT, whi[:, slot, w], AH[:, kt, :], kt == 0, False))
            T.quiet(mm(kpeT, wlo[:, slot, w], AH[:, kt, :], False, False))
            last = T.do(mm(kpeT, whi[:, slot, w], AL[:, kt, :], False, kt == 15))
        used_up(last)

        def kpe_side(bank=bank, last=last):
            half, free = yield from wait_for(halves)
            tc = A.do(P(nc.scalar.activation, half[0:64, 0:256], banks[bank][0:64, 0:256], ACT.Copy), last, free)
            misc.give(bank, tc)
            yield
            bank, bfree = yield from wait_for(misc)
            T.wait([tc, bfree])
            for t in range(2):
                tk = T.do(P(nc.tensor.transpose, banks[bank][:, 64 * t:64 * t + 64], half[0:64, 128 * t:128 * t + 128],
                            ident[0:64, 0:64]))
            halves.give(half, tk)
            yield
            tc = A.do(P(nc.scalar.activation, kpe, banks[bank][:, 0:128].rearrange("p (t n) -> p t n", t=2), ACT.Copy),
                      tk)
            misc.give(bank, tc)
            t_kpe.append(tc)

        tasks.append(kpe_side())
        step()

        qsw_t = []

        def q_side(ts, te, j):
            tn = []
            yield from head_norm(ts.rearrange("p t (u l) -> p t u l", u=8), 8, 64, 0.125, [te], tn)
            yield
            for k0 in (0, 2):
                bank, bfree = yield from wait_for(misc)
                tk = transposed([ts[:, t, 128 * (k0 + i):128 * (k0 + i) + 128] for i in range(2) for t in range(2)],
                                bank, tn, bfree)
                tc = A.do(P(nc.scalar.activation, qswT[:, 4 * j + k0:4 * j + k0 + 2, :],
                            banks[bank][:, :].rearrange("p (k n) -> p k n", k=2), ACT.Copy, scale=GC[:, 90:91]), tk)
                misc.give(bank, tc)
                qsw_t.append(tc)
            toks_.give(ts, tk)

        for j in range(2):
            pair, b, last = gemm("w_in_a", 16 + 8 * j, 16, AH, AL, nA, 2)
            ts, free = take(toks_)
            te = evac2(pair, b, last, lambda t: ts[:, t, :], free)
            tasks.append(q_side(ts, te, j))
        a_free = [last]

        OM, OS = Y[:, :, 0:1024], Y[:, :, 1024:2048]
        ps3 = [M[:, 10240 + 512 * i:10752 + 512 * i] for i in range(3)]
        psw = Slots(ps3)
        os_done = []

        def swa_unit(t, h0):
            U = 2 if t else 4
            nk = 256 if t else 128

            def scores(bank, bfree):
                assert len(qsw_t) == 4 and len(t_ksw) == 2 and len(bias_done) == 12
                T.wait([qsw_t, t_ksw, bias_done[-1], bfree])
                for u in range(U):
                    h = h0 + u
                    o = banks[bank][:, u * nk:(u + 1) * nk]
                    bs = bias[:, h, 1:3, :].rearrange("p s k -> p (s k)") if t else bias[:, h, 0, :]
                    T.quiet(mm(o, ident, bs, True, False))
                    f = mm(o, qswT[:, h // 2, 128 * t:128 * t + 128], kswT[:, 2 * (h // 8) + h % 2, 0:nk], False, True)
                    tk = T.do(f)
                return tk

            def pv(bank, pt, toks):
                T.wait(toks)
                for u in range(U):
                    kvh = h0 // 8
                    for kb in range(nk // 128):
                        f = mm(banks[bank][:, 64 * u:64 * u + 64], pt[:, u * nk + 128 * kb:u * nk + 128 * kb + 128],
                               swa_k[:, kb, 384 + 64 * kvh:448 + 64 * kvh], kb == 0, kb == nk // 128 - 1)
                        tk = T.do(f)
                return tk

            def finish(o, ri, toks):
                tf = V.do(P(nc.vector.tensor_tensor,
                            OS[:, t, :].rearrange("p (u l) -> p u l", u=16)[:, h0:h0 + U, :],
                            o.rearrange("p (u l) -> p u l", u=U), ri.unsqueeze(2).to_broadcast([128, U, 64]),
                            ALU.mult), toks, bias_done[-1])
                os_done.append(tf)
                return tf

            return attend(scores, U, nk, 1.0, sinks[:, h0:h0 + U], psw, 4, pv, 64 * U, finish)

        def swa():
            while len(qsw_t) < 4:
                yield
            yield from pipelined([swa_unit(0, h) for h in range(0, 16, 4)] + [swa_unit(1, h) for h in range(0, 16, 2)], 3)

        idle.append(swa())

        VM = row2(0, 2048, Rf)
        rq, rk = stat(16).rearrange("p (t h) -> p t h", t=2), stat(16).rearrange("p (t h) -> p t h", t=2)
        ssq, ssk = stat(32).rearrange("p (a t h) -> p a t h", a=2, t=2), stat(16).rearrange("p (t h) -> p t h", t=2)
        sspe = stat(2)
        t_ssk = []
        t_ssq, qt_done, kt_done, t_rq, t_rk = [], [], [], [], []

        def squares(x, U, L, out, toks):
            half, free = yield from wait_for(halves)
            tmp = half[:, 0:U * L].rearrange("p (u l) -> p u l", u=U)
            a = A.do(P(nc.scalar.activation, tmp, x, ACT.Square), toks, free)
            yield
            a = V.do(P(nc.vector.tensor_reduce, out, tmp, AX.X, ALU.add), a)
            halves.give(half, a)
            return a

        def rope_alone(*args):
            while len(halves.free) < 2:
                yield
            f = [f for _, f in halves.free]
            a = rope(*args[:-1], [args[-1], f])
            halves.free[:] = [(h, [a]) for h, _ in halves.free]
            return a

        def q_nope(ts, te, j):
            for t in range(2):
                t_ssq.append((yield from squares(ts[:, t, :].rearrange("p (u l) -> p u l", u=4), 4, 128,
                                                 ssq[:, 0, t, 4 * j:4 * j + 4], te)))
                yield
            yield from trans_split(lambda kt, t: ts[:, t, 128 * kt:128 * kt + 128], 4, hl(AH, 4 * j), hl(AL, 4 * j),
                                   lambda kt: GC[:, 88:89], te, a_free, qt_done)
            toks_.give(ts, t_ssq, T.now())

        def q_rope(ts, te, j):
            tr = []
            for t in range(2):
                x = ts[:, t, :].rearrange("p (u l) -> p u l", u=8)
                a = yield from squares(x, 8, 64, ssq[:, 1, t, :], te)
                a = V.do(P(nc.vector.tensor_tensor, x, x, gq[:, 128:192].unsqueeze(1).to_broadcast([128, 8, 64]),
                           ALU.mult), a, t_gr)
                yield
                tr.append((yield from rope_alone(ts[:, t, :].rearrange("p (u c h) -> p u c h", u=8, c=2), 8, 32,
                                                 CS[:, 0, t], CS[:, 1, t], [a, t_rope])))
                yield
            yield from trans_split(lambda kt, t: ts[:, t, 128 * kt:128 * kt + 128], 4, hl(AH, 8), hl(AL, 8),
                                   None, tr, a_free, qt_done)
            toks_.give(ts, T.now())

        def q_scale():
            a = V.do(P(nc.vector.tensor_tensor, ssq[:, 0], ssq[:, 0], ssq[:, 1], ALU.add), t_ssq, V.now())
            flat_rq, flat_ssq = rq.rearrange("p t h -> p (t h)"), ssq[:, 0].rearrange("p t h -> p (t h)")
            t_rq.append(rstd(flat_ssq, 16, 192, a, 192 ** -0.5, flat_rq)[1])

        def k_nope(ts, te, j):
            h = slice(4 * j, 4 * j + 4)
            tn = []
            for t in range(2):
                x = ts[:, t, :].rearrange("p (u l) -> p u l", u=4)
                t_ssk.append((yield from squares(x, 4, 128, ssk[:, t, h], te)))
                if j == 0:
                    half, free = yield from wait_for(halves)
                    a = A.do(P(nc.scalar.activation, half[:, 0:64], kpe[:, t, :], ACT.Square,
                               accum_out=sspe[:, t:t + 1]), t_kpe, free)
                    halves.give(half, a)
                    t_ssk.append(a)
            while len(t_ssk) < 6:
                yield
            if not t_rk:
                a = V.do(P(nc.vector.tensor_tensor, ssk, ssk, sspe.unsqueeze(2).to_broadcast([128, 2, 8]), ALU.add), t_ssk)
                t_rk.append(rstd(ssk.rearrange("p t h -> p (t h)"), 16, 192, a, 1.0, rk.rearrange("p t h -> p (t h)"))[1])
                yield
            for t in range(2):
                x = ts[:, t, :].rearrange("p (u l) -> p u l", u=4)
                tn.append(V.do(P(nc.vector.tensor_tensor, x, x, rk[:, t, h].unsqueeze(2).to_broadcast([128, 4, 128]),
                                 ALU.mult), t_rk))
                yield
            yield from trans_split(lambda kt, t: ts[:, t, 128 * kt:128 * kt + 128], 4, hl(BH, 6 + 4 * j),
                                   hl(BL, 6 + 4 * j), lambda kt: GC[:, 89:90], tn, None, kt_done)
            toks_.give(ts, T.now())

        def odd(buf):
            return lambda kt, n: buf[:, (4, 14)[kt // 2]:(4, 14)[kt // 2] + n, :]

        def k_rope():
            while not t_rk:
                yield
            a = []
            for t in range(2):
                w = V.do(P(nc.vector.tensor_tensor, kpe[:, t, :], kpe[:, t, :], gk[:, 128:192], ALU.mult), t_kpe, t_gr,
                         t_rk, A.now())
                a.append((yield from rope_alone(kpe[:, t, :].rearrange("p (u c h) -> p u c h", u=1, c=2), 1, 32,
                                                CS[:, 0, t], CS[:, 1, t], [w, t_rope])))
                yield
            for d, (hi, lo, free_d) in enumerate(((hl(AH, 12), hl(AL, 12), a_free), (odd(BH), odd(BL), kv_free))):
                ts, free = yield from wait_for(toks_)
                tz = G.do(P(nc.gpsimd.memset, ts, 0.0), free)
                tr = []
                for t in range(2):
                    x = ts[:, t, :].rearrange("p (h n) -> p h n", h=4)[:, :, 64 * d:64 * d + 64]
                    tr.append(V.do(P(nc.vector.tensor_tensor, x, kpe[:, t, :].unsqueeze(1).to_broadcast([128, 4, 64]),
                                     rk[:, t, d:8:2].unsqueeze(2).to_broadcast([128, 4, 64]), ALU.mult), a, tz))
                yield
                yield from trans_split(lambda kt, t: ts[:, t, 128 * kt:128 * kt + 128], 4, hi, lo, None, tr, free_d,
                                       kt_done)
                toks_.give(ts, T.now())

        t_v = []
        for j in range(4):
            pair, b, last = gemm("w_kv_b", j, 2, BH[:, 4:6, :], BL[:, 4:6, :], nKV, 2)
            if j < 2:
                ts, free = take(toks_)
                te = evac2(pair, b, last, lambda t: ts[:, t, :], free)
                tasks.append(k_nope(ts, te, j))
                step(2)
            else:
                t_v += evac2(pair, b, last, lambda t: VM[:, t, 512 * (j - 2):512 * (j - 2) + 512], x_read, T.now())
        assert len(nQ) == 2
        kv_free = [last]
        tasks.append(k_rope())

        for j in (2, 0, 1):
            pair, b, last = gemm("w_q_b", 2 * j, 4, BH, BL, nQ, 2)
            ts, free = take(toks_)
            te = evac2(pair, b, last, lambda t: ts[:, t, :], free)
            tasks.append(q_nope(ts, te, j) if j < 2 else q_rope(ts, te, j))
            step(2)
        lend_banks()
        finish_idle()
        pml = Slots(ps3 + [M[:, 512 * i:512 * i + 512] for i in range(3)], everyone())
        om_free = everyone()
        om_done = []

        def mla_unit(t, h0):
            U = 2 if t else 4
            nk = 256 if t else 128

            def scores(bank, bfree):
                T.wait([qt_done, kt_done, bfree])
                a = slice(128 * t, 128 * t + 128)
                for u in range(U):
                    h = h0 + u
                    n = min(256, 512 - u * nk)
                    o = banks[bank][:, u * nk:u * nk + n]
                    for i, (ql, kl) in enumerate(((AH, BH), (AH, BL), (AL, BH))):
                        T.quiet(mm(o, ql[:, h, a], kl[:, 6 + h, 0:n], i == 0, False))
                    kh, kl, q = (BH, BL, (4, 5, 14, 15)[h // 2]) if h % 2 else (AH, AL, 12 + h // 2)
                    for ql, kk in ((AH, kh), (AH, kl), (AL, kh)):
                        T.quiet(mm(o, ql[:, 8 + h // 2, a], kk[:, q, 0:n], False, False))
                    tk = T.do(mm(banks[bank][:, u * nk + 128 * t:u * nk + 128 * t + 128], ident, causal, False, True))
                return tk

            def pv(bank, pt, toks):
                T.wait([toks, t_v])
                for u in range(U):
                    v0 = 128 * (h0 + u)
                    for kb in range(nk // 128):
                        tk = T.do(mm(banks[bank][:, 128 * u:128 * u + 128],
                                     pt[:, u * nk + 128 * kb:u * nk + 128 * kb + 128],
                                     VM[:, kb, v0:v0 + 128], kb == 0, kb == nk // 128 - 1))
                return tk

            def finish(o, ri, toks):
                tf = V.do(P(nc.vector.tensor_tensor,
                            OM[:, t, :].rearrange("p (u l) -> p u l", u=8)[:, h0:h0 + U, :],
                            o.rearrange("p (u l) -> p u l", u=U), ri.unsqueeze(2).to_broadcast([128, U, 128]),
                            ALU.mult), toks, om_free)
                om_done.append(tf)
                return tf

            return attend(scores, U, nk, None, None, pml, 4, pv, 128 * U, finish,
                          per_head=rq[:, t, h0:h0 + U])

        idle.append(pipelined([mla_unit(0, 0), mla_unit(0, 4)] + [mla_unit(1, h) for h in range(0, 8, 2)], 6, 6))
        step()
        q_scale()
        for q in (V, A):
            q.wait(t_rq)
        mix_free = [T.now(), om_free]
        nM = []
        tasks.append(norm_T(lambda t: OS[:, t, :], 1024, 30, hl(AH), hl(AL), lambda t: row2(2048, 2048, M)[:, t, :],
                            [os_done, om_free], mix_free, done=nM, delay=3))
        finish_idle()
        return_banks()
        everything = everyone()
        t_x = load(R[:, :, :], D["x"].rearrange("(t p) n -> p t n", p=128), everything)
        tasks.append(norm_T(lambda t: OM[:, t, :], 1024, 22, hl(AH, 8), hl(AL, 8), lambda t: row2(4096, 2048, M)[:, t, :],
                            [om_done, om_free], mix_free, done=nM, delay=2))
        t_R = [t_x]
        ssr = stat(8).rearrange("p (t c) -> p t c", t=2)

        def add_residual(b, last, j, toks, final=True):
            c = slice(512 * j, 512 * j + 512)
            out = []
            for t in range(2):
                a = V.do(P(nc.vector.tensor_tensor, R[:, t, c], R[:, t, c], b[t][:, :], ALU.add), last, toks)
                out.append(a)
            if final:
                for t in range(2):
                    out.append(A.do(P(nc.scalar.activation, Y[:, t, c], R[:, t, c], ACT.Square,
                                      accum_out=ssr[:, t, j:j + 1]), out[t]))
            return out

        for j in range(4):
            pair, b, last = gemm("w_out", 8 * j, 16, AH, AL, nM, hold=4)
            t_R += add_residual(b, last, j, t_x)
            accs.give(pair, t_R[-1], t_R[-3])

        everything = everyone()
        nA = norm_T(lambda t: R[:, t, :], 2048, 38, hl(AH), hl(AL), lambda t: Y[:, t, :], everything,
                    everything, ssp=ssr)
        nB = []
        for j in range(4):
            pair, b, last = gemm_t("peer_w_q", 8 * j, 16, AH, AL, nA)
            th = [A.do(P(nc.scalar.activation, BH[:, 4 * j + 2 * i:4 * j + 2 * i + 2, :],
                         b[i][:, :].rearrange("p (k n) -> p k n", k=2), ACT.Copy), last, everything) for i in range(2)]
            for i in range(2):
                k = slice(4 * j + 2 * i, 4 * j + 2 * i + 2)
                nB.append(V.do(P(nc.vector.tensor_tensor, BL[:, k, :], b[i][:, :].rearrange("p (k n) -> p k n", k=2),
                                 bf(BH[:, k, :]), ALU.subtract), th[i]))
            accs.give(pair, nB[-1])
        norm_read = everyone()
        SC = Y[:, :, :].rearrange("p t (h n) -> p t h n", h=16)
        t_sc = []

        def sub_scores():
            for c in range(2):
                slot, tok = piece("sub_keys", c)
                T.wait([tok, nB])
                for q4 in range(2):
                    for t in range(2):
                        bank, bfree = take(misc)
                        T.wait([bfree])
                        for i in range(4):
                            hp = 8 * c + 4 * q4 + i
                            w = slice(128 * (4 * q4 + i), 128 * (4 * q4 + i) + 128)
                            a = slice(128 * t, 128 * t + 128)
                            o = banks[bank][:, 128 * i:128 * i + 128]
                            T.quiet(mm(o, BH[:, hp, a], whi[:, slot, w], True, False))
                            T.quiet(mm(o, BH[:, hp, a], wlo[:, slot, w], False, False))
                            last = T.do(mm(o, BL[:, hp, a], whi[:, slot, w], False, True))
                        h0 = 8 * c + 4 * q4
                        te = A.do(P(nc.scalar.activation, SC[:, t, h0:h0 + 4, :],
                                    banks[bank][:, :].rearrange("p (h n) -> p h n", h=4), ACT.Copy), last, norm_read)
                        misc.give(bank, te)
                        t_sc.append(te)
                used_up(last)

        V16 = M[:, 4096:4608].rearrange("p (t h k) -> p t h k", t=2, h=16)
        I16 = M[:, 4608:5120].rearrange("p (t h k) -> p t h k", t=2, h=16)
        I16u = I16.bitcast(u32)
        cand = M[:, 5120:7168].rearrange("p (h a b) -> p h a b", h=8, a=16)
        cmp_ = M[:, 7168:9216].rearrange("p (h k r) -> p h k r", h=8, k=16)
        W2 = M[:, 9216:9344].rearrange("p (h k) -> p h k", h=8)
        P2 = M[:, 9344:9472].rearrange("p (h k) -> p h k", h=8)
        P2u = P2.bitcast(u32)
        pij = [M[:, 9472 + 128 * i:9600 + 128 * i] for i in range(2)]
        idg = [M[:, 9728 + 128 * i:9856 + 128 * i] for i in range(3)]
        IDT = M[:, 10240:11008].rearrange("p (a t) -> p a t", a=3)
        OA = BH[:, 0:4, :].rearrange("p (s x) (y n) -> p s (x y) n", s=2, y=2)
        OBh = BH[:, 4:8, :].rearrange("p (s x) (y n) -> p s (x y) n", s=2, y=2)
        OBl = BH[:, 8:12, :].rearrange("p (s x) (y n) -> p s (x y) n", s=2, y=2)
        gh, gl_ = BH[:, 12, :], M[:, 11008:11264]
        stg = [Yf[:, 0:4096].rearrange("p (i t) -> p i t", t=32),
               M[:, 4096:8192].rearrange("p (i t) -> p i t", t=32)]
        s_g = [sem(f"s_gw{i}") for i in range(2)]
        g_written = []

        def top8(vals, outv, outi, toks):
            t1 = V.do(P(nc.vector.max, outv[:, 0:8], vals), toks)
            V.do(P(nc.vector.max_index, outi[:, 0:8], outv[:, 0:8], vals), t1)
            t2 = V.do(P(nc.vector.match_replace, vals, outv[:, 0:8], vals, -3.0e38), V.now())
            t3 = V.do(P(nc.vector.max, outv[:, 8:16], vals), t2)
            return V.do(P(nc.vector.max_index, outi[:, 8:16], outv[:, 8:16], vals), t3)

        def routing():
            t_id = []
            for t in range(2):
                for hp in range(16):
                    last = top8(SC[:, t, hp, :], V16[:, t, hp, :], I16u[:, t, hp, :], [t_sc, everything])
                    yield
            last = V.do(P(nc.vector.tensor_copy, I16, I16u), last)
            for t in range(2):
                v4 = V16[:, t].rearrange("p (h q) k -> p h q k", q=2)
                for h in range(8):
                    if h == 4:
                        yield
                    last = V.do(P(nc.vector.tensor_tensor, cand[:, h],
                                  v4[:, h, 0, :].unsqueeze(2).to_broadcast([128, 16, 16]),
                                  v4[:, h, 1, :].unsqueeze(1).to_broadcast([128, 16, 16]), ALU.add), last)
                yield
                for h in range(8):
                    last = top8(cand[:, h].rearrange("p a b -> p (a b)"), W2[:, h, :], P2u[:, h, :], last)
                    yield
                w3 = idg[2].rearrange("p (h k) -> p h k", h=8)
                sm, ri = stat(8), stat(8)
                a = V.do(P(nc.vector.tensor_tensor, w3, W2, W2[:, :, 0:1].to_broadcast([128, 8, 16]), ALU.subtract),
                         last, t_id)
                a = A.do(P(nc.scalar.activation, idg[2], idg[2], ACT.Exp), a)
                a = V.do(P(nc.vector.tensor_reduce, sm, w3, AX.X, ALU.add), a)
                a = V.do(P(nc.vector.reciprocal, ri, sm), a)
                tg = V.do(P(nc.vector.tensor_tensor, w3, w3, ri.unsqueeze(2).to_broadcast([128, 8, 16]), ALU.mult), a)
                yield
                pu = [x.bitcast(u32) for x in pij]
                flatp = P2u.rearrange("p h k -> p (h k)")
                a1 = V.do(P(nc.vector.tensor_single_scalar, pu[0], flatp, 4, ALU.logical_shift_right), last)
                a2 = V.do(P(nc.vector.tensor_single_scalar, pu[1], flatp, 15, ALU.bitwise_and), last)
                a1 = V.do(P(nc.vector.tensor_copy, pij[0], pu[0]), a1)
                a2 = V.do(P(nc.vector.tensor_copy, pij[1], pu[1]), a2)
                i4 = I16[:, t].rearrange("p (h q) k -> p h q k", q=2)
                for q in range(2):
                    parts = []
                    for h in (0, 4):
                        hs = slice(h, h + 4)
                        p_ = pij[q].rearrange("p (h k) -> p h k", h=8)[:, hs].unsqueeze(3).to_broadcast([128, 4, 16, 16])
                        io = iota16.unsqueeze(1).unsqueeze(1).to_broadcast([128, 4, 16, 16])
                        a = V.do(P(nc.vector.tensor_tensor, cmp_[:, hs], p_, io, ALU.is_equal), a2, V.now())
                        yield
                        a = V.do(P(nc.vector.tensor_tensor, cmp_[:, hs], cmp_[:, hs],
                                   i4[:, hs, q, :].unsqueeze(2).to_broadcast([128, 4, 16, 16]), ALU.mult), a)
                        yield
                        last = V.do(P(nc.vector.tensor_reduce, idg[q].rearrange("p (h k) -> p h k", h=8)[:, hs],
                                      cmp_[:, hs], AX.X, ALU.add), a, t_id)
                        yield
                bank, bfree = yield from wait_for(misc)
                tk = transposed(idg, bank, last, tg, bfree)
                t_id = [tk]
                tc = A.do(P(nc.scalar.activation, IDT[:, :, 128 * t:128 * t + 128],
                            banks[bank][:, 0:384].rearrange("p (a t) -> p a t", a=3), ACT.Copy), tk, everything)
                misc.give(bank, tc)
                yield
            th = A.do(P(nc.scalar.activation, gh, IDT[:, 2, :], ACT.Copy), tc, q_read)
            ready = V.do(P(nc.vector.tensor_tensor, gl_, IDT[:, 2, :], bf(gh), ALU.subtract), th)
            ready = [ready, T.now()]
            ofree, sfree, tb = {}, {}, {}

            def build(g, k):
                i = g % 2
                for k in (k, k + 1):
                    tt = 4 * g + k
                    w = [ready, ofree.get(g - 2), q_read]
                    V.do(P(nc.vector.tensor_scalar, OA[:, i, k, :], iota, IDT[:, 0, tt:tt + 1], None, ALU.is_equal), w)
                    for ob, gg in ((OBh, bf(gh)), (OBl, gl_)):
                        tb[g] = V.do(P(nc.vector.tensor_scalar, ob[:, i, k, :], iota, IDT[:, 1, tt:tt + 1],
                                       gg[:, tt:tt + 1], ALU.is_equal, ALU.mult), w)

            held = {}

            def multiply(g):
                i = g % 2
                bank, bfree = yield from wait_for(misc)
                T.wait([tb[g], bfree])
                for k in range(4):
                    o = banks[bank][:, 128 * k:128 * k + 128]
                    T.quiet(mm(o, OBh[:, i, k, :], OA[:, i, k, :], True, False))
                    tk = T.do(mm(o, OBl[:, i, k, :], OA[:, i, k, :], False, True))
                ofree[g] = tk
                held[g] = bank

            def keep(g):
                s, bank, tk = (g // 8) % 2, held[g], ofree[g]
                tev = A.do(P(nc.scalar.activation, stg[s][:, :, 4 * (g % 8):4 * (g % 8) + 4],
                             banks[bank][:, :].rearrange("p (t i) -> p i t", t=4), ACT.Copy), tk,
                           sfree.get(g // 8 - 2), ready)
                misc.give(bank, tev)
                if g % 8 == 7:
                    c = g // 8
                    w = G.dma(P(nc.gpsimd.dma_start, D["scr_g"][c, :, :],
                                stg[s].rearrange("p i t -> p (i t)")), s_g[s], 16 * (c // 2 + 1), tev)
                    sfree[c] = w
                    g_written.append(w)

            for g in range(65):
                if g < 64:
                    build(g, 0)
                if g > 0:
                    yield from multiply(g - 1)
                yield
                if g < 64:
                    build(g, 2)
                if g > 0:
                    keep(g - 1)
                yield
            bar.append(everyone())
            fetch(0)
            fetch(1)
            for _ in range(4):
                yield
            yield from prepare(0)

        gls = Slots([(i, M[:, 2048 + 1024 * i:3072 + 1024 * i].rearrange("p (k n) -> p k n", k=4)) for i in range(2)],
                    everything)
        s_a = [sem(f"s_aw{i}") for i in range(2)]
        na = [0, 0]
        a_written = {}

        def u_post(pair, b, last, j):
            (gi, gl), gfree = take(gls)
            for i in range(2):
                tg = A.do(P(nc.scalar.activation, gl[:, 2 * i:2 * i + 2, :],
                            b[i][:, :].rearrange("p (k n) -> p k n", k=2), ACT.Gelu_apprx_tanh), last, gfree)
            accs.give(pair, tg)
            na[gi] += 16
            h = j % 2
            a_written[j] = G.dma(P(nc.gpsimd.dma_start, D["scr_a"][j // 2, :, 1024 * h:1024 * h + 1024],
                                   gl.rearrange("p k n -> p (k n)")), s_a[gi], na[gi], tg)
            gls.give((gi, gl), a_written[j])

        s_la = [sem(f"s_la{i}") for i in range(2)]
        s_lg = [sem(f"s_lg{i}") for i in range(2)]
        glt = [M[:, 4096 * (1 + i):4096 * (1 + i) + 2048] for i in range(2)]
        gtt = [M[:, 4096 * (1 + i) + 2048:4096 * (1 + i) + 4096] for i in range(2)]
        bar = []
        lt = {}
        wB = {}
        vdone = {}
        tw_free = {}

        def fetch(sc):
            i = sc % 2
            w = bar if sc < 2 else tw_free[sc - 2]
            l1 = G.dma(P(nc.gpsimd.dma_start, glt[i], D["scr_a"][sc, :, :]), s_la[i], 16 * (sc // 2 + 1),
                       w, a_written[2 * sc], a_written[2 * sc + 1])
            l2 = G.dma(P(nc.gpsimd.dma_start, gtt[i].rearrange("p (c n) -> p c n", c=8),
                         D["scr_g"][:, :, 256 * sc:256 * sc + 256].rearrange("c p n -> p c n")),
                       s_lg[i], 16 * (sc // 2 + 1), w, g_written)
            lt[sc] = [l1, l2]

        def prepare(sc):
            i = sc % 2
            a = glt[i].rearrange("p (k c t) -> p k c t", k=8, c=8)
            g = gtt[i].rearrange("p (c k t) -> p k c t", k=8, c=8)
            free = vdone.get(sc - 2)
            done = wB[sc] = []
            for k0 in range(0, 8, 2):
                t1 = None
                for k in (k0, k0 + 1):
                    t1 = V.do(P(nc.vector.tensor_tensor, a[:, k], a[:, k], g[:, k], ALU.mult), lt[sc])
                src = glt[i][:, 256 * k0:256 * k0 + 512].rearrange("p (k n) -> p k n", k=2)
                o = 8 * i + k0
                h = A.do(P(nc.scalar.activation, BH[:, o:o + 2, :], src, ACT.Copy), t1, free, bar)
                done.append(V.do(P(nc.vector.tensor_tensor, BL[:, o:o + 2, :], src, bf(BH[:, o:o + 2, :]), ALU.subtract), h))
                yield
            tw_free[sc] = [done[-1]]
            if sc + 2 < 16:
                fetch(sc + 2)

        for j in range(32):
            pair, b, last = gemm_t("peer_u", 8 * j, 16, AH, AL, nA)
            u_post(pair, b, last, j)
            if j == 0:
                finish_tasks()
                sub_scores()
                q_read = T.now()
                idle.append(routing())
        while len(wB.get(0, ())) < 4:
            step()
        lastR = t_R
        for sc in range(16):
            if sc + 1 < 16:
                tasks.append(prepare(sc + 1))
            o = 8 * (sc % 2)
            for j in range(4):
                pair, b, last = gemm("peer_v", 16 * sc + 4 * j, 8, BH[:, o:o + 8, :], BL[:, o:o + 8, :], wB[sc])
                out_r = add_residual(b, last, j, lastR, sc == 15)
                accs.give(pair, out_r)
                if sc == 15:
                    t_R = t_R + out_r
            lastR = [V.now()]
            vdone[sc] = [last]
            finish_tasks()

        everything = everyone()
        nA = norm_T(lambda t: R[:, t, :], 2048, 54, hl(AH), hl(AL), lambda t: Y[:, t, :], everything,
                    everything, ssp=ssr)
        QA = M[:, 0:2048].rearrange("p (k n) -> p k n", k=8)
        KA = M[:, 2048:4096].rearrange("p (k n) -> p k n", k=8)
        VA = M[:, 4096:6144].rearrange("p (t n) -> p t n", t=2)
        VN = M[:, 6144:8192].rearrange("p (t n) -> p t n", t=2)
        QN = Yf[:, 0:2048].rearrange("p (k n) -> p k n", k=8)
        KN = Yf[:, 2048:4096].rearrange("p (k n) -> p k n", k=8)
        toks_ = Slots([M[:, 8192 + 1024 * i:9216 + 1024 * i].rearrange("p (t n) -> p t n", t=2) for i in range(2)],
                      everything)
        pslots = Slots([M[:, 10240 + 512 * i:10752 + 512 * i] for i in range(2)], everything)
        nbs = [M[:, 11264 + 512 * i:11776 + 512 * i] for i in range(2)]

        lamb = TMP[:, 0:512]
        t_l = load(lamb, D["lam"], everything)
        ls, le, lam = stat(2), stat(2), stat(1)
        for i in range(2):
            t1 = V.do(P(nc.vector.tensor_tensor_reduce, out=TMP[:, 512 + 128 * i:640 + 128 * i],
                        in0=TMP[:, 256 * i:256 * i + 128], in1=TMP[:, 256 * i + 128:256 * i + 256], scale=1.0,
                        scalar=0.0, op0=ALU.mult, op1=ALU.add, accum_out=ls[:, i:i + 1]), t_l, everything)
        t2 = A.do(P(nc.scalar.activation, le, ls, ACT.Exp), t1)
        t3 = V.do(P(nc.vector.tensor_tensor, lam, le[:, 0:1], le[:, 1:2], ALU.subtract), t2)
        t_lam = V.do(P(nc.vector.tensor_scalar, lam, lam, 0.8 - 0.6 * float(np.exp(-0.0)), None, ALU.add), t3)

        tdone = {"QA": [], "KA": [], "QN": [], "KN": [], "VA": [], "VN": []}

        def qk_post(pair, b, last, name, dst, j):
            ts, free = take(toks_)
            te = evac2(pair, b, last, lambda t: ts[:, t, :], free)

            def later():
                yield
                tt = []
                for t in range(2):
                    tt.append(rope(ts[:, t, :].rearrange("p (u c h) -> p u c h", u=4, c=2), 4, 64,
                                   cos2[:, t], sin2[:, t], [te, t_lam]))
                    yield
                for k0 in (0, 2):
                    bank, bfree = yield from wait_for(misc)
                    tk = transposed([ts[:, t, 128 * (k0 + i):128 * (k0 + i) + 128] for i in range(2) for t in range(2)],
                                    bank, tt, bfree)
                    yield
                    tc = A.do(P(nc.scalar.activation, dst[:, 4 * j + k0:4 * j + k0 + 2, :],
                                banks[bank][:, :].rearrange("p (k n) -> p k n", k=2), ACT.Copy), tk, everything, y_free)
                    misc.give(bank, tc)
                    tdone[name].append(tc)
                toks_.give(ts, tk)
            tasks.append(later())

        def da_unit(h, t):
            def scores(bank, bfree):
                T.wait([tdone["QA"], tdone["KA"], bfree])
                for c in range(2):
                    tk = T.do(mm(banks[bank][:, 256 * c:256 * c + 256], QA[:, 2 * h + c, 128 * t:128 * t + 128],
                                 KA[:, 2 * h + c, :], True, True))
                return tk

            def combine(ps, ri, toks):
                rl = stat(1)
                a = V.do(P(nc.vector.tensor_tensor, rl, ri[:, 1:2], lam, ALU.mult), toks, t_lam)
                a = V.do(P(nc.vector.tensor_scalar, ps[:, 256:512], ps[:, 256:512], rl, None, ALU.mult), a)
                return V.do(P(nc.vector.scalar_tensor_tensor, out=ps[:, 0:256], in0=ps[:, 0:256],
                              scalar=ri[:, 0:1], in1=ps[:, 256:512], op0=ALU.mult, op1=ALU.subtract), a)

            def pv(bank, pt, toks):
                T.wait([toks, tdone["VA"]])
                for kb in range(2):
                    tk = T.do(mm(banks[bank][:, 0:256], pt[:, 128 * kb:128 * kb + 128],
                                 VA[:, kb, 256 * h:256 * h + 256], kb == 0, kb == 1))
                return tk

            def finish(o, ri, toks):
                tf = A.do(P(nc.scalar.activation, QA[:, 2 * h:2 * h + 2, 128 * t:128 * t + 128],
                            o.rearrange("p (c n) -> p c n", c=2), ACT.Copy), toks)
                oa_done.append(tf)
                return tf

            return attend(scores, 2, 256, 128 ** -0.5, None, pslots, 2, pv, 256, finish, combine)

        s_nb = [sem(f"s_nb{i}") for i in range(2)]
        nb_t, nb_free = {}, {}

        def nb_fetch(h):
            i = h % 2
            nb_t[h] = G.dma(P(nc.gpsimd.dma_start, nbs[i], D["na_bias"][h, :, :]), s_nb[i], 16 * (h // 2 + 1),
                            nb_free.get(h - 2, everything))

        def na_unit(h):
            i = h % 2

            def scores(bank, bfree):
                v = nbs[i].rearrange("p (r c) -> p r c", c=64)
                tb = V.do(P(nc.vector.tensor_tensor, v, v, namask.unsqueeze(1).to_broadcast([128, 8, 64]), ALU.add),
                          nb_t[h])
                T.wait([tdone["QN"], tdone["KN"], bfree, tb])
                for t in range(2):
                    o = banks[bank][:, 256 * t:256 * t + 256]
                    T.quiet(mm(o, QN[:, h, 128 * t:128 * t + 128], KN[:, h, :], True, False))
                    tk = T.do(mm(o, ident, nbs[i][:, 256 * t:256 * t + 256], False, True))
                nb_free[h] = [tk]
                if h + 2 < 8:
                    nb_fetch(h + 2)
                return tk

            def pv(bank, pt, toks):
                T.wait([toks, tdone["VN"]])
                for t in range(2):
                    for kb in range(2):
                        tk = T.do(mm(banks[bank][:, 128 * t:128 * t + 128],
                                     pt[:, 256 * t + 128 * kb:256 * t + 128 * kb + 128],
                                     VN[:, kb, 128 * h:128 * h + 128], kb == 0, kb == 1))
                return tk

            def finish(o, ri, toks):
                tf = V.do(P(nc.vector.tensor_tensor, QN[:, h, :].rearrange("p (t n) -> p t n", t=2),
                            o.rearrange("p (t n) -> p t n", t=2), ri.unsqueeze(2).to_broadcast([128, 2, 128]),
                            ALU.mult), toks)
                on_done.append(tf)
                return tf

            return attend(scores, 2, 256, 1.0, None, pslots, 4, pv, 256, finish)

        oa_done, on_done, nBa, nBb = [], [], [], []

        def branch_a():
            yield from pipelined([da_unit(h, t) for h in range(4) for t in range(2)], 2)
            tt = []
            for t in range(2):
                v = QA[:, :, 128 * t:128 * t + 128]
                t8 = TMP[:, 0:1024].rearrange("p (k n) -> p k n", k=8)
                a = V.do(P(nc.vector.tensor_tensor, t8, v, v, ALU.mult), oa_done, V.now())
                yield
                s8, s4 = stat(8), stat(4)
                a = V.do(P(nc.vector.tensor_reduce, s8, t8, AX.X, ALU.add), a)
                s82 = s8.rearrange("p (h c) -> p h c", c=2)
                a = V.do(P(nc.vector.tensor_tensor, s4.unsqueeze(2), s82[:, :, 0:1], s82[:, :, 1:2], ALU.add), a)
                r, a = rstd(s4, 4, 256, a, 1.0 - (0.8 - 0.6 * float(np.exp(-0.0))))
                v4 = v.rearrange("p (h c) n -> p h c n", c=2)
                for c in range(2):
                    tt.append(V.do(P(nc.vector.tensor_tensor, v4[:, :, c, :], v4[:, :, c, :],
                                     r.unsqueeze(2).to_broadcast([128, 4, 128]), ALU.mult), a))
                yield
            yield from trans_split(lambda kt, t: QA[:, kt, 128 * t:128 * t + 128], 8, hl(BH, 0), hl(BL, 0),
                                   lambda kt: GC[:, 86 + kt % 2:87 + kt % 2], tt, everything, nBa)

        def branch_b():
            yield from pipelined([na_unit(h) for h in range(8)], 2)
            yield from trans_split(lambda kt, t: QN[:, kt, 128 * t:128 * t + 128], 8, hl(BH, 8), hl(BL, 8),
                                   None, on_done, everything, nBb)

        nb_fetch(0)
        nb_fetch(1)
        for n, (name, dst, rp_, mul) in enumerate((("QA", QA, True, 1.0), ("KA", KA, True, 1.0), ("VA", VA, None, 1.0),
                                                   ("QN", QN, False, 128 ** -0.5), ("KN", KN, False, 1.0), ("VN", VN, None, 1.0))):
            for j in range(2):
                g = gemm_t if name in ("QN", "KN") else gemm
                pair, b, last = g("w_in_2", 16 * n + 8 * j, 16, AH, AL, nA)
                if n == 0 and j == 0:
                    finish_tasks()
                    y_free = everyone()
                if rp_ is None:
                    tdone[name] += evac2(pair, b, last, lambda t: dst[:, t, 512 * j:512 * j + 512], everything)
                elif rp_:
                    qk_post(pair, b, last, name, dst, j)
                else:
                    for i in range(2):
                        tdone[name].append(A.do(P(nc.scalar.activation, dst[:, 4 * j + 2 * i:4 * j + 2 * i + 2, :],
                                                  b[i][:, :].rearrange("p (k n) -> p k n", k=2), ACT.Copy,
                                                  scale=mul), last, everything, y_free))
                    accs.give(pair, tdone[name][-1])
            if name == "VA":
                finish_tasks()
                idle.append(branch_a())
        finish_idle()
        a_over = everyone()
        idle.append(branch_b())
        gate = [M[:, 2048 + 1024 * j:3072 + 1024 * j] for j in range(4)] + \
               [Yf[:, 2048:3072], Yf[:, 3072:4096], M[:, 0:1024], M[:, 1024:2048]]
        gate = [g.rearrange("p (t n) -> p t n", t=2) for g in gate]
        t_gate = {}
        for j in range(8):
            pair, b, last = gemm_t("w_in_2", 96 + 8 * j, 16, AH, AL, nA)
            if j == 4:
                finish_idle()
                b_over = everyone()
            w = a_over if j < 4 else b_over
            for t in range(2):
                t_gate[j, t] = A.do(P(nc.scalar.activation, gate[j][:, t, :], b[t][:, :], ACT.Sigmoid), last, w)
            accs.give(pair, t_gate[j, 1])
        tm, nC = [], []

        def mixed(j, toks):
            yield
            for i in range(2):
                k = slice(4 * j + 2 * i, 4 * j + 2 * i + 2)
                v = gate[j][:, i, :].rearrange("p (k n) -> p k n", k=2)
                h = A.do(P(nc.scalar.activation, AH[:, k, :], v, ACT.Copy), toks[i], t_gate[7, 1])
                nC.append(V.do(P(nc.vector.tensor_tensor, AL[:, k, :], v, bf(AH[:, k, :]), ALU.subtract), h))
                yield

        for j in range(4):
            pair, b, last = gemm_t("w_branch_a", 4 * j, 8, BH[:, 0:8, :], BL[:, 0:8, :], nBa)
            for t in range(2):
                ta = V.do(P(nc.vector.tensor_tensor, gate[j][:, t, :], gate[j][:, t, :], b[t][:, :], ALU.mult),
                          last, t_gate[j, t])
            accs.give(pair, ta)
            pair, b, last = gemm_t("w_branch_b", 4 * j, 8, BH[:, 8:16, :], BL[:, 8:16, :], nBb)
            for t in range(2):
                tb = V.do(P(nc.vector.tensor_tensor, gate[4 + j][:, t, :], gate[4 + j][:, t, :], b[t][:, :],
                            ALU.mult), last, t_gate[4 + j, t])
                tm.append(V.do(P(nc.vector.tensor_tensor, gate[j][:, t, :], gate[j][:, t, :], gate[4 + j][:, t, :],
                                 ALU.add), tb, ta))
            accs.give(pair, tb)
            tasks.append(mixed(j, tm[-2:]))
        finish_tasks()
        everything = everyone()
        grow = M[:, 8192:10240]
        t_gw = load(grow, D["post_mix"].partition_broadcast(128), everything)
        junks = [M[:, 10240 + 512 * i:10752 + 512 * i] for i in range(4)]
        squared = [None] * 4

        def square(x, acc, toks):
            squared.append(A.do(P(nc.scalar.activation, junks[len(squared) % 4], x, ACT.Square, accum_out=acc),
                                toks, squared[-4]))
            return squared[-1]

        def weigh(j, ty, t_gw, ssy):
            c = slice(512 * j, 512 * j + 512)
            for t in range(2):
                a = square(Y[:, t, c], ssy[:, t, j:j + 1], [ty, everything])
                a = V.do(P(nc.vector.tensor_tensor, Y[:, t, c], Y[:, t, c], grow[:, c], ALU.mult), a, t_gw)
            return a

        def residual(ssy, toks, lastR, store):
            ss = stat(2)
            a = V.do(P(nc.vector.tensor_reduce, ss, ssy, AX.X, ALU.add), toks, A.now())
            r, tr = rstd(ss, 2, 2048, a)
            ends = []
            for j in range(4):
                c = slice(512 * j, 512 * j + 512)
                for t in range(2):
                    a = V.do(P(nc.vector.scalar_tensor_tensor, out=R[:, t, c], in0=Y[:, t, c], scalar=r[:, t:t + 1],
                               in1=R[:, t, c], op0=ALU.mult, op1=ALU.add), tr, toks, lastR)
                    if store is None:
                        a = square(R[:, t, c], ssr[:, t, j:j + 1], a)
                    else:
                        a = store(j, t, a)
                    ends.append(a)
            return ends

        ssy = stat(8).rearrange("p (t c) -> p t c", t=2)
        for j in range(4):
            pair, b, last = gemm("w_out_2", 8 * j, 16, AH, AL, nC)
            c = slice(512 * j, 512 * j + 512)
            a0 = square(b[0][:, :], ssy[:, 0, j:j + 1], [last, everything])
            ty = []
            for t in (1, 0):
                ty.append(V.do(P(nc.vector.tensor_tensor, Y[:, t, c], b[t][:, :], grow[:, c], ALU.mult), last, t_gw,
                               everything, a0 if t == 0 else None))
            a1 = square(b[1][:, :], ssy[:, 1, j:j + 1], ty[0])
            accs.give(pair, ty, a1)
        t_R = residual(ssy, ty, t_R, None)
        everything = everyone()
        t_gw = load(grow, D["post_mlp"].partition_broadcast(128), everything)
        nA = norm_T(lambda t: R[:, t, :], 2048, 70, hl(AH), hl(AL), lambda t: Y[:, t, :], [t_R, everything],
                    everything, ssp=ssr)
        y_free = None
        toks_ = Slots([M[:, 4096 + 512 * i:4608 + 512 * i] for i in range(4)], everything)
        wB, vdone = {s: [] for s in range(8)}, {}

        def up(s):
            for j in range(2):
                pair, b, last = gemm_t("w_up", 16 * s + 8 * j, 16, AH, AL, nA)
                for i in range(2):
                    ts, free = take(toks_)
                    a = A.do(P(nc.scalar.activation, ts, b[i][:, :], ACT.Relu), last, free)
                    tasks.append(squared_split(s, ts, a, 8 * (s % 2) + 4 * j + 2 * i))
                accs.give(pair, a)

        def squared_split(s, ts, a, k):
            a = V.do(P(nc.vector.tensor_tensor, ts, ts, ts, ALU.mult), a)
            yield
            v = ts.rearrange("p (k n) -> p k n", k=2)
            a = A.do(P(nc.scalar.activation, BH[:, k:k + 2, :], v, ACT.Copy), a, [everything, vdone.get(s - 2)])
            yield
            a = V.do(P(nc.vector.tensor_tensor, BL[:, k:k + 2, :], v, bf(BH[:, k:k + 2, :]), ALU.subtract), a)
            wB[s].append(a)
            toks_.give(ts, a)

        ty = {}
        for s in range(9):
            if s < 8:
                up(s)
            if s == 0:
                continue
            d = s - 1
            o = 8 * (d % 2)
            if d == 0:
                finish_tasks()
                y_free = everyone()
            for j in range(4):
                pair, b, last = gemm("w_down", 16 * d + 4 * j, 8, BH[:, o:o + 8, :], BL[:, o:o + 8, :], wB[d])
                c = slice(512 * j, 512 * j + 512)
                if d == 0:
                    ty[j] = evac2(pair, b, last, lambda t: Y[:, t, c], y_free)
                else:
                    for t in range(2):
                        a = V.do(P(nc.vector.tensor_tensor, Y[:, t, c], Y[:, t, c], b[t][:, :], ALU.add), last, ty[j])
                    ty[j] = [a]
                    accs.give(pair, a)
                if d == 7:
                    ty[j] = weigh(j, ty[j], t_gw, ssy)
            vdone[d] = [last]
        s_out = [sem(f"s_out{i}") for i in range(8)]
        out_v = out.rearrange("(t p) n -> p t n", p=128)

        def store(j, t, a):
            c = slice(512 * j, 512 * j + 512)
            return S.dma(P(nc.sync.dma_start, out_v[:, t, c], R[:, t, c]), s_out[2 * j + t], 16, a)

        stored = residual(ssy, list(ty.values()), t_R, store)

        finish_idle()
        assert at[0] == len(order)
        S.wait(stored)
        S.wait([g_written, list(a_written.values())])

        block = ctx.enter_context(nc.Block())

        @block.sync
        def _(e):
            for f in S.q:
                f()

        @block.gpsimd
        def _(e):
            for f in G.q:
                f()

        @block.scalar
        def _(e):
            for f in A.q:
                f()

        @block.vector
        def _(e):
            for f in V.q:
                f()

        @block.tensor
        def _(e):
            for f in T.q:
                f()


def cut(w):
    K, N = w.shape
    v = w.reshape(K // 256, 2, 128, N // 512, 512).transpose(3, 0, 2, 1, 4)
    return np.ascontiguousarray(v).reshape(-1, 128, NPIECE)


def cut_t(w):
    K, N = w.shape
    v = w.reshape(K // 512, 4, 128, N // 512, 2, 2, 128).transpose(3, 5, 0, 2, 1, 4, 6)
    return np.ascontiguousarray(v).reshape(-1, 128, NPIECE)


def cut_down(w):
    return np.concatenate([cut(w[k:k + 1024]) for k in range(0, w.shape[0], 1024)])


def columns(g):
    return g.reshape(-1, 128).T


def spread(g):
    return np.broadcast_to(g.reshape(1, -1), (128, g.size))


def kernel(**inputs):
    import numpy as np
    import concourse.bacc as bacc
    from concourse import mybir
    from concourse.bass_utils import run_bass_kernel_spmd as run

    I = {k: np.asarray(v) for k, v in inputs.items()}
    w_in = I["w_in"][0]
    lat, kvl, pe, qs, ks, vs = np.split(w_in, [512, 768, 832, 1856, 1984], axis=1)
    A = {}
    A["x"] = I["x"][0]
    A["consts"] = constants()
    A["gain_cols"] = np.concatenate(
        [columns(I[n][0]) for n in ("norm1_gain", "q_a_gain", "kv_a_gain", "group_out_gain", "norm2_gain",
                                    "norm_mix_pre_2", "norm_mlp_pre_2", "subln_w_2")] +
        [columns(I[n][0, :128]) for n in ("mla_q_gain", "mla_k_gain")] +
        [columns(np.concatenate([I[n][0]] * 2)) for n in ("swa_q_gain", "swa_k_gain")], axis=1)
    A["gain_rows"] = np.concatenate(
        [spread(I[n][0]) for n in ("mla_q_gain", "mla_k_gain", "swa_sinks")], axis=1)
    pos = I["positions"][0]
    p = np.arange(128)
    kidx = 128 * np.arange(2)[None, :, None] + 32 * (p // 32)[:, None, None] + np.arange(32)[None, None, :]
    A["pos"] = np.concatenate([spread(pos), pos[kidx].reshape(128, 64), pos.reshape(2, 128).T], axis=1)
    table = np.zeros((4, 32, 4, 16), np.float32)
    for g in range(4):
        table[g, :, g, :] = I["rel_bias_table"]
    A["table"] = table.reshape(128, 64)
    A["w_in_a"] = cut(np.concatenate([lat, kvl, ks, vs, qs], axis=1))
    A["w_in_b"] = pe.reshape(16, 128, 64).transpose(1, 0, 2).reshape(1, 128, NPIECE)
    for n, per in (("w_q_b", 192), ("w_kv_b", 256)):
        w = I[n][0].reshape(-1, 8, per)
        A[n] = cut(np.concatenate([w[:, :, :128].reshape(-1, 1024), w[:, :, 128:].reshape(w.shape[0], -1)], axis=1))
    A["w_out"] = cut(np.concatenate([I["w_out"][0][1024:], I["w_out"][0][:1024]]))
    for n in ("peer_w_q",):
        A[n] = cut_t(I[n][0])
    A["sub_keys"] = I["peer_sub_keys"][0].reshape(2, 8, 128, 128).transpose(0, 3, 1, 2).reshape(2, 128, NPIECE)
    A["peer_u"] = cut_t(I["peer_u"][0].T)
    A["peer_v"] = cut_down(I["peer_v"][0])
    w = I["w_in_2"][0]
    A["w_in_2"] = np.concatenate([cut(w[:, :3072]), cut_t(w[:, 3072:5120]), cut(w[:, 5120:6144]), cut_t(w[:, 6144:])])
    A["w_branch_a"] = cut_t(I["w_branch_a_2"][0])
    A["w_branch_b"] = cut_t(I["w_branch_b_2"][0])
    A["w_out_2"] = cut(I["w_out_2"][0])
    A["w_up"] = cut_t(I["w_up_2"][0])
    A["w_down"] = cut_down(I["w_down_2"][0])
    A["lam"] = np.concatenate([spread(I[n][0]) for n in ("lam_q1_2", "lam_k1_2", "lam_q2_2", "lam_k2_2")], axis=1)
    A["post_mix"] = I["norm_mix_post_2"][0]
    A["post_mlp"] = I["norm_mlp_post_2"][0]
    q = np.arange(256)
    dr = q[None, :] // 64 - q[:, None] // 64 + 7
    dc = np.clip(q[None, :] % 64 - q[:, None] % 64 + 15, 0, 30)
    nb = I["na_rpb_2"][0][:, dr, dc]
    A["na_bias"] = nb.reshape(8, 2, 128, 256).transpose(0, 2, 1, 3).reshape(8, 128, 512)

    nc = bacc.Bacc("TRN2", target_bir_lowering=False, num_devices=1)
    arrays, D = {}, {}
    for n, a in A.items():
        a = np.ascontiguousarray(a)
        arrays["in_" + n] = a
        D[n] = nc.dram_tensor("in_" + n, a.shape, mybir.dt.from_np(a.dtype), kind="ExternalInput").ap()
    D["scr_g"] = nc.dram_tensor("scr_g", (8, 128, 4096), mybir.dt.float32, kind="Internal").ap()
    D["scr_a"] = nc.dram_tensor("scr_a", (16, 128, 2048), mybir.dt.float32, kind="Internal").ap()
    o = nc.dram_tensor("out_0", (256, 2048), mybir.dt.float32, kind="ExternalOutput").ap()
    build(nc, D, o)
    r = run(nc, [arrays], core_ids=[0])
    return r.results[0]["out_0"].reshape(1, 256, 2048)
```
